# Optimizing a Trainium2 kernel written in Bass

```python
import math
import jax, jax.numpy as jnp
from jax import lax
import numpy as np

D_MODEL = 1024
BATCH = 1
SEQ = 512
DEPTH = 2

N_A_LAYERS = DEPTH // 2
N_B_LAYERS = DEPTH - N_A_LAYERS

EXPAND = 2
D_A = EXPAND * D_MODEL
POOL_WINDOWS = (2, 4, 8, 16)
N_POOL_GROUPS = len(POOL_WINDOWS)
POOL_GW = D_A // N_POOL_GROUPS

ATTN_PAIRS = ((128, 1), (512, 4), (2048, 16))
N_GROUPS = len(ATTN_PAIRS)
N_HEADS = 16
HEAD_DIM = D_MODEL // N_HEADS
D_B = N_HEADS * HEAD_DIM
BLK = 128

DN_ALPHA = (2 * DEPTH) ** 0.25
DN_BETA = (8 * DEPTH) ** -0.25
LN_EPS = 1e-5
NEG_INF = -1e30


def layer_norm(x, g, b):
    xf = x.astype(jnp.float32)
    mu = jnp.mean(xf, axis=-1, keepdims=True)
    var = jnp.mean(jnp.square(xf - mu), axis=-1, keepdims=True)
    y = (xf - mu) * lax.rsqrt(var + LN_EPS) * g.astype(jnp.float32) + b.astype(jnp.float32)
    return y.astype(x.dtype)

def alibi_slopes():
    n = N_GROUPS * N_HEADS
    i = jnp.arange(1, n + 1, dtype=jnp.float32)
    return (2.0 ** (-8.0 * i / n)).reshape(N_GROUPS, N_HEADS)

def pool_mixer(h, w_in, w_grp, scale, w_out):
    B, S, _ = h.shape
    proj = h @ w_in
    u, gate = proj[..., :D_A], proj[..., D_A:]
    uf = u.astype(jnp.float32).reshape(B, S, N_POOL_GROUPS, POOL_GW)
    pos = jnp.arange(S)
    pooled = []
    for g, w in enumerate(POOL_WINDOWS):
        ug = uf[:, :, g]
        cs = jnp.cumsum(ug, axis=1)
        shifted = jnp.pad(cs, ((0, 0), (w, 0), (0, 0)))[:, :S]
        cnt = jnp.minimum(pos + 1, w).astype(jnp.float32)
        pooled.append((cs - shifted) / cnt[None, :, None] - ug)
    pooled = jnp.stack(pooled, axis=2)
    mixed = jnp.einsum('bsgc,gce->bsge', pooled, w_grp.astype(jnp.float32))
    mixed = (mixed.reshape(B, S, D_A) * scale.astype(jnp.float32)).astype(h.dtype)
    return (mixed * jax.nn.silu(gate)) @ w_out

def dilated_window_attention(q, k, v, window, dilation, slopes):
    B, S, H, dh = q.shape
    L = S // dilation
    nblk = -(-L // BLK)
    Lp = nblk * BLK
    win_sub = window // dilation

    def to_sub(t):
        t = t.reshape(B, L, dilation, H, dh)
        t = jnp.pad(t, ((0, 0), (0, Lp - L), (0, 0), (0, 0), (0, 0)))
        return t.reshape(B, nblk, BLK, dilation, H, dh)

    qb, kb, vb = to_sub(q), to_sub(k), to_sub(v)

    def with_prev(t):
        prev = jnp.concatenate([jnp.zeros_like(t[:, :1]), t[:, :-1]], axis=1)
        return jnp.concatenate([prev, t], axis=2)

    kk, vv = with_prev(kb), with_prev(vb)
    scores = jnp.einsum('bnqrhd,bnkrhd->bnrhqk', qb, kk) * (HEAD_DIM ** -0.5)

    a = jnp.arange(BLK)[:, None]
    c = jnp.arange(2 * BLK)[None, :]
    rel = BLK + a - c
    key_pos = (jnp.arange(nblk)[:, None, None] - 1) * BLK + c[None]
    valid = (rel >= 0)[None] & (rel <= win_sub)[None] & (key_pos >= 0)
    bias = -slopes[:, None, None] * (dilation * rel).astype(jnp.float32)[None]
    scores = jnp.where(valid[None, :, None, None], scores + bias[None, None, None], NEG_INF)

    lse = jax.nn.logsumexp(scores, axis=-1)
    p = jnp.exp(scores - lse[..., None])
    out = jnp.einsum('bnrhqk,bnkrhd->bnqrhd', p, vv)
    out = out.reshape(B, Lp, dilation, H, dh)[:, :L].reshape(B, S, H, dh)
    lse = jnp.transpose(lse, (0, 1, 4, 2, 3)).reshape(B, Lp, dilation, H)[:, :L].reshape(B, S, H)
    return out, lse

def dilated_mixer(h, w_in, w_out, k_sh, v_sh, slopes):
    B, S, _ = h.shape
    proj = h @ w_in
    q_all = proj[..., :N_GROUPS * D_B].astype(jnp.float32).reshape(B, S, N_GROUPS, N_HEADS, HEAD_DIM)
    gate = proj[..., N_GROUPS * D_B:]
    kf = k_sh.astype(jnp.float32)
    vf = v_sh.astype(jnp.float32)
    outs, lses = [], []
    for g, (window, dilation) in enumerate(ATTN_PAIRS):
        o, l = dilated_window_attention(q_all[:, :, g], kf[:, :, g], vf[:, :, g], window, dilation, slopes[g])
        outs.append(o)
        lses.append(l)
    wts = jax.nn.softmax(jnp.stack(lses, axis=0), axis=0)
    merged = jnp.sum(wts[..., None] * jnp.stack(outs, axis=0), axis=0)
    merged = merged.reshape(B, S, D_B).astype(h.dtype)
    return (merged * jax.nn.silu(gate)) @ w_out

def first_inputs(seed: int = 0) -> dict:
    key = jax.random.key(seed)
    ks = jax.random.split(key, 12)
    f32 = jnp.float32
    x = jax.random.normal(ks[0], (BATCH, SEQ, D_MODEL), f32)
    w_in_a = jax.random.normal(ks[1], (N_A_LAYERS, D_MODEL, 2 * D_A), f32) * D_MODEL ** -0.5
    w_grp_a = jax.random.normal(ks[2], (N_A_LAYERS, N_POOL_GROUPS, POOL_GW, POOL_GW), f32) * POOL_GW ** -0.5
    scale_a = 1.0 + 0.1 * jax.random.normal(ks[3], (N_A_LAYERS, D_A), f32)
    w_out_a = jax.random.normal(ks[4], (N_A_LAYERS, D_A, D_MODEL), f32) * (D_A ** -0.5) * DN_BETA
    w_kv = jax.random.normal(ks[5], (D_MODEL, 2 * N_GROUPS * D_B), f32) * D_MODEL ** -0.5
    w_in_b = jax.random.normal(ks[6], (N_B_LAYERS, D_MODEL, (N_GROUPS + 1) * D_B), f32) * D_MODEL ** -0.5
    w_out_b = jax.random.normal(ks[7], (N_B_LAYERS, D_B, D_MODEL), f32) * (D_B ** -0.5) * DN_BETA
    ln_g = 1.0 + 0.02 * jax.random.normal(ks[8], (DEPTH, D_MODEL), f32)
    ln_b = 0.02 * jax.random.normal(ks[9], (DEPTH, D_MODEL), f32)
    return {"x": x, "w_in_a": w_in_a, "w_grp_a": w_grp_a, "scale_a": scale_a, "w_out_a": w_out_a,
            "w_kv": w_kv, "w_in_b": w_in_b, "w_out_b": w_out_b, "ln_g": ln_g, "ln_b": ln_b}

def first_block(x, w_in_a, w_grp_a, scale_a, w_out_a, w_kv, w_in_b, w_out_b, ln_g, ln_b):
    B, S, _ = x.shape
    slopes = alibi_slopes()
    h = x
    k_sh = None
    v_sh = None
    for l in range(DEPTH):
        if l < N_A_LAYERS:
            y = pool_mixer(h, w_in_a[l], w_grp_a[l], scale_a[l], w_out_a[l])
        else:
            j = l - N_A_LAYERS
            y = dilated_mixer(h, w_in_b[j], w_out_b[j], k_sh, v_sh, slopes)
        h = layer_norm(DN_ALPHA * h + y, ln_g[l], ln_b[l])
        if l == N_A_LAYERS - 1:
            kv = h @ w_kv
            k_sh = kv[..., :N_GROUPS * D_B].reshape(B, S, N_GROUPS, N_HEADS, HEAD_DIM)
            v_sh = kv[..., N_GROUPS * D_B:].reshape(B, S, N_GROUPS, N_HEADS, HEAD_DIM)
    return h


DEPTH_2 = 1

MIX_W = 1024
CONV_K = 3
CONV_GROUPS = 8
HEAD_DIM_2 = 64
N_KV = 4
HPG = N_HEADS // N_KV
KV_W = N_KV * HEAD_DIM_2
L_CMP = 32
STRIDE_CMP = 16
CMP_HIDDEN = 128
L_SEL = 64
N_SEL_BLOCKS = 16
WINDOW = 512
Q_BLOCK = 16
CHUNK = 128
GM_GROUPS = 8
GM_GW = MIX_W // GM_GROUPS
N_BRANCH = 3
EPS = 1e-6
NEG = -1e30

A_OFF = 0
A_COLS = 4 * MIX_W
B_OFF = A_OFF + A_COLS
B_COLS = 2 * MIX_W + 6 * KV_W + 3 * N_HEADS
C_OFF = B_OFF + B_COLS
C_COLS = 3 * MIX_W
G_OFF = C_OFF + C_COLS
G_COLS = N_BRANCH * D_MODEL
IN_COLS = G_OFF + G_COLS


def rmsnorm(x, g):
    x32 = x.astype(jnp.float32)
    y = x32 * lax.rsqrt(jnp.mean(x32 * x32, axis=-1, keepdims=True) + EPS)
    return y.astype(x.dtype) * g

def layernorm(x, g, b):
    x32 = x.astype(jnp.float32)
    mu = jnp.mean(x32, axis=-1, keepdims=True)
    xc = x32 - mu
    y = xc * lax.rsqrt(jnp.mean(xc * xc, axis=-1, keepdims=True) + EPS)
    return y.astype(x.dtype) * g + b

def masked_softmax(s, mask):
    p = jax.nn.softmax(jnp.where(mask, s, NEG), axis=-1)
    return jnp.where(mask, p, 0.0)

def alibi_slopes_2():
    i = jnp.arange(1, N_HEADS + 1, dtype=jnp.float32)
    return (2.0 ** (-8.0 * i / N_HEADS)).reshape(N_KV, HPG)

def short_conv_mixer(h, w_in_a, conv_w, conv_b):
    S = h.shape[1]
    b, cg, xin, z = jnp.split(h @ w_in_a, 4, axis=-1)
    y = cg * xin
    yp = jnp.pad(y, ((0, 0), (CONV_K - 1, 0), (0, 0)))
    conv = conv_b + sum(conv_w[k] * yp[:, k:k + S] for k in range(CONV_K))
    return b * conv * jax.nn.silu(z)

def nsa_mixer(h, w_in_b, pos_ck, w_ck1, w_ck2, pos_cv, w_cv1, w_cv2):
    Bsz, S, _ = h.shape
    sizes = [MIX_W] + [KV_W] * 6 + [MIX_W]
    q, kc, vc, ks, vs, kw, vw, z, gl = jnp.split(h @ w_in_b, np.cumsum(sizes).tolist(), axis=-1)

    def heads_kv(t):
        return t.reshape(Bsz, S, N_KV, HEAD_DIM_2).transpose(0, 2, 1, 3)

    n_cmp = (S - L_CMP) // STRIDE_CMP + 1
    cmp_start = jnp.arange(n_cmp) * STRIDE_CMP
    cmp_end = cmp_start + (L_CMP - 1)
    cmp_idx = cmp_start[:, None] + jnp.arange(L_CMP)[None, :]

    def compress(t, pos, w1, w2):
        blocks = heads_kv(t)[:, :, cmp_idx] + pos
        flat = blocks.reshape(Bsz, N_KV, n_cmp, L_CMP * HEAD_DIM_2)
        return jax.nn.silu(flat @ w1) @ w2

    k_cmp = compress(kc, pos_ck, w_ck1, w_ck2)
    v_cmp = compress(vc, pos_cv, w_cv1, w_cv2)

    n_sel = S // L_SEL
    k_top = min(N_SEL_BLOCKS, n_sel)
    k_blk = heads_kv(ks).reshape(Bsz, N_KV, n_sel, L_SEL, HEAD_DIM_2)
    v_blk = heads_kv(vs).reshape(Bsz, N_KV, n_sel, L_SEL, HEAD_DIM_2)
    sel_ids = jnp.arange(n_sel)
    overlap = ((cmp_start[:, None] <= (sel_ids[None, :] + 1) * L_SEL - 1)
               & (cmp_end[:, None] >= sel_ids[None, :] * L_SEL)).astype(jnp.float32)

    pad = ((0, 0), (0, 0), (WINDOW - 1, 0), (0, 0))
    k_win = jnp.pad(heads_kv(kw), pad)
    v_win = jnp.pad(heads_kv(vw), pad)
    span = Q_BLOCK + WINDOW - 1

    nq = S // Q_BLOCK
    qh = q.reshape(Bsz, nq, Q_BLOCK, N_KV, HPG, HEAD_DIM_2).transpose(1, 0, 3, 4, 2, 5)
    gh = gl.reshape(Bsz, nq, Q_BLOCK, N_KV, HPG, 3).transpose(1, 0, 3, 4, 2, 5)
    slopes = alibi_slopes_2()
    scale = HEAD_DIM_2 ** -0.5
    bi = jnp.arange(Bsz)[:, None, None, None]
    gi = jnp.arange(N_KV)[None, :, None, None]

    def block_fn(args):
        ci, qb, gb = args
        t0 = ci * Q_BLOCK
        tq = t0 + jnp.arange(Q_BLOCK)
        d_c = tq[:, None] - cmp_end[None, :]
        s = jnp.einsum('bgnqd,bgkd->bgnqk', qb, k_cmp).astype(jnp.float32) * scale \
            - slopes[:, :, None, None] * d_c.astype(jnp.float32)
        p_cmp = masked_softmax(s, d_c >= 0)
        o_cmp = jnp.einsum('bgnqk,bgkd->bgnqd', p_cmp.astype(v_cmp.dtype), v_cmp)
        imp = jnp.einsum('bgnqk,ks->bgqs', p_cmp, overlap)
        cur = tq // L_SEL
        valid = sel_ids[None, :] * L_SEL <= tq[:, None]
        forced = (sel_ids[None, :] == 0) | (sel_ids[None, :] == cur[:, None]) | (sel_ids[None, :] == cur[:, None] - 1)
        score = jnp.where(forced, jnp.inf, jnp.where(valid, imp, -jnp.inf))
        _, sel = lax.top_k(score, k_top)
        kg = k_blk[bi, gi, sel]
        vg = v_blk[bi, gi, sel]
        spos = sel[..., None] * L_SEL + jnp.arange(L_SEL)
        d_s = (tq[None, None, :, None, None] - spos)[:, :, None]
        s = jnp.einsum('bgnqd,bgqkld->bgnqkl', qb, kg).astype(jnp.float32) * scale \
            - slopes[:, :, None, None, None] * d_s.astype(jnp.float32)
        m = jnp.broadcast_to(d_s >= 0, s.shape)
        flat_shape = (Bsz, N_KV, HPG, Q_BLOCK, k_top * L_SEL)
        p = masked_softmax(s.reshape(flat_shape), m.reshape(flat_shape))
        o_slc = jnp.einsum('bgnqm,bgqmd->bgnqd', p.astype(vg.dtype),
                           vg.reshape(Bsz, N_KV, Q_BLOCK, k_top * L_SEL, HEAD_DIM_2))
        kwb = lax.dynamic_slice_in_dim(k_win, t0, span, axis=2)
        vwb = lax.dynamic_slice_in_dim(v_win, t0, span, axis=2)
        kpos = t0 - (WINDOW - 1) + jnp.arange(span)
        d_w = tq[:, None] - kpos[None, :]
        m_w = (d_w >= 0) & (d_w < WINDOW) & (kpos[None, :] >= 0)
        s = jnp.einsum('bgnqd,bgkd->bgnqk', qb, kwb).astype(jnp.float32) * scale \
            - slopes[:, :, None, None] * d_w.astype(jnp.float32)
        p = masked_softmax(s, m_w)
        o_win = jnp.einsum('bgnqk,bgkd->bgnqd', p.astype(vwb.dtype), vwb)
        g = jax.nn.sigmoid(gb)
        return g[..., 0:1] * o_cmp + g[..., 1:2] * o_slc + g[..., 2:3] * o_win

    o = lax.map(block_fn, (jnp.arange(nq), qh, gh))
    o = o.transpose(1, 0, 4, 2, 3, 5).reshape(Bsz, S, MIX_W)
    return o * jax.nn.silu(z)

def gmlp_mixer(h, w_in_c, ln_g, ln_b, w_s, b_s):
    Bsz, S, _ = h.shape
    u, v, z = jnp.split(h @ w_in_c, 3, axis=-1)
    u = jax.nn.gelu(u)
    v = layernorm(jax.nn.gelu(v), ln_g, ln_b)
    vr = v.reshape(Bsz, S // CHUNK, CHUNK, GM_GROUPS, GM_GW)
    tril = jnp.tril(jnp.ones((CHUNK, CHUNK), dtype=bool))
    wm = jnp.where(tril, w_s, 0.0)
    sp = jnp.einsum('gij,bnjgc->bnigc', wm, vr) + b_s.T[:, :, None]
    return u * sp.reshape(Bsz, S, MIX_W) * jax.nn.silu(z)

def hybrid_layer(x, c, g_pre, g_post, w_ada, b_ada, w_in, conv_w, conv_b, pos_ck, w_ck1, w_ck2,
                 pos_cv, w_cv1, w_cv2, ln_g, ln_b, w_s, b_s, w_br, w_out):
    shift, scl, gate = jnp.split(jax.nn.silu(c) @ w_ada + b_ada, 3, axis=-1)
    h = rmsnorm(x, g_pre) * (1.0 + scl[:, None]) + shift[:, None]
    ys = (
        short_conv_mixer(h, w_in[:, A_OFF:A_OFF + A_COLS], conv_w, conv_b),
        nsa_mixer(h, w_in[:, B_OFF:B_OFF + B_COLS], pos_ck, w_ck1, w_ck2, pos_cv, w_cv1, w_cv2),
        gmlp_mixer(h, w_in[:, C_OFF:C_OFF + C_COLS], ln_g, ln_b, w_s, b_s),
    )
    merged = None
    for i in range(N_BRANCH):
        g_i = jax.nn.sigmoid(h @ w_in[:, G_OFF + i * D_MODEL:G_OFF + (i + 1) * D_MODEL])
        term = g_i * (ys[i] @ w_br[i])
        merged = term if merged is None else merged + term
    out = rmsnorm(merged @ w_out, g_post)
    return x + gate[:, None] * out

def second_inputs(seed: int = 0) -> dict:
    key = jax.random.key(seed)
    k = jax.random.split(key, 24)
    nrm = jax.random.normal
    f = jnp.float32
    return {
        "x": nrm(k[0], (BATCH, SEQ, D_MODEL), f),
        "c": nrm(k[1], (BATCH, D_MODEL), f),
        "g_pre": 1.0 + 0.02 * nrm(k[2], (DEPTH_2, D_MODEL), f),
        "g_post": 1.0 + 0.02 * nrm(k[3], (DEPTH_2, D_MODEL), f),
        "w_ada": 0.5 * D_MODEL ** -0.5 * nrm(k[4], (DEPTH_2, D_MODEL, 3 * D_MODEL), f),
        "b_ada": 0.02 * nrm(k[5], (DEPTH_2, 3 * D_MODEL), f),
        "w_in": D_MODEL ** -0.5 * nrm(k[6], (DEPTH_2, D_MODEL, IN_COLS), f),
        "conv_w": CONV_K ** -0.5 * nrm(k[7], (DEPTH_2, CONV_K, MIX_W), f),
        "conv_b": 0.02 * nrm(k[8], (DEPTH_2, MIX_W), f),
        "pos_ck": 0.02 * nrm(k[9], (DEPTH_2, L_CMP, HEAD_DIM_2), f),
        "w_ck1": (L_CMP * HEAD_DIM_2) ** -0.5 * nrm(k[10], (DEPTH_2, L_CMP * HEAD_DIM_2, CMP_HIDDEN), f),
        "w_ck2": CMP_HIDDEN ** -0.5 * nrm(k[11], (DEPTH_2, CMP_HIDDEN, HEAD_DIM_2), f),
        "pos_cv": 0.02 * nrm(k[12], (DEPTH_2, L_CMP, HEAD_DIM_2), f),
        "w_cv1": (L_CMP * HEAD_DIM_2) ** -0.5 * nrm(k[13], (DEPTH_2, L_CMP * HEAD_DIM_2, CMP_HIDDEN), f),
        "w_cv2": CMP_HIDDEN ** -0.5 * nrm(k[14], (DEPTH_2, CMP_HIDDEN, HEAD_DIM_2), f),
        "ln_g": 1.0 + 0.02 * nrm(k[15], (DEPTH_2, MIX_W), f),
        "ln_b": 0.02 * nrm(k[16], (DEPTH_2, MIX_W), f),
        "w_s": CHUNK ** -0.5 * nrm(k[17], (DEPTH_2, GM_GROUPS, CHUNK, CHUNK), f),
        "b_s": 1.0 + 0.02 * nrm(k[18], (DEPTH_2, GM_GROUPS, CHUNK), f),
        "w_br": MIX_W ** -0.5 * nrm(k[19], (DEPTH_2, N_BRANCH, MIX_W, D_MODEL), f),
        "w_out": D_MODEL ** -0.5 * nrm(k[20], (DEPTH_2, D_MODEL, D_MODEL), f),
    }

def second_block(x, c, g_pre, g_post, w_ada, b_ada, w_in, conv_w, conv_b, pos_ck, w_ck1, w_ck2,
              pos_cv, w_cv1, w_cv2, ln_g, ln_b, w_s, b_s, w_br, w_out):
    for l in range(DEPTH_2):
        x = hybrid_layer(x, c, g_pre[l], g_post[l], w_ada[l], b_ada[l], w_in[l], conv_w[l], conv_b[l],
                         pos_ck[l], w_ck1[l], w_ck2[l], pos_cv[l], w_cv1[l], w_cv2[l],
                         ln_g[l], ln_b[l], w_s[l], b_s[l], w_br[l], w_out[l])
    return x


_first_inputs = second_inputs


def second_inputs(seed=0):
    import zlib

    import numpy as np

    out = dict(_first_inputs(seed))
    spreads = {}
    factors = {'g_pre': 5.22,
     'g_post': 24.252,
     'conv_b': 64.0,
     'pos_ck': 64.0,
     'w_ck1': 28.755,
     'w_ck2': 27.98,
     'pos_cv': 64.0,
     'ln_g': 64.0,
     'ln_b': 64.0,
     'b_s': 64.0,
     'w_cv1': 4.757,
     'w_cv2': 4.267}
    for name, (base, spread) in spreads.items():
        noise = np.random.default_rng([zlib.crc32(name.encode()), seed]).standard_normal(out[name].shape)
        drawn = base * np.exp(spread * noise) if base else spread * noise
        out[name] = __import__('jax').numpy.asarray(drawn.astype(out[name].dtype))
    for name, factor in factors.items():
        out[name] = (out[name] * factor).astype(out[name].dtype)
    return out


_narrow_inputs = second_inputs


def second_inputs(seed=0):

    out = dict(_narrow_inputs(seed))
    wider = {'g_post': 3.18, 'conv_b': 3.31, 'ln_g': 6.88, 'ln_b': 6.47, 'b_s': 4.7}
    for name, times in wider.items():
        mean = out[name].mean()
        out[name] = (mean + times * (out[name] - mean)).astype(out[name].dtype)
    return out


DEPTH_3 = 1

GRID_W = 64
CTX_LEN = 256
HG_HEAD_DIM = 128
HG_DIM = D_MODEL
HG_HEADS = HG_DIM // HG_HEAD_DIM
CHUNK_3 = 64
CV_DIM = D_MODEL
CONV_K_3 = 31
FFN_DIM = ((8 * D_MODEL // 3 + 255) // 256) * 256
FFN_K = 3
N_MOD = 6
G_MIN = 1e-6
SPLIT_SIZES = (HG_DIM, HG_DIM, HG_DIM, HG_DIM, HG_DIM, CV_DIM, CV_DIM, D_MODEL, D_MODEL)
P_TOTAL = 5 * HG_DIM + 2 * CV_DIM + 2 * D_MODEL


def rmsnorm_3(x, w):
    xf = x.astype(jnp.float32)
    y = xf * lax.rsqrt(jnp.mean(xf * xf, axis=-1, keepdims=True) + EPS)
    return (y * w.astype(jnp.float32)).astype(x.dtype)

def layernorm_3(x, w, b):
    xf = x.astype(jnp.float32)
    mu = jnp.mean(xf, axis=-1, keepdims=True)
    xc = xf - mu
    y = xc * lax.rsqrt(jnp.mean(xc * xc, axis=-1, keepdims=True) + EPS)
    return (y * w.astype(jnp.float32) + b.astype(jnp.float32)).astype(x.dtype)

def split_proj(p):
    return jnp.split(p, np.cumsum(SPLIT_SIZES)[:-1], axis=-1)

def heads(t):
    return t.reshape(t.shape[0], t.shape[1], HG_HEADS, HG_HEAD_DIM)

def dwconv1d(x, w, b):
    k = w.shape[0]
    y = lax.conv_general_dilated(x, w[:, None, :], window_strides=(1,), padding=[(k // 2, k // 2)],
                                 dimension_numbers=('NWC', 'WIO', 'NWC'), feature_group_count=x.shape[-1])
    return y + b

def dwconv2d(x, w, b):
    k = w.shape[0]
    y = lax.conv_general_dilated(x, w[:, :, None, :], window_strides=(1, 1),
                                 padding=[(k // 2, k // 2), (k // 2, k // 2)],
                                 dimension_numbers=('NHWC', 'HWIO', 'NHWC'), feature_group_count=x.shape[-1])
    return y + b

def gla_chunked(q, k, v, logf, s0):
    bsz, length, nh, _ = q.shape
    dv = v.shape[-1]
    n_chunks = length // CHUNK_3

    def to_chunks(t):
        return t.astype(jnp.float32).reshape(bsz, n_chunks, CHUNK_3, nh, t.shape[-1]).transpose(1, 0, 3, 2, 4)

    tril = jnp.tril(jnp.ones((CHUNK_3, CHUNK_3), dtype=bool))[:, :, None]

    def step(state, inp):
        qc, kc, vc, fc = inp
        b = jnp.cumsum(fc, axis=2)
        o_inter = jnp.einsum('bhtd,bhde->bhte', qc * jnp.exp(b), state)
        rel = b[:, :, :, None, :] - b[:, :, None, :, :]
        decay = jnp.where(tril, jnp.exp(jnp.minimum(rel, 0.0)), 0.0)
        scores = jnp.einsum('bhtd,bhsd,bhtsd->bhts', qc, kc, decay)
        o = o_inter + jnp.einsum('bhts,bhse->bhte', scores, vc)
        b_end = b[:, :, -1]
        new_state = jnp.exp(b_end)[..., None] * state + jnp.einsum(
            'bhsd,bhse->bhde', kc * jnp.exp(jnp.minimum(b_end[:, :, None, :] - b, 0.0)), vc)
        return new_state, o

    s_fin, o = lax.scan(step, s0.astype(jnp.float32),
                        (to_chunks(q), to_chunks(k), to_chunks(v), to_chunks(logf)))
    o = o.transpose(1, 0, 3, 2, 4).reshape(bsz, length, nh, dv)
    return o, s_fin

def hgrn2_gates(f_logit, lb):
    f = f_logit.astype(jnp.float32)
    lb = lb.astype(jnp.float32)
    g = lb + (1.0 - lb) * jax.nn.sigmoid(f)
    log_g = jnp.log(jnp.clip(g, G_MIN, 1.0))
    k = (1.0 - lb) * jax.nn.sigmoid(-f)
    return k, log_g

def hgrn2_bidir(q, i, f_fwd, f_bwd, lb_fwd, lb_bwd, s_fwd, s_bwd):
    q, i = heads(q), heads(i)
    k_f, lg_f = hgrn2_gates(heads(f_fwd), lb_fwd.reshape(HG_HEADS, HG_HEAD_DIM))
    k_b, lg_b = hgrn2_gates(heads(f_bwd), lb_bwd.reshape(HG_HEADS, HG_HEAD_DIM))
    o_f, sf = gla_chunked(q, k_f, i, lg_f, s_fwd)
    flip = lambda t: jnp.flip(t, axis=1)
    o_b, sb = gla_chunked(flip(q), flip(k_b), flip(i), flip(lg_b), s_bwd)
    return o_f + flip(o_b), sf, sb

def mixer_merge(o_hg, g, cv_a, cv_b, gate_hg, gate_cv, gn_w, w_hg_out, dw_w, dw_b, ln_w, ln_b, w_cv_out, w_out):
    bsz, length = g.shape[:2]
    o = rmsnorm_3(o_hg.astype(g.dtype), gn_w) * jax.nn.silu(heads(g))
    y_hg = o.reshape(bsz, length, HG_DIM) @ w_hg_out
    u = cv_a * jax.nn.sigmoid(cv_b)
    u = jax.nn.silu(layernorm_3(dwconv1d(u, dw_w, dw_b), ln_w, ln_b))
    y_cv = u @ w_cv_out
    y = jax.nn.sigmoid(gate_hg) * y_hg + jax.nn.sigmoid(gate_cv) * y_cv
    return y @ w_out

def conv_ffn(h, w_up, dw_w, dw_b, w_down):
    u, v = jnp.split(h @ w_up, 2, axis=-1)
    u = dwconv2d(u, dw_w, dw_b)
    return (jax.nn.gelu(u, approximate=False) * v) @ w_down

def third_inputs(seed: int = 0) -> dict:
    key = jax.random.key(seed)
    ks = jax.random.split(key, 23)
    nrm = lambda k, shape, s: s * jax.random.normal(k, shape, jnp.float32)
    return {
        'x': nrm(ks[0], (BATCH, SEQ, D_MODEL), 1.0),
        'c': nrm(ks[1], (BATCH, D_MODEL), 1.0),
        'ctx': nrm(ks[2], (BATCH, CTX_LEN, D_MODEL), 1.0),
        'c_ctx': nrm(ks[3], (D_MODEL,), 1.0),
        'w_mod': nrm(ks[4], (DEPTH_3, D_MODEL, N_MOD * D_MODEL), 0.5 * D_MODEL ** -0.5),
        'b_mod': nrm(ks[5], (DEPTH_3, N_MOD * D_MODEL), 0.01),
        'norm1_w': 1.0 + nrm(ks[6], (DEPTH_3, D_MODEL), 0.02),
        'w_in': nrm(ks[7], (DEPTH_3, D_MODEL, P_TOTAL), D_MODEL ** -0.5),
        'hg_lb_logits': nrm(ks[8], (2, DEPTH_3, HG_DIM), 0.5),
        'hg_gnorm_w': 1.0 + nrm(ks[9], (DEPTH_3, HG_HEAD_DIM), 0.02),
        'w_hg_out': nrm(ks[10], (DEPTH_3, HG_DIM, D_MODEL), HG_DIM ** -0.5),
        'cv_dw_w': nrm(ks[11], (DEPTH_3, CONV_K_3, CV_DIM), CONV_K_3 ** -0.5),
        'cv_dw_b': nrm(ks[12], (DEPTH_3, CV_DIM), 0.01),
        'cv_ln_w': 1.0 + nrm(ks[13], (DEPTH_3, CV_DIM), 0.02),
        'cv_ln_b': nrm(ks[14], (DEPTH_3, CV_DIM), 0.01),
        'w_cv_out': nrm(ks[15], (DEPTH_3, CV_DIM, D_MODEL), CV_DIM ** -0.5),
        'w_out': nrm(ks[16], (DEPTH_3, D_MODEL, D_MODEL), D_MODEL ** -0.5),
        'norm2_w': 1.0 + nrm(ks[17], (DEPTH_3, D_MODEL), 0.02),
        'w_up': nrm(ks[18], (DEPTH_3, D_MODEL, 2 * FFN_DIM), D_MODEL ** -0.5),
        'ffn_dw_w': nrm(ks[19], (DEPTH_3, FFN_K, FFN_K, FFN_DIM), 1.0 / FFN_K),
        'ffn_dw_b': nrm(ks[20], (DEPTH_3, FFN_DIM), 0.01),
        'w_down': nrm(ks[21], (DEPTH_3, FFN_DIM, D_MODEL), FFN_DIM ** -0.5),
        'final_norm_w': 1.0 + nrm(ks[22], (D_MODEL,), 0.02),
    }

def third_block(x, c, ctx, c_ctx, w_mod, b_mod, norm1_w, w_in, hg_lb_logits, hg_gnorm_w, w_hg_out,
              cv_dw_w, cv_dw_b, cv_ln_w, cv_ln_b, w_cv_out, w_out, norm2_w, w_up, ffn_dw_w, ffn_dw_b,
              w_down, final_norm_w):
    bsz, length, _ = x.shape
    rows = length // GRID_W
    lb_sm = jax.nn.softmax(hg_lb_logits.astype(jnp.float32), axis=1)
    lbs = jnp.cumsum(lb_sm, axis=1) - lb_sm[:, :1]
    cx = ctx
    zero_state = jnp.zeros((bsz, HG_HEADS, HG_HEAD_DIM, HG_HEAD_DIM), jnp.float32)
    for l in range(DEPTH_3):
        mod = (jax.nn.silu(c) @ w_mod[l] + b_mod[l])[:, None, :]
        mod_c = jax.nn.silu(c_ctx) @ w_mod[l] + b_mod[l]
        sh1, sc1, gt1, sh2, sc2, gt2 = jnp.split(mod, N_MOD, axis=-1)
        csh1, csc1, cgt1, csh2, csc2, cgt2 = jnp.split(mod_c, N_MOD, axis=-1)

        h = rmsnorm_3(x, norm1_w[l]) * (1 + sc1) + sh1
        hc = rmsnorm_3(cx, norm1_w[l]) * (1 + csc1) + csh1
        pq, pff, pfb, pi, pg, pa, pb, pgh, pgc = split_proj(h @ w_in[l])
        cq, cff, cfb, ci, cg, ca, cb, cgh, cgc = split_proj(hc @ w_in[l])
        o_ctx, s_f, s_b = hgrn2_bidir(cq, ci, cff, cfb, lbs[0, l], lbs[1, l], zero_state, zero_state)
        o_lat, _, _ = hgrn2_bidir(pq, pi, pff, pfb, lbs[0, l], lbs[1, l], s_f, s_b)
        layer_w = (hg_gnorm_w[l], w_hg_out[l], cv_dw_w[l], cv_dw_b[l], cv_ln_w[l], cv_ln_b[l], w_cv_out[l], w_out[l])
        x = x + gt1 * mixer_merge(o_lat, pg, pa, pb, pgh, pgc, *layer_w)

        h2 = (rmsnorm_3(x, norm2_w[l]) * (1 + sc2) + sh2).reshape(bsz, rows, GRID_W, D_MODEL)
        x = x + gt2 * conv_ffn(h2, w_up[l], ffn_dw_w[l], ffn_dw_b[l], w_down[l]).reshape(bsz, length, D_MODEL)

        if l < DEPTH_3 - 1:
            cx = cx + cgt1 * mixer_merge(o_ctx, cg, ca, cb, cgh, cgc, *layer_w)
            hc2 = (rmsnorm_3(cx, norm2_w[l]) * (1 + csc2) + csh2)[:, None]
            cx = cx + cgt2 * conv_ffn(hc2, w_up[l], ffn_dw_w[l], ffn_dw_b[l], w_down[l])[:, 0]
    return rmsnorm_3(x, final_norm_w)


_first_inputs_3 = third_inputs


def third_inputs(seed=0):
    import zlib

    import numpy as np

    out = dict(_first_inputs_3(seed))
    spreads = {}
    factors = {'ctx': 8.0,
     'c_ctx': 8.0,
     'b_mod': 5.412,
     'norm1_w': 8.0,
     'hg_gnorm_w': 8.0,
     'cv_dw_b': 64.0,
     'cv_ln_w': 64.0,
     'cv_ln_b': 64.0,
     'norm2_w': 8.0,
     'ffn_dw_b': 52.838,
     'final_norm_w': 8.192}
    for name, (base, spread) in spreads.items():
        noise = np.random.default_rng([zlib.crc32(name.encode()), seed]).standard_normal(out[name].shape)
        drawn = base * np.exp(spread * noise) if base else spread * noise
        out[name] = __import__('jax').numpy.asarray(drawn.astype(out[name].dtype))
    for name, factor in factors.items():
        out[name] = (out[name] * factor).astype(out[name].dtype)
    return out


_narrow_inputs_3 = third_inputs


def third_inputs(seed=0):

    out = dict(_narrow_inputs_3(seed))
    wider = {'hg_gnorm_w': 3.2, 'cv_ln_w': 3.55, 'cv_ln_b': 7.43, 'final_norm_w': 3.26}
    for name, times in wider.items():
        mean = out[name].mean()
        out[name] = (mean + times * (out[name] - mean)).astype(out[name].dtype)
    return out


def setup_inputs(seed=0):
    out = dict(first_inputs(seed))
    for name, value in second_inputs(seed + 1).items():
        if name != "x":
            out[name + "_2"] = value
    for name, value in third_inputs(seed + 2).items():
        if name != "x":
            out[name + "_3"] = value
    return out


def reference(
    x, w_in_a, w_grp_a, scale_a, w_out_a, w_kv, w_in_b, w_out_b, ln_g, ln_b, c_2, g_pre_2,
    g_post_2, w_ada_2, b_ada_2, w_in_2, conv_w_2, conv_b_2, pos_ck_2, w_ck1_2, w_ck2_2,
    pos_cv_2, w_cv1_2, w_cv2_2, ln_g_2, ln_b_2, w_s_2, b_s_2, w_br_2, w_out_2, c_3, ctx_3,
    c_ctx_3, w_mod_3, b_mod_3, norm1_w_3, w_in_3, hg_lb_logits_3, hg_gnorm_w_3, w_hg_out_3,
    cv_dw_w_3, cv_dw_b_3, cv_ln_w_3, cv_ln_b_3, w_cv_out_3, w_out_3, norm2_w_3, w_up_3,
    ffn_dw_w_3, ffn_dw_b_3, w_down_3, final_norm_w_3,
):
    x = first_block(
        x, w_in_a, w_grp_a, scale_a, w_out_a, w_kv, w_in_b, w_out_b, ln_g, ln_b,
    )
    x = second_block(
        x, c_2, g_pre_2, g_post_2, w_ada_2, b_ada_2, w_in_2, conv_w_2, conv_b_2, pos_ck_2,
        w_ck1_2, w_ck2_2, pos_cv_2, w_cv1_2, w_cv2_2, ln_g_2, ln_b_2, w_s_2, b_s_2, w_br_2,
        w_out_2,
    )
    return third_block(
        x, c_3, ctx_3, c_ctx_3, w_mod_3, b_mod_3, norm1_w_3, w_in_3, hg_lb_logits_3,
        hg_gnorm_w_3, w_hg_out_3, cv_dw_w_3, cv_dw_b_3, cv_ln_w_3, cv_ln_b_3, w_cv_out_3,
        w_out_3, norm2_w_3, w_up_3, ffn_dw_w_3, ffn_dw_b_3, w_down_3, final_norm_w_3,
    )


_drawn_inputs = setup_inputs


def setup_inputs(seed=0):
    import zlib

    import numpy as np

    out = dict(_drawn_inputs(seed))
    spreads = {}
    factors = {'norm2_w_3': 3.184}
    for name, (base, spread) in spreads.items():
        noise = np.random.default_rng([zlib.crc32(name.encode()), seed]).standard_normal(out[name].shape)
        drawn = base * np.exp(spread * noise) if base else spread * noise
        out[name] = __import__('jax').numpy.asarray(drawn.astype(out[name].dtype))
    for name, factor in factors.items():
        out[name] = (out[name] * factor).astype(out[name].dtype)
    return out
```

```python
import math
import numpy as np
import concourse.bass as bass
from concourse import mybir
from contextlib import ExitStack

F32 = mybir.dt.float32
ACT = mybir.ActivationFunctionType
ALU = mybir.AluOpType
AX = mybir.AxisListType

P = 128
S = 512
D = 1024
KT = D // P
DEPTH = 2
ALPHA = (2 * DEPTH) ** 0.25
LN_EPS = 1e-5
EPS = 1e-6
NH, HD, NG = 16, 64, 3
RING = 8
NBANK = 4
N_CMP = 31
FT = 22
WINDOWS = (2, 4, 8, 16)
MASKED = 1e33
CTX = 256
CH = 128
LEVELS = 7

PARAMS = [
    ("scale_a", 16), ("ln_g", 16), ("ln_b", 16),
    ("g_pre", 8), ("g_post", 8), ("c_2", 8), ("b_ada", 24), ("conv_w", 24), ("conv_b", 8),
    ("c_3", 16), ("b_mod", 48), ("norm1_w", 8), ("gnorm_w", 1), ("cv_w", 31 * 8),
    ("cv_b", 8), ("cv_ln_w", 8), ("cv_ln_b", 8), ("norm2_w", 8), ("ffn_w", 9 * FT),
    ("ffn_b", FT), ("final_w", 8),
]
CONSTS = [("neg_slope_1", 48), ("neg_slope_2", 16), ("cmp_valid", 4), ("pool_fix", 64),
          ("identity", 128), ("mean_d", 128), ("mean_h", 128), ("eps", 1), ("eps_ln", 1)]


def columns(spec):
    at, out = 0, {}
    for name, n in spec:
        out[name] = at
        at += n
    return out, at


PCOL, NPAR = columns(PARAMS)
CCOL, NCON = columns(CONSTS)


def build(nc, d, out_t, parts=(1, 2, 3), upto=99, dump=None):
    weights = d["weights"]
    n_tiles = weights.shape[0]
    ctx = ExitStack()
    with ctx:
        def sb(name, n):
            return ctx.enter_context(nc.sbuf_tensor(name, [P, n], F32))

        def sem(name):
            return ctx.enter_context(nc.semaphore(name))

        ring = sb("ring", RING * 1024)
        par = sb("par", NPAR)
        con = sb("con", NCON)
        small = sb("small", 256)
        arena = sb("arena", 81 * S)
        psum = ctx.enter_context(nc.psum_tensor("psum", [P, 8, S], F32))

        def slot(s):
            return ring[:, s * 1024:(s + 1) * 1024].rearrange("p (b m) -> p b m", m=P)

        def wide(s):
            return ring[:, s * 1024:(s + 1) * 1024].rearrange("p (b m) -> p b m", m=S)

        def tiles(t0, n):
            return arena[:, t0 * S:(t0 + n) * S].rearrange("p (k n) -> p k n", n=S)

        def pcol(name, i=0):
            return par[:, PCOL[name] + i:PCOL[name] + i + 1]

        def ccol(name, i=0, n=1):
            return con[:, CCOL[name] + i:CCOL[name] + i + n]

        ident = ccol("identity", 0, P)
        mean_d = ccol("mean_d", 0, P)
        mean_h = ccol("mean_h", 0, P)

        w_in = [sem(f"w_in{s}") for s in range(RING)]
        w_used = sem("w_used")
        bank_free = [sem(f"bank_free{b}") for b in range(NBANK)]
        par_in = sem("par_in")
        tab_in = sem("tab_in")
        pool_in = sem("pool_in")
        pool_at = [0]
        w_at = [0]
        o_at = [0]
        tab_at = [0]

        def turns(eng, n, body, unroll=RING):
            full = n // unroll
            if full > 1:
                with eng.Fori(0, full) as it:
                    for j in range(unroll):
                        body(it, j)
            elif full == 1:
                for j in range(unroll):
                    body(0, j)
            for j in range(n % unroll):
                body(full, j)

        def refill(sp, w0, n):
            n = min(n, n_tiles - RING - w0)

            def load(it, j):
                s = (w0 + j) % RING
                sp.wait_ge(w_used, it * RING + w0 + j + 1)
                sp.dma_start(ring[:, s * 1024:(s + 1) * 1024],
                             weights[it * RING + (w0 + j + RING)]).then_inc(w_in[s], 16)

            if n > 0:
                turns(sp, n, load)

        def tile_ready(pe, w0, it, j):
            pe.wait_ge(w_in[(w0 + j) % RING], it * 16 + ((w0 + j) // RING + 1) * 16)

        def bank_ready(pe, o0, it, j, per_turn=RING):
            pe.wait_ge(bank_free[(o0 + j) % NBANK],
                       it * (per_turn // NBANK) + ((o0 + j) // NBANK + 1))

        def project(pe, w0, o0, n, act, per_out=1):
            def one(it, j):
                tile_ready(pe, w0, it, j)
                part = j % per_out
                if part == 0:
                    bank_ready(pe, o0, it, j // per_out, RING // per_out)
                for k in range(KT):
                    last = nc.tensor.matmul(
                        psum[:, (o0 + j // per_out) % NBANK], slot((w0 + j) % RING)[:, k],
                        act(j, part * KT + k), start=(part == 0 and k == 0),
                        stop=(part == per_out - 1 and k == KT - 1))
                last.then_inc(w_used, 1)

            turns(pe, n, one)

        def project_wide(pe, w0, o0, n_groups, tok):
            for g in range(n_groups):
                for q in range(4):
                    tile_ready(pe, w0, 0, 4 * g + q)
                    for kk in range(2):
                        for j in range(4):
                            if q == 0 and kk == 0:
                                bank_ready(pe, o0, 0, 4 * g + j)
                            last = nc.tensor.matmul(psum[:, (o0 + j) % NBANK],
                                                    tok(g, 2 * q + kk, j),
                                                    wide((w0 + 4 * g + q) % RING)[:, kk],
                                                    start=(q == 0 and kk == 0),
                                                    stop=(q == 3 and kk == 1))
                    last.then_inc(w_used, 1)

        def took(n_w, n_o):
            w_at[0] += n_w
            o_at[0] += n_o

        mean_in = sem("norm_mean_in")
        centred = sem("norm_centred")
        squared = sem("norm_squared")
        summed = sem("norm_summed")
        rooted = sem("norm_rooted")
        scaled = sem("norm_scaled")
        norms, means = [0], [0]
        sig_in = sem("sig_in")
        sig_used = sem("sig_used")
        merges = [0]

        def norm(name, z, h, sq0, finish, mean=False, eps="eps", n=S, add=None):
            sq, st = tiles(sq0, 2), tiles(sq0 + 2, 2)
            n0, m0 = norms[0], means[0]
            norms[0] += 1
            means[0] += mean
            with nc.Block() as block:
                @block.tensor
                def _(pe):
                    if mean:
                        for k in range(KT):
                            last = nc.tensor.matmul(psum[:, 4, :n], mean_d, z[:, k],
                                                    start=(k == 0), stop=(k == KT - 1))
                        last.then_inc(mean_in, 1)
                    for k in range(KT):
                        pe.wait_ge(squared, KT * n0 + k + 1)
                        nc.tensor.matmul(psum[:, 5, :n], mean_d, sq[:, k % 2, :n], start=(k == 0),
                                         stop=(k == KT - 1)).then_inc(summed, 1)

                @block.scalar
                def _(act):
                    for k in range(KT):
                        if mean:
                            act.wait_ge(centred, KT * m0 + k + 1)
                        if k >= 2:
                            act.wait_ge(summed, KT * n0 + k - 1)
                        nc.scalar.activation(sq[:, k % 2, :n], z[:, k],
                                             ACT.Square).then_inc(squared, 1)
                    act.wait_ge(summed, KT * (n0 + 1))
                    nc.scalar.activation(st[:, 0, :n], psum[:, 5, :n], ACT.Sqrt,
                                         bias=ccol(eps)).then_inc(rooted, 1)
                    if finish is not None:
                        for k in range(KT):
                            act.wait_ge(scaled, KT * n0 + k + 1)
                            finish(k)

                @block.vector
                def _(dve):
                    if mean:
                        dve.wait_ge(mean_in, m0 + 1)
                        for k in range(KT):
                            nc.vector.tensor_tensor(z[:, k], z[:, k], psum[:, 4, :n],
                                                    ALU.subtract).then_inc(centred, 1)
                    dve.wait_ge(rooted, n0 + 1)
                    nc.vector.reciprocal(st[:, 1, :n], st[:, 0, :n])
                    dve.drain()
                    for k in range(KT):
                        nc.vector.tensor_tensor(h[:, k], z[:, k], st[:, 1, :n],
                                                ALU.mult).then_inc(scaled, 1)
                    if add is not None:
                        dve.drain()
                        for k in range(KT):
                            add(k)

        def affine(t, scale_of, bias_of):
            def finish(k):
                nc.scalar.activation(t[:, k], t[:, k], ACT.Identity, scale=scale_of(k),
                                     bias=bias_of(k))
            return finish

        def merge(gate_act, branch_act, out, sg0, first):
            sgm = tiles(sg0, 2)
            n0 = KT * merges[0]
            merges[0] += 1
            w0, o0 = w_at[0], o_at[0]
            with nc.Block() as block:
                @block.sync
                def _(sp):
                    refill(sp, w0, 2 * KT)

                @block.tensor
                def _(pe):
                    project(pe, w0, o0, 2 * KT,
                            lambda j, k: gate_act[:, k] if j % 2 == 0 else branch_act[:, k])

                @block.scalar
                def _(act):
                    def one(it, j):
                        act.wait_ge(w_used, it * 4 + (w0 + 2 * j + 1))
                        act.wait_ge(sig_used, it * 2 + (n0 + j + 1))
                        b = (o0 + 2 * j) % NBANK
                        nc.scalar.activation(sgm[:, j], psum[:, b], ACT.Sigmoid)
                        act.drain().then_inc(bank_free[b], 1)
                        act.sem_inc(sig_in, 1)
                    turns(act, KT, one, 2)

                @block.vector
                def _(dve):
                    def one(it, j):
                        dve.wait_ge(w_used, it * 4 + (w0 + 2 * j + 2))
                        dve.wait_ge(sig_in, it * 2 + (n0 + j + 1))
                        b = (o0 + 2 * j + 1) % NBANK
                        m = it * 2 + j
                        if first:
                            nc.vector.tensor_tensor(out[:, m], sgm[:, j], psum[:, b],
                                                    ALU.mult)
                            dve.drain().then_inc(bank_free[b], 1)
                            dve.sem_inc(sig_used, 1)
                        else:
                            nc.vector.tensor_tensor(sgm[:, j], sgm[:, j], psum[:, b], ALU.mult)
                            dve.drain().then_inc(bank_free[b], 1)
                            nc.vector.tensor_tensor(out[:, m], out[:, m], sgm[:, j],
                                                    ALU.add).then_inc(sig_used, 1)
                    turns(dve, KT, one, 2)
            took(2 * KT, 2 * KT)

        def modulation(vec, n_vec, n_out, dst, bias):
            w0 = w_at[0]
            with nc.Block() as block:
                @block.sync
                def _(sp):
                    refill(sp, w0, n_out)

                @block.tensor
                def _(pe):
                    for t in range(n_out // RING):
                        for j in range(RING):
                            tile_ready(pe, w0, 0, RING * t + j)
                            m = RING * t + j
                            for k in range(KT):
                                last = nc.tensor.matmul(
                                    psum[:, 6, n_vec * m:n_vec * m + n_vec],
                                    slot((w0 + j) % RING)[:, k], vec[:, k, :], start=(k == 0),
                                    stop=(k == KT - 1))
                            last.then_inc(w_used, 1)

                @block.vector
                def _(dve):
                    dve.wait_ge(w_used, w0 + n_out)
                    for i in range(n_vec):
                        nc.vector.tensor_tensor(
                            dst[:, :, i], psum[:, 6, 0:n_vec * n_out].rearrange(
                                "p (m i) -> p m i", i=n_vec)[:, :, i], bias, ALU.add)
            took(n_out, 0)

        with nc.Block() as block:
            @block.sync
            def _(sp):
                sp.dma_start(tiles(0, KT), d["x_t"].rearrange("(k p) n -> p k n", p=P)).then_inc(par_in, 16)
                sp.dma_start(con[:], d["con"]).then_inc(par_in, 16)
                sp.dma_start(par[:], d["par"]).then_inc(par_in, 16)
                for s in range(RING):
                    sp.dma_start(ring[:, s * 1024:(s + 1) * 1024], weights[s]).then_inc(w_in[s], 16)
                sp.wait_ge(par_in, 48)

            @block.vector
            def _(dve):
                if dump is not None:
                    nc.vector.memset(arena[:, 8 * S:], 0.0)
                for b in range(NBANK):
                    dve.sem_inc(bank_free[b], 1)
                dve.sem_inc(sig_used, 2)

        dumped = [0]

        def dump_tiles(t0, n):
            if dump is not None:
                done = sem(f"dump{dumped[0]}")
                with nc.Block() as block:
                    @block.sync
                    def _(sp):
                        sp.dma_start(dump[dumped[0]:dumped[0] + n].rearrange("k p n -> p k n"), tiles(t0, n)).then_inc(done, 16)
                        sp.wait_ge(done, 16)
                dumped[0] += n


        def first_block():
            X0, PL0, SG0 = 0, 8, 24
            x_in, pooled, sg = tiles(X0, KT), tiles(PL0, 16), tiles(SG0, 16)
            PADS = 16
            WID = PADS + S
            ubuf = [arena[:, 40 * S + b * WID:40 * S + (b + 1) * WID] for b in range(2)]
            sbuf = [arena[:, 44 * S + b * WID:44 * S + (b + 1) * WID] for b in range(2)]
            u_in = sem("u_in")
            u_free = sem("u_free")
            pads = sem("pads")
            w0, o0 = w_at[0], o_at[0]
            with nc.Block() as block:
                @block.sync
                def _(sp):
                    refill(sp, w0, 16)

                @block.tensor
                def _(pe):
                    project(pe, w0, o0, 16, lambda j, k: x_in[:, k])

                @block.scalar
                def _(act):
                    act.wait_ge(pads, 1)
                    for o in range(16):
                        act.wait_ge(w_used, w0 + o + 1)
                        if o >= 2:
                            act.wait_ge(u_free, o - 1)
                        nc.scalar.activation(ubuf[o % 2][:, PADS:], psum[:, (o0 + o) % NBANK],
                                             ACT.Copy).then_inc(bank_free[(o0 + o) % NBANK], 1)
                        act.drain().then_inc(u_in, 1)

                @block.vector
                def _(dve):
                    for b in range(2):
                        nc.vector.memset(ubuf[b][:, :PADS], 0.0)
                        nc.vector.memset(sbuf[b][:, :PADS], 0.0)
                    dve.drain().then_inc(pads, 1)
                    for o in range(16):
                        dve.wait_ge(u_in, o + 1)
                        g = o // 4
                        src = ubuf[o % 2]
                        u = src
                        for level in range(g + 1):
                            sh, dst = 1 << level, sbuf[level % 2]
                            nc.vector.tensor_tensor(dst[:, sh:], src[:, sh:], src[:, :WID - sh], ALU.add)
                            dve.drain()
                            src = dst
                        nc.vector.tensor_tensor(src[:, PADS:2 * PADS], src[:, PADS:2 * PADS],
                                                ccol("pool_fix", 16 * g, 16), ALU.mult)
                        dve.drain()
                        nc.vector.scalar_tensor_tensor(pooled[:, o], src[:, PADS:], 1.0 / WINDOWS[g],
                                                       u[:, PADS:], ALU.mult,
                                                       ALU.subtract).then_inc(u_free, 1)
                        dve.drain()
            took(16, 16)
            if upto == 1:
                dump_tiles(PL0, 16)
                return

            w0, o0 = w_at[0], o_at[0]
            with nc.Block() as block:
                @block.sync
                def _(sp):
                    refill(sp, w0, 16)

                @block.tensor
                def _(pe):
                    project(pe, w0, o0, 16, lambda j, k: x_in[:, k])

                @block.scalar
                def _(act):
                    def one(it, j):
                        act.wait_ge(w_used, it * NBANK + w0 + j + 1)
                        nc.scalar.activation(sg[:, it * NBANK + j], psum[:, (o0 + j) % NBANK],
                                             ACT.Silu).then_inc(bank_free[(o0 + j) % NBANK], 1)
                    turns(act, 16, one, NBANK)
            took(16, 16)

            w0, o0 = w_at[0], o_at[0]
            with nc.Block() as block:
                @block.sync
                def _(sp):
                    refill(sp, w0, 8)

                @block.tensor
                def _(pe):
                    for j in range(8):
                        tile_ready(pe, w0, 0, j)
                        for half in range(2):
                            o = 2 * j + half
                            bank_ready(pe, o0, 0, o)
                            for k in range(4):
                                last = nc.tensor.matmul(psum[:, (o0 + o) % NBANK],
                                                        slot((w0 + j) % RING)[:, 4 * half + k],
                                                        pooled[:, 4 * (o // 4) + k],
                                                        start=(k == 0), stop=(k == 3))
                        last.then_inc(w_used, 1)

                @block.vector
                def _(dve):
                    def one(it, j):
                        dve.wait_ge(w_used, it * 2 + w0 + j // 2 + 1)
                        nc.vector.scalar_tensor_tensor(
                            sg[:, it * NBANK + j], psum[:, (o0 + j) % NBANK],
                            par[:, bass.ds(it * NBANK + (PCOL["scale_a"] + j), 1)], sg[:, it * NBANK + j],
                            ALU.mult, ALU.mult).then_inc(bank_free[(o0 + j) % NBANK], 1)
                    turns(dve, 16, one, NBANK)
            took(8, 16)

            Z0 = 8
            z = tiles(Z0, KT)
            w0, o0 = w_at[0], o_at[0]

            def residual(name, w0, o0, per_out, resid, act_of, z):
                with nc.Block() as block:
                    @block.sync
                    def _(sp):
                        refill(sp, w0, 8 * per_out)

                    @block.tensor
                    def _(pe):
                        project(pe, w0, o0, 8 * per_out, act_of, per_out)

                    @block.vector
                    def _(dve):
                        def one(it, j):
                            dve.wait_ge(w_used, it * NBANK * per_out + w0 + (j + 1) * per_out)
                            nc.vector.scalar_tensor_tensor(
                                z[:, it * NBANK + j], resid[:, it * NBANK + j], ALPHA,
                                psum[:, (o0 + j) % NBANK], ALU.mult, ALU.add).then_inc(bank_free[(o0 + j) % NBANK], 1)
                        turns(dve, 8, one, NBANK)
                took(8 * per_out, 8)

            residual("pool", w0, o0, 2, x_in, lambda j, k: sg[:, k], z)
            norm("ln1", z, x_in, 40, affine(x_in, lambda k: pcol("ln_g", k), lambda k: pcol("ln_b", k)),
                 mean=True, eps="eps_ln")
            if upto == 2:
                dump_tiles(0, 8)
                return

            h = tiles(0, KT)
            M0, Q0, K0, V0, ST0, S0, D0 = 8, 16, 28, 40, 52, 70, 78
            gated, qt, kt = tiles(M0, KT), tiles(Q0, 12), tiles(K0, 12)
            q_st = [tiles(ST0 + 6 * b, 3) for b in range(2)]
            k_st = [tiles(ST0 + 6 * b + 3, 3) for b in range(2)]
            v_st = [tiles(ST0 + 12 + 3 * b, 3).rearrange("p a (c m) -> p (a c) m", m=P) for b in range(2)]
            score = [arena[:, S0 * S + b * 768:S0 * S + (b + 1) * 768] for b in range(3)]
            prob_t = [arena[:, S0 * S + (3 + b) * 768:S0 * S + (4 + b) * 768] for b in range(2)]
            dist0 = arena[:, D0 * S:D0 * S + S + 3]
            dist12 = arena[:, D0 * S + S + 4:D0 * S + S + 260]
            nmax = [small[:, b:b + 1] for b in range(3)]
            rsum = [small[:, 3 + b:4 + b] for b in range(3)]
            rinv = [small[:, 6 + b:7 + b] for b in range(3)]
            with nc.Block() as block:
                @block.sync
                def _(sp):
                    sp.dma_start(dist0, d["dist0"]).then_inc(tab_in, 16)
                    sp.dma_start(dist12, d["dist12"]).then_inc(tab_in, 16)
                    sp.wait_ge(tab_in, 32)
            tab_at[0] += 32

            for half in range(2):
                w0, o0 = w_at[0], o_at[0]
                with nc.Block() as block:
                    @block.sync
                    def _(sp):
                        refill(sp, w0, 40)

                    @block.tensor
                    def _(pe):
                        project(pe, w0, o0, 28, lambda j, k: h[:, k])

                        def tok(g, k, j):
                            return h[:, k, j * P:(j + 1) * P] if g == 0 else h[:, k, j::4]
                        project_wide(pe, w0 + 28, o0 + 28, NG, tok)

                    @block.scalar
                    def _(act):
                        def q_out(it, j):
                            act.wait_ge(w_used, it * NBANK + w0 + j + 1)
                            nc.scalar.activation(qt[:, it * NBANK + j], psum[:, (o0 + j) % NBANK],
                                                 ACT.Copy, scale=HD ** -0.5).then_inc(bank_free[(o0 + j) % NBANK], 1)
                        turns(act, 12, q_out, NBANK)

                        def k_out(it, j):
                            act.wait_ge(w_used, it * NBANK + w0 + 12 + j + 1)
                            nc.scalar.activation(kt[:, it * NBANK + j], psum[:, (o0 + j) % NBANK],
                                                 ACT.Copy).then_inc(bank_free[(o0 + j) % NBANK], 1)
                        turns(act, 12, k_out, NBANK)
                        for j in range(4):
                            act.wait_ge(w_used, w0 + 24 + j + 1)
                            nc.scalar.activation(gated[:, 4 * half + j], psum[:, (o0 + j) % NBANK],
                                                 ACT.Silu).then_inc(bank_free[(o0 + j) % NBANK], 1)
                        for g in range(NG):
                            act.wait_ge(w_used, w0 + 28 + 4 * g + 4)
                            for j in range(4):
                                nc.scalar.activation(tiles(V0 + 3 * j + g, 1)[:, 0],
                                                     psum[:, (o0 + j) % NBANK],
                                                     ACT.Copy).then_inc(bank_free[(o0 + j) % NBANK], 1)
                took(40, 40)
                if upto == 3 and half == 0:
                    dump_tiles(M0, 4)
                    dump_tiles(Q0, 36)
                    return

                n = f"a{half}_"
                staged = [sem(n + "staged0"), sem(n + "staged1")]
                qk_done = sem(n + "qk_done")
                qk_read = sem(n + "qk_read")
                max_done = sem(n + "max_done")
                exp_done = sem(n + "exp_done")
                p_done = sem(n + "p_done")
                tr_done = sem(n + "tr_done")
                pt_done = sem(n + "pt_done")
                pv_done = sem(n + "pv_done")
                out_read = sem(n + "out_read")
                UNITS = 16
                with nc.Block() as block:
                    @block.sync
                    def _(sp):
                        with sp.Fori(0, 2) as it:
                            for b in range(2):
                                sp.wait_ge(pv_done, it * UNITS + 8 * b + 1)
                                pair = it * 2 + b
                                for g in range(NG):
                                    sp.dma_start(q_st[b][:, g], qt[:, pair + 4 * g]).then_inc(staged[b], 16)
                                    sp.dma_start(k_st[b][:, g], kt[:, pair + 4 * g]).then_inc(staged[b], 16)
                                sp.dma_start(v_st[b], arena[:, V0 * S:(V0 + 12) * S].rearrange(
                                    "p (c a m) -> p c a m", a=4, m=P)[:, :, pair, :]).then_inc(staged[b], 16)

                    @block.tensor
                    def _(pe):
                        pe.sem_inc(tr_done, 3)
                        pe.sem_inc(pv_done, 9)

                        def unit(u):
                            return u // 8, 64 * (u // 4 % 2), u % 4

                        def qk(it, u):
                            b, off, r = unit(u)
                            if u % 8 == 0:
                                pe.wait_ge(staged[b], it * 112 + 112)
                            pe.wait_ge(qk_read, it * UNITS + u + 1)
                            bank = 2 * (u % 2)
                            nc.tensor.matmul(psum[:, bank], q_st[b][off:off + HD, 0, r::4],
                                             k_st[b][off:off + HD, 0], start=True, stop=True)
                            for g in (1, 2):
                                last = nc.tensor.matmul(psum[:, bank + 1, (g - 1) * P:g * P],
                                                        q_st[b][off:off + HD, g, r::4],
                                                        k_st[b][off:off + HD, g, r::4],
                                                        start=True, stop=True)
                            last.then_inc(qk_done, 1)

                        with pe.Fori(0, 2) as it:
                            qk(it, 0)
                            qk(it, 1)
                            for u in range(UNITS):
                                b, off, r = unit(u)
                                pe.wait_ge(p_done, it * UNITS + u + 1)
                                pe.wait_ge(pt_done, it * UNITS + u + 1)
                                for c in range(6):
                                    last = nc.tensor.transpose(
                                        psum[:, 4 + c // 4, (c % 4) * P:(c % 4 + 1) * P],
                                        score[u % 3][:, c * P:(c + 1) * P], ident)
                                last.then_inc(tr_done, 1)
                                if u + 2 < UNITS:
                                    qk(it, u + 2)
                                pe.wait_ge(pt_done, it * UNITS + u + 2)
                                if u % 8 == 0:
                                    pe.wait_ge(out_read, it * 2 + b + 1)
                                for c in range(6):
                                    vi = 3 * c if c < 4 else 3 * r + c - 3
                                    last = nc.tensor.matmul(psum[off:off + HD, 6 + b, r::4],
                                                            v_st[b][:, vi, off:off + HD],
                                                            prob_t[u % 2][:, c * P:(c + 1) * P],
                                                            start=(c == 0), stop=(c == 5))
                                last.then_inc(pv_done, 1)

                    @block.vector
                    def _(dve):
                        dve.sem_inc(qk_read, 2)
                        dve.sem_inc(out_read, 2)

                        def front(it, u):
                            pair, head, r = u // 8, u // 4, u % 4
                            sc = score[u % 3]
                            bank = 2 * (u % 2)
                            dve.wait_ge(qk_done, it * UNITS + u + 1)
                            dve.wait_ge(tr_done, it * UNITS + u + 1)

                            def slope(g):
                                return con[:, bass.ds(it * 4 + (CCOL["neg_slope_1"] + g * NH + 8 * half + head), 1)]
                            nc.vector.scalar_tensor_tensor(sc[:, 0:S], dist0[:, 3 - r:3 - r + S], slope(0), psum[:, bank],
                                                           ALU.mult, ALU.add)
                            nc.vector.scalar_tensor_tensor(sc[:, S:S + P], dist12[:, 0:P], slope(1),
                                                           psum[:, bank + 1, 0:P], ALU.mult, ALU.add)
                            nc.vector.scalar_tensor_tensor(sc[:, S + P:], dist12[:, P:], slope(2),
                                                           psum[:, bank + 1, P:2 * P], ALU.mult,
                                                           ALU.add).then_inc(qk_read, 1)
                            dve.drain()
                            nc.vector.tensor_reduce(nmax[u % 3], sc, axis=AX.X, op=ALU.max,
                                                    negate=True).then_inc(max_done, 1)

                        def back(it, u):
                            dve.wait_ge(exp_done, it * UNITS + u + 1)
                            nc.vector.reciprocal(rinv[u % 3], rsum[u % 3])
                            dve.drain()
                            nc.vector.tensor_scalar(score[u % 3], score[u % 3], rinv[u % 3], None,
                                                    ALU.mult).then_inc(p_done, 1)

                        def gate(it, b):
                            dve.wait_ge(pv_done, it * UNITS + 8 * (b + 1) + 9)
                            t = gated[:, it * 2 + (4 * half + b)]
                            nc.vector.tensor_tensor(t, psum[:, 6 + b], t, ALU.mult).then_inc(out_read, 1)

                        with dve.Fori(0, 2) as it:
                            front(it, 0)
                            front(it, 1)
                            for u in range(UNITS):
                                back(it, u)
                                if u + 2 < UNITS:
                                    front(it, u + 2)
                                if u == 9:
                                    gate(it, 0)
                            gate(it, 1)
                            dve.drain()

                    @block.scalar
                    def _(act):
                        act.sem_inc(pt_done, 1)

                        def exp(it, u):
                            act.wait_ge(max_done, it * UNITS + u + 1)
                            nc.scalar.activation(score[u % 3], score[u % 3], ACT.Exp, bias=nmax[u % 3],
                                                 accum_out=rsum[u % 3])
                            act.drain().then_inc(exp_done, 1)

                        with act.Fori(0, 2) as it:
                            exp(it, 0)
                            exp(it, 1)
                            for u in range(UNITS):
                                act.wait_ge(tr_done, it * UNITS + u + 4)
                                act.wait_ge(pv_done, it * UNITS + u + 8)
                                nc.scalar.activation(prob_t[u % 2], psum[:, 4:6].rearrange(
                                    "p a n -> p (a n)")[:, 0:768], ACT.Copy).then_inc(pt_done, 1)
                                if u + 2 < UNITS:
                                    exp(it, u + 2)

            if upto == 4:
                dump_tiles(M0, 8)
                return
            w0, o0 = w_at[0], o_at[0]
            Z0 = 16
            z = tiles(Z0, KT)
            residual("attn", w0, o0, 1, h, lambda j, k: gated[:, k], z)
            norm("ln2", z, h, 40, affine(h, lambda k: pcol("ln_g", 8 + k), lambda k: pcol("ln_b", 8 + k)),
                 mean=True, eps="eps_ln")
            if upto == 5:
                dump_tiles(0, 8)
                return

        def hybrid_block():
            x, hn, y, mg = tiles(0, KT), tiles(8, KT), tiles(16, KT), tiles(24, KT)
            mod = small[:, 16:40].rearrange("p (m i) -> p m i", i=1)
            a_col, g_col = small[:, 40:48], small[:, 48:56]
            c_silu = small[:, 56:64]

            with nc.Block() as block:
                @block.scalar
                def _(act):
                    nc.scalar.activation(c_silu, par[:, PCOL["c_2"]:PCOL["c_2"] + 8], ACT.Silu)
            modulation(c_silu.rearrange("p (k i) -> p k i", i=1), 1, 24, mod,
                       par[:, PCOL["b_ada"]:PCOL["b_ada"] + 24])
            with nc.Block() as block:
                @block.vector
                def _(dve):
                    nc.vector.scalar_tensor_tensor(a_col, small[:, 24:32], 1.0,
                                                   par[:, PCOL["g_pre"]:PCOL["g_pre"] + 8],
                                                   ALU.add, ALU.mult)
                    nc.vector.tensor_tensor(g_col, small[:, 32:40],
                                            par[:, PCOL["g_post"]:PCOL["g_post"] + 8], ALU.mult)
            norm("h_pre", x, hn, 72, affine(hn, lambda k: a_col[:, k:k + 1],
                                            lambda k: small[:, 16 + k:17 + k]))
            if upto == 1:
                dump_tiles(8, 8)
                return

            TAPS = 3
            YW = S + TAPS - 1
            cg = tiles(72, 2)
            zs = tiles(74, 2)
            ypad = [arena[:, (32 + 2 * b) * S:(32 + 2 * b) * S + YW] for b in range(2)]
            acc = tiles(36, 2)
            cg_in, z_in = sem("cv_cg_in"), sem("cv_z_in")
            cg_used, z_used = sem("cv_cg_used"), sem("cv_z_used")
            w0, o0 = w_at[0], o_at[0]
            with nc.Block() as block:
                @block.sync
                def _(sp):
                    refill(sp, w0, 32)

                @block.tensor
                def _(pe):
                    project(pe, w0, o0, 32, lambda j, k: hn[:, k])

                @block.scalar
                def _(act):
                    def one(it, j):
                        act.wait_ge(w_used, it * 8 + (w0 + 4 * j + 1))
                        act.wait_ge(cg_used, it * 2 + j + 1)
                        b = o0 % NBANK
                        nc.scalar.activation(cg[:, j], psum[:, b], ACT.Copy)
                        act.drain().then_inc(bank_free[b], 1)
                        act.sem_inc(cg_in, 1)
                        act.wait_ge(w_used, it * 8 + (w0 + 4 * j + 4))
                        act.wait_ge(z_used, it * 2 + j + 1)
                        b = (o0 + 3) % NBANK
                        nc.scalar.activation(zs[:, j], psum[:, b], ACT.Silu)
                        act.drain().then_inc(bank_free[b], 1)
                        act.sem_inc(z_in, 1)
                    turns(act, KT, one, 2)

                @block.vector
                def _(dve):
                    dve.sem_inc(cg_used, 2)
                    dve.sem_inc(z_used, 2)
                    for b in range(2):
                        nc.vector.memset(ypad[b][:, :TAPS - 1], 0.0)
                    dve.drain()

                    def one(it, j):
                        def par_m(name, tap):
                            return par[:, bass.ds(it * 2 + (PCOL[name] + 8 * tap + j), 1)]
                        dve.wait_ge(w_used, it * 8 + (w0 + 4 * j + 2))
                        dve.wait_ge(cg_in, it * 2 + j + 1)
                        b = (o0 + 1) % NBANK
                        nc.vector.tensor_tensor(ypad[j][:, TAPS - 1:], cg[:, j], psum[:, b],
                                                ALU.mult)
                        dve.drain().then_inc(bank_free[b], 1)
                        dve.sem_inc(cg_used, 1)
                        nc.vector.tensor_scalar(acc[:, j], ypad[j][:, 0:S], par_m("conv_w", 0),
                                                par_m("conv_b", 0), ALU.mult, ALU.add)
                        for tap in range(1, TAPS):
                            dve.drain()
                            nc.vector.scalar_tensor_tensor(acc[:, j], ypad[j][:, tap:tap + S],
                                                           par_m("conv_w", tap), acc[:, j],
                                                           ALU.mult, ALU.add)
                        dve.drain()
                        dve.wait_ge(w_used, it * 8 + (w0 + 4 * j + 3))
                        b = (o0 + 2) % NBANK
                        nc.vector.tensor_tensor(acc[:, j], acc[:, j], psum[:, b], ALU.mult)
                        dve.drain().then_inc(bank_free[b], 1)
                        dve.wait_ge(z_in, it * 2 + j + 1)
                        nc.vector.tensor_tensor(y[:, it * 2 + j], acc[:, j], zs[:, j],
                                                ALU.mult).then_inc(z_used, 1)
                        dve.drain()
                    turns(dve, KT, one, 2)
            took(32, 32)
            merge(hn, y, mg, 72, True)
            if upto == 2:
                dump_tiles(16, 8)
                dump_tiles(24, 8)
                return

            pt, v_all = tiles(32, 16), tiles(48, 4)
            wgl = tiles(52, 1)[:, 0, 0:KT * 48].rearrange("p (k n) -> p k n", n=48)
            gates = tiles(53, 1)[:, 0, 0:192]
            w1 = [arena[:, (54 + 8 * t) * S:(62 + 8 * t) * S].rearrange("p (l m) -> p l m", m=P)
                  for t in range(2)]
            w2 = arena[:, 76 * S:76 * S + P]
            hid = [arena[:, 76 * S + P + 124 * t:76 * S + P + 124 * (t + 1)] for t in range(2)]
            kcmp = arena[:, 77 * S:77 * S + 124]
            vcmp = arena[0:N_CMP, 77 * S + 128:77 * S + 384]
            pos = arena[:, 70 * S:70 * S + 64]
            hb = small[:, 64:66]
            rel, cdist = tiles(79, 1)[:, 0], tiles(80, 1)[:, 0, 0:124]
            w0, o0 = w_at[0], o_at[0]
            t0 = pool_at[0]
            pool_at[0] += 9 * 16
            gl_done, gl_read = sem("gl_done"), sem("gl_read")
            pb_done, pb_read = sem("pb_done"), sem("pb_read")
            hd_done, hd_read = sem("hd_done"), sem("hd_read")
            cm_done = sem("cm_done")
            with nc.Block() as block:
                @block.gpsimd
                def _(pool):
                    w1_src = [d[n].rearrange("(l d) m -> d l m", d=HD) for n in ("w_ck1", "w_cv1")]
                    pool.dma_start(tiles(52, 1)[:, 0, 0:KT * 48], d["w_gl"]).then_inc(pool_in, 16)
                    for t in range(2):
                        for half in range(2):
                            pool.dma_start(w1[t][half * HD:(half + 1) * HD],
                                           w1_src[t]).then_inc(pool_in, 16)
                    pool.dma_start(w2, d["w_c2"]).then_inc(pool_in, 16)
                    pool.dma_start(pos, d["pos"]).then_inc(pool_in, 16)
                    pool.dma_start(rel, d["rel"]).then_inc(pool_in, 16)
                    pool.dma_start(cdist, d["cmp_dist"]).then_inc(pool_in, 16)
                    pool.wait_ge(pool_in, t0 + 144)

                @block.sync
                def _(sp):
                    refill(sp, w0, 28)

                @block.tensor
                def _(pe):
                    project(pe, w0, o0, 24, lambda j, k: hn[:, k])
                    project_wide(pe, w0 + 24, o0 + 24, 1,
                                 lambda g, k, j: hn[:, k, j * P:(j + 1) * P])
                    pe.wait_ge(pool_in, t0 + 144)
                    for j in range(4):
                        for k in range(KT):
                            last = nc.tensor.matmul(psum[:, 4, 48 * j:48 * (j + 1)],
                                                    hn[:, k, j * P:(j + 1) * P], wgl[:, k],
                                                    start=(k == 0), stop=(k == KT - 1))
                    last.then_inc(gl_done, 1)
                    for t in range(2):
                        for l in range(32):
                            last = nc.tensor.matmul(psum[:, 7, t:t + 1], w1[t][0:HD, l],
                                                    pos[0:HD, 32 * t + l:32 * t + l + 1],
                                                    start=(l == 0), stop=(l == 31))
                    last.then_inc(pb_done, 1)
                    pe.wait_ge(cm_done, 1)
                    for t in range(2):
                        for half in range(2):
                            rows = slice(half * HD, (half + 1) * HD)
                            for l in range(32):
                                last = nc.tensor.matmul(
                                    psum[:, 5 + half, 64 * t:64 * t + 62],
                                    w1[t][rows, l],
                                    pt[rows, 8 + 2 * t:10 + 2 * t, l:l + 16 * N_CMP - 15:16],
                                    start=(l == 0), stop=(l == 31))
                    last.then_inc(hd_done, 1)
                    pe.wait_ge(hd_read, 1)
                    nc.tensor.matmul(psum[0:HD, 7, 0:124], w2[:, 0:HD], hid[0], start=True, stop=True)
                    nc.tensor.matmul(psum[HD:P, 7, 0:124], w2[:, 0:HD], hid[0], start=True, stop=True)
                    for g in range(4):
                        at = g * N_CMP
                        last = nc.tensor.matmul(psum[0:N_CMP, 4, HD * g:HD * (g + 1)],
                                                hid[1][:, at:at + N_CMP], w2[:, HD:P],
                                                start=True, stop=True)
                    last.then_inc(cm_done, 1)

                @block.scalar
                def _(act):
                    def q_out(it, j):
                        act.wait_ge(w_used, it * NBANK + (w0 + j + 1))
                        nc.scalar.activation(pt[:, it * NBANK + j], psum[:, (o0 + j) % NBANK],
                                             ACT.Copy, scale=HD ** -0.5
                                             ).then_inc(bank_free[(o0 + j) % NBANK], 1)
                    turns(act, 8, q_out, NBANK)

                    def kv_out(it, j):
                        act.wait_ge(w_used, it * NBANK + (w0 + 8 + j + 1))
                        nc.scalar.activation(pt[:, it * NBANK + (8 + j)], psum[:, (o0 + j) % NBANK],
                                             ACT.Copy).then_inc(bank_free[(o0 + j) % NBANK], 1)
                    turns(act, 8, kv_out, NBANK)
                    act.drain().then_inc(cm_done, 1)

                    def z_out(it, j):
                        act.wait_ge(w_used, it * NBANK + (w0 + 16 + j + 1))
                        nc.scalar.activation(y[:, it * NBANK + j], psum[:, (o0 + j) % NBANK],
                                             ACT.Silu).then_inc(bank_free[(o0 + j) % NBANK], 1)
                    turns(act, 8, z_out, NBANK)
                    act.wait_ge(w_used, w0 + 28)
                    for j in range(4):
                        nc.scalar.activation(v_all[:, j], psum[:, (o0 + j) % NBANK],
                                             ACT.Copy).then_inc(bank_free[(o0 + j) % NBANK], 1)
                    act.wait_ge(gl_done, 1)
                    nc.scalar.activation(gates, psum[:, 4, 0:192], ACT.Sigmoid)
                    act.wait_ge(pb_done, 1)
                    nc.scalar.activation(hb, psum[:, 7, 0:2], ACT.Copy)
                    act.drain()
                    act.wait_ge(hd_done, 1)
                    for t in range(2):
                        for half in range(2):
                            nc.scalar.activation(
                                hid[t].rearrange("p (g n) -> p g n", g=4)[:, half::2],
                                psum[:, 5 + half, 64 * t:64 * t + 62].rearrange(
                                    "p (g n) -> p g n", g=2), ACT.Silu, bias=hb[:, t:t + 1])
                    act.drain().then_inc(hd_read, 1)
                    act.wait_ge(cm_done, 2)
                    nc.scalar.activation(kcmp, psum[:, 7, 0:124], ACT.Copy)
                    nc.scalar.activation(vcmp, psum[0:N_CMP, 4, 0:256], ACT.Copy)
            took(28, 28)
            if upto == 3:
                dump_tiles(32, 16)
                dump_tiles(48, 4)
                dump_tiles(53, 1)
                dump_tiles(77, 1)
                return

            k_dup = tiles(54, 8)
            dup_in = sem("dup_in")
            with nc.Block() as block:
                @block.sync
                def _(sp):
                    for g in range(4):
                        rows = slice(HD * (g % 2), HD * (g % 2) + HD)
                        for half in range(2):
                            for kind in range(2):
                                sp.dma_start(k_dup[half * HD:(half + 1) * HD, 4 * kind + g],
                                             pt[rows, 12 + 2 * kind + g // 2]).then_inc(dup_in, 16)
                    sp.wait_ge(dup_in, 256)

            q_st, ks_st, kw_st = tiles(71, 2), tiles(73, 1)[:, 0], tiles(74, 1)[:, 0]
            v_st = tiles(75, 1)[:, 0].rearrange("p (j c m) -> p j c m", j=4, m=HD)
            kc_st = tiles(78, 1)[:, 0, 0:N_CMP]
            vc_st = arena[0:N_CMP, 78 * S + 64:78 * S + 128]
            WB = P + 2 * S
            score = [arena[:, 62 * S + b * WB:62 * S + (b + 1) * WB] for b in range(3)]
            prob_t = [arena[:, 40 * S + b * WB:40 * S + (b + 1) * WB] for b in range(2)]
            nmax = [small[:, 64 + 4 * b:67 + 4 * b] for b in range(3)]
            rsum = [small[:, 76 + 4 * b:79 + 4 * b] for b in range(3)]
            coef = [small[:, 88 + 4 * b:91 + 4 * b] for b in range(3)]
            staged = sem("n_staged")
            qk_done, qk_read = sem("n_qk_done"), sem("n_qk_read")
            max_done, exp_done, p_done = sem("n_max_done"), sem("n_exp_done"), sem("n_p_done")
            tr_done, pt_done = sem("n_tr_done"), sem("n_pt_done")
            pv_done, out_read = sem("n_pv_done"), sem("n_out_read")
            UNITS = 16

            def unit(u):
                n, i = u // 4, u % 4
                return n, i, HD * (n % 2), P * (i + 1)

            with nc.Block() as block:
                @block.sync
                def _(sp):
                    with sp.Fori(0, 4) as it:
                        sp.wait_ge(pv_done, it * UNITS + 2)
                        sp.dma_start(q_st, arena[:, bass.ds(it * 2 * S + 32 * S, 2 * S)].rearrange(
                            "p (k n) -> p k n", n=S)).then_inc(staged, 16)
                        sp.dma_start(ks_st, k_dup[:, it]).then_inc(staged, 16)
                        sp.dma_start(kw_st, k_dup[:, it + 4]).then_inc(staged, 16)
                        for c in range(2):
                            sp.dma_start(v_st[:, :, c], v_all[:, :, bass.ds(it * HD + 256 * c, HD)]
                                         ).then_inc(staged, 16)
                        sp.dma_start(kc_st, kcmp[:, bass.ds(it * N_CMP, N_CMP)]).then_inc(staged, 16)
                        sp.dma_start(vc_st, vcmp[:, bass.ds(it * HD, HD)]).then_inc(staged, 16)

                @block.tensor
                def _(pe):
                    pe.sem_inc(tr_done, 3)
                    pe.sem_inc(pv_done, 2)

                    def qk(it, u):
                        n, i, off, w = unit(u)
                        if u == 0:
                            pe.wait_ge(staged, it * 112 + 112)
                        pe.wait_ge(qk_read, it * UNITS + u + 1)
                        b = u % 2
                        q = q_st[off:off + HD, n // 2, i * P:(i + 1) * P]
                        nc.tensor.matmul(psum[:, 2 * b, 0:w], q, ks_st[off:off + HD, 0:w],
                                         start=True, stop=True)
                        nc.tensor.matmul(psum[:, 2 * b + 1, 0:w], q, kw_st[off:off + HD, 0:w],
                                         start=True, stop=True)
                        pe.wait_ge(qk_read, it * UNITS + u + 2)
                        if u >= 2:
                            pe.wait_ge(pt_done, it * UNITS + u)
                        nc.tensor.matmul(psum[:, 4, 32 * b:32 * b + N_CMP], q,
                                         kc_st[off:off + HD], start=True,
                                         stop=True).then_inc(qk_done, 1)

                    with pe.Fori(0, 4) as it:
                        qk(it, 0)
                        qk(it, 1)
                        for u in range(UNITS):
                            n, i, off, w = unit(u)
                            pe.wait_ge(p_done, it * UNITS + u + 1)
                            pe.wait_ge(pt_done, it * UNITS + u + 1)
                            for c in range(2 * (i + 1)):
                                nc.tensor.transpose(
                                    psum[:, 5 + c // 4, (c % 4) * P:(c % 4 + 1) * P],
                                    score[u % 3][:, (c + 1) * P:(c + 2) * P], ident)
                            pe.wait_ge(qk_read, it * UNITS + min(u + 2, UNITS) + 2)
                            last = nc.tensor.transpose(psum[:, 4, P:2 * P], score[u % 3][:, 0:P], ident)
                            last.then_inc(tr_done, 1)
                            if u + 2 < UNITS:
                                qk(it, u + 2)
                            pe.wait_ge(pt_done, it * UNITS + u + 2)
                            if u % 8 == 0:
                                pe.wait_ge(out_read, it * 2 + u // 8 + 1)
                            out = psum[off:off + HD, 7, i * P:(i + 1) * P]
                            nc.tensor.matmul(out, vc_st, prob_t[u % 2][0:N_CMP, 0:P], start=True,
                                             stop=False)
                            for c in range(2 * (i + 1)):
                                last = nc.tensor.matmul(out, v_st[:, c % (i + 1), c // (i + 1)],
                                                        prob_t[u % 2][:, (c + 1) * P:(c + 2) * P],
                                                        start=False, stop=(c == 2 * i + 1))
                            last.then_inc(pv_done, 1)

                @block.vector
                def _(dve):
                    dve.sem_inc(qk_read, 2)
                    dve.sem_inc(out_read, 1)
                    for b in range(3):
                        nc.vector.memset(score[b][:, 0:P], 0.0)
                    dve.drain()

                    def front(it, u):
                        n, i, off, w = unit(u)
                        b, bank = u % 3, 2 * (u % 2)
                        dve.wait_ge(qk_done, it * UNITS + u + 1)
                        dve.wait_ge(tr_done, it * UNITS + u + 1)
                        slope = con[:, bass.ds(it * 4 + (CCOL["neg_slope_2"] + n), 1)]
                        reach = rel[:, S - w:S]
                        nc.vector.scalar_tensor_tensor(score[b][:, P:P + w], reach, slope,
                                                       psum[:, bank, 0:w], ALU.mult, ALU.add)
                        nc.vector.scalar_tensor_tensor(score[b][:, P + w:P + 2 * w], reach, slope,
                                                       psum[:, bank + 1, 0:w], ALU.mult, ALU.add)
                        nc.vector.scalar_tensor_tensor(
                            score[b][:, 0:N_CMP], cdist[:, N_CMP * i:N_CMP * (i + 1)], slope,
                            psum[:, 4, 16 * bank:16 * bank + N_CMP], ALU.mult, ALU.add)
                        dve.drain().then_inc(qk_read, 1)
                        nc.vector.tensor_reduce(nmax[b][:, 0:1], score[b][:, 0:N_CMP], axis=AX.X,
                                                op=ALU.max, negate=True)
                        nc.vector.tensor_reduce(
                            nmax[b][:, 1:3], score[b][:, P:P + 2 * w].rearrange(
                                "p (c w) -> p c w", c=2), axis=AX.X, op=ALU.max, negate=True)
                        dve.drain().then_inc(max_done, 1)

                    def back(it, u):
                        n, i, off, w = unit(u)
                        b = u % 3
                        dve.wait_ge(exp_done, it * UNITS + u + 1)
                        nc.vector.reciprocal(coef[b], rsum[b])
                        dve.drain()
                        nc.vector.tensor_tensor(
                            coef[b], coef[b], gates[:, bass.ds(it * 12 + (48 * i + 3 * n), 3)],
                            ALU.mult)
                        if i == 0:
                            dve.drain()
                            nc.vector.tensor_tensor(coef[b][:, 0:1], coef[b][:, 0:1],
                                                    ccol("cmp_valid"), ALU.mult)
                        dve.drain()
                        nc.vector.tensor_scalar(score[b][:, 0:N_CMP], score[b][:, 0:N_CMP],
                                                coef[b][:, 0:1], None, ALU.mult)
                        for c in range(2):
                            part = score[b][:, P + c * w:P + (c + 1) * w]
                            nc.vector.tensor_scalar(part, part, coef[b][:, 1 + c:2 + c], None,
                                                    ALU.mult)
                        dve.drain().then_inc(p_done, 1)

                    def gate(it, a):
                        dve.wait_ge(pv_done, it * UNITS + 8 * (a + 1) + 2)
                        t = y[:, it * 2 + a]
                        nc.vector.tensor_tensor(t, psum[:, 7], t, ALU.mult).then_inc(out_read, 1)

                    with dve.Fori(0, 4) as it:
                        front(it, 0)
                        front(it, 1)
                        for u in range(UNITS):
                            back(it, u)
                            if u + 2 < UNITS:
                                front(it, u + 2)
                            if u == 7:
                                gate(it, 0)
                        gate(it, 1)
                        dve.drain()

                @block.scalar
                def _(act):
                    act.sem_inc(pt_done, 1)

                    def exp(it, u):
                        n, i, off, w = unit(u)
                        b = u % 3
                        act.wait_ge(max_done, it * UNITS + u + 1)
                        for c, (lo, hi) in enumerate(((0, N_CMP), (P, P + w), (P + w, P + 2 * w))):
                            nc.scalar.activation(score[b][:, lo:hi], score[b][:, lo:hi], ACT.Exp,
                                                 bias=nmax[b][:, c:c + 1],
                                                 accum_out=rsum[b][:, c:c + 1])
                        act.drain().then_inc(exp_done, 1)

                    with act.Fori(0, 4) as it:
                        exp(it, 0)
                        exp(it, 1)
                        for u in range(UNITS):
                            n, i, off, w = unit(u)
                            act.wait_ge(tr_done, it * UNITS + u + 4)
                            act.wait_ge(pv_done, it * UNITS + u + 1)
                            nc.scalar.activation(prob_t[u % 2][:, 0:P], psum[:, 4, P:2 * P], ACT.Copy)
                            nc.scalar.activation(prob_t[u % 2][:, P:P + 2 * w],
                                                 psum[:, 5:7].rearrange("p a n -> p (a n)")[:, 0:2 * w],
                                                 ACT.Copy)
                            act.drain().then_inc(pt_done, 1)
                            if u + 2 < UNITS:
                                exp(it, u + 2)
            if upto == 4:
                dump_tiles(16, 8)
                return
            merge(hn, y, mg, 72, False)

            vt = arena[:, 32 * S:40 * S].rearrange("p (j n) -> p j n", j=4)
            ln_bc = tiles(44, 4).rearrange("p a n -> p (a n)")
            ws = arena[:, 48 * S:50 * S].rearrange("p (g i) -> p g i", i=P)
            bs, ones = arena[0:1, 50 * S:52 * S], arena[0:1, 52 * S:52 * S + P]
            stats = arena[:, 53 * S:53 * S + 64]
            zs = tiles(74, 2)
            w0, o0 = w_at[0], o_at[0]
            t0 = pool_at[0]
            pool_at[0] += 48
            v_in, v_ready, ws_ready = sem("g_v_in"), sem("g_v_ready"), sem("g_ws_ready")
            var_in, root_in = sem("g_var_in"), sem("g_root_in")
            z_in, z_used, u_in = sem("g_z_in"), sem("g_z_used"), sem("g_u_in")
            sp_done, sp_read = sem("g_sp_done"), sem("g_sp_read")
            with nc.Block() as block:
                @block.gpsimd
                def _(pool):
                    pool.dma_start(ln_bc, d["ln_bc"]).then_inc(pool_in, 16)
                    pool.dma_start(arena[:, 48 * S:50 * S], d["w_s"]).then_inc(pool_in, 16)
                    pool.dma_start(bs, d["b_s"]).then_inc(pool_in, 16)
                    nc.gpsimd.memset(ones, 1.0)
                    pool.wait_ge(pool_in, t0 + 48)
                    nc.gpsimd.affine_select(out=ws, in_=ws, pattern=[[0, 8], [1, P]],
                                            compare_op=ALU.is_ge, fill=0.0, base=0,
                                            channel_multiplier=-1)
                    pool.drain().then_inc(ws_ready, 1)

                @block.sync
                def _(sp):
                    refill(sp, w0, 24)

                @block.tensor
                def _(pe):
                    project_wide(pe, w0, o0, 2, lambda g, k, j: hn[:, k, j * P:(j + 1) * P])
                    project(pe, w0 + 8, o0 + 8, 8, lambda j, k: hn[:, k])
                    pe.wait_ge(ws_ready, 1)
                    pe.wait_ge(v_ready, 1)
                    for g in range(8):
                        pe.wait_ge(sp_read, g + 1)
                        b = 4 + g % 2
                        nc.tensor.matmul(psum[:, b].rearrange("p (n i) -> p n i", i=P), ones,
                                         bs[:, g * P:(g + 1) * P].unsqueeze(1).to_broadcast(
                                             [1, 4, P]), start=True, stop=False,
                                         skip_group_check=True)
                        for n in range(4):
                            last = nc.tensor.matmul(psum[:, b, n * P:(n + 1) * P],
                                                    vt[:, n, g * P:(g + 1) * P], ws[:, g],
                                                    start=False, stop=(n == 3),
                                                    skip_group_check=True)
                        last.then_inc(sp_done, 1)
                        tile_ready(pe, w0 + 16, 0, g)
                        bank_ready(pe, o0 + 16, 0, g)
                        for k in range(KT):
                            last = nc.tensor.matmul(psum[:, (o0 + g) % NBANK],
                                                    slot((w0 + 16 + g) % RING)[:, k], hn[:, k],
                                                    start=(k == 0), stop=(k == KT - 1))
                        last.then_inc(w_used, 1)

                @block.scalar
                def _(act):
                    for g in range(2):
                        act.wait_ge(w_used, w0 + 4 * g + 4)
                        for j in range(4):
                            nc.scalar.activation(vt[:, j, g * S:(g + 1) * S],
                                                 psum[:, (o0 + j) % NBANK], ACT.Gelu_apprx_tanh
                                                 ).then_inc(bank_free[(o0 + j) % NBANK], 1)
                    act.drain().then_inc(v_in, 1)

                    def u_out(it, j):
                        act.wait_ge(w_used, it * NBANK + (w0 + 8 + j + 1))
                        nc.scalar.activation(y[:, it * NBANK + j], psum[:, (o0 + j) % NBANK],
                                             ACT.Gelu_apprx_tanh
                                             ).then_inc(bank_free[(o0 + j) % NBANK], 1)
                    act.wait_ge(var_in, 1)
                    for j in range(4):
                        nc.scalar.activation(stats[:, 56 + j:57 + j], stats[:, 49 + 2 * j:50 + 2 * j],
                                             ACT.Sqrt, bias=ccol("eps"))
                    act.drain().then_inc(root_in, 1)
                    turns(act, 8, u_out, NBANK)
                    act.drain().then_inc(u_in, 1)
                    for g in range(8):
                        act.wait_ge(w_used, w0 + 16 + g + 1)
                        act.wait_ge(z_used, g + 1)
                        b = (o0 + g) % NBANK
                        nc.scalar.activation(zs[:, g % 2], psum[:, b], ACT.Silu)
                        act.drain().then_inc(bank_free[b], 1)
                        act.sem_inc(z_in, 1)

                @block.vector
                def _(dve):
                    dve.sem_inc(z_used, 2)
                    dve.sem_inc(sp_read, 2)
                    dve.wait_ge(v_in, 1)
                    for j in range(4):
                        for g in range(2):
                            nc.vector.bn_stats(stats[:, 12 * j + 6 * g:12 * j + 6 * g + 6],
                                               vt[:, j, g * S:(g + 1) * S])
                    dve.drain()
                    for j in range(4):
                        nc.vector.bn_aggr(stats[:, 48 + 2 * j:50 + 2 * j], stats[:, 12 * j:12 * j + 12])
                    dve.drain().then_inc(var_in, 1)
                    dve.wait_ge(root_in, 1)
                    nc.vector.reciprocal(stats[:, 60:64], stats[:, 56:60])
                    dve.drain()
                    dve.wait_ge(pool_in, t0 + 48)
                    for j in range(4):
                        nc.vector.tensor_scalar(vt[:, j], vt[:, j], stats[:, 48 + 2 * j:49 + 2 * j],
                                                stats[:, 60 + j:61 + j], ALU.subtract, ALU.mult)
                    dve.drain()
                    for j in range(4):
                        nc.vector.tensor_tensor(vt[:, j], vt[:, j], ln_bc[:, 0:D], ALU.mult)
                    dve.drain()
                    for j in range(4):
                        nc.vector.tensor_tensor(vt[:, j], vt[:, j], ln_bc[:, D:2 * D], ALU.add)
                    dve.drain().then_inc(v_ready, 1)
                    dve.wait_ge(u_in, 1)
                    for g in range(8):
                        dve.wait_ge(sp_done, g + 1)
                        nc.vector.tensor_tensor(y[:, g], y[:, g], psum[:, 4 + g % 2], ALU.mult)
                        dve.drain().then_inc(sp_read, 1)
                        dve.wait_ge(z_in, g + 1)
                        nc.vector.tensor_tensor(y[:, g], y[:, g], zs[:, g % 2],
                                                ALU.mult).then_inc(z_used, 1)
            took(24, 24)
            if upto == 5:
                dump_tiles(16, 8)
                return
            merge(hn, y, mg, 72, False)

            z = tiles(32, KT)
            w0, o0 = w_at[0], o_at[0]
            with nc.Block() as block:
                @block.sync
                def _(sp):
                    refill(sp, w0, 8)

                @block.tensor
                def _(pe):
                    project(pe, w0, o0, 8, lambda j, k: mg[:, k])

                @block.scalar
                def _(act):
                    for o in range(8):
                        act.wait_ge(w_used, w0 + o + 1)
                        nc.scalar.activation(z[:, o], psum[:, (o0 + o) % NBANK], ACT.Copy
                                             ).then_inc(bank_free[(o0 + o) % NBANK], 1)
            took(8, 8)

            def add(k):
                nc.vector.scalar_tensor_tensor(x[:, k], z[:, k], g_col[:, k:k + 1], x[:, k],
                                               ALU.mult, ALU.add)
            norm("h_post", z, z, 72, None, add=add)
            if upto == 6:
                dump_tiles(0, 8)
                return

        def recurrent_block():
            x, hn, mg = tiles(0, KT), tiles(8, KT), tiles(24, KT)
            mod = small[:, 88:184].rearrange("p (m i) -> p m i", i=2)
            a1, a1c, a2 = small[:, 184:192], small[:, 192:200], small[:, 200:208]
            c_silu = small[:, 208:224]
            XC, HC = 40, 16
            ctx_x = arena[:, XC * S:(XC + 4) * S].rearrange("p (k n) -> p k n", n=CTX)
            ctx_h = arena[:, HC * S:(HC + 4) * S].rearrange("p (k n) -> p k n", n=CTX)
            ctx_in = sem("ctx_in")

            with nc.Block() as block:
                @block.scalar
                def _(act):
                    nc.scalar.activation(c_silu, par[:, PCOL["c_3"]:PCOL["c_3"] + 16], ACT.Silu)

                @block.gpsimd
                def _(pool):
                    pool.dma_start(ctx_x, d["ctx_t"].rearrange("(k p) n -> p k n", p=P)
                                   ).then_inc(ctx_in, 16)
                    pool.wait_ge(ctx_in, 16)
            modulation(c_silu.rearrange("p (k i) -> p k i", i=2), 2, 48, mod,
                       par[:, PCOL["b_mod"]:PCOL["b_mod"] + 48])
            with nc.Block() as block:
                @block.vector
                def _(dve):
                    for dst, at, i, name in ((a1, 8, 0, "norm1_w"), (a1c, 8, 1, "norm1_w"),
                                             (a2, 32, 0, "norm2_w")):
                        nc.vector.scalar_tensor_tensor(dst, mod[:, at:at + 8, i], 1.0,
                                                       par[:, PCOL[name]:PCOL[name] + 8],
                                                       ALU.add, ALU.mult)
            norm("r_n1", x, hn, 76, affine(hn, lambda k: a1[:, k:k + 1], lambda k: mod[:, k, 0:1]))
            norm("r_n1c", ctx_x, ctx_h, 76, affine(ctx_h, lambda k: a1c[:, k:k + 1],
                                                   lambda k: mod[:, k, 1:2]), n=CTX)
            if upto == 1:
                dump_tiles(8, 12)
                return

            vx = tiles(24, KT).rearrange("p (j a) n -> p j (a n)", j=4)
            vc = tiles(32, 4).rearrange("p (j a) n -> p j (a n)", j=2)
            iv_read = sem("iv_read")
            w0, o0 = w_at[0], o_at[0]
            with nc.Block() as block:
                @block.sync
                def _(sp):
                    refill(sp, w0, 8)

                @block.tensor
                def _(pe):
                    for g in range(2):
                        for q in range(4):
                            tile_ready(pe, w0, 0, 4 * g + q)
                            for kk in range(2):
                                k = 2 * q + kk
                                for j in range(6):
                                    if q == 0 and kk == 0:
                                        if j < 4:
                                            bank_ready(pe, o0, 0, 4 * g + j)
                                        elif g == 1:
                                            pe.wait_ge(iv_read, 1)
                                    act_k = (hn[:, k, j * P:(j + 1) * P] if j < 4 else
                                             ctx_h[:, k, (j - 4) * P:(j - 3) * P])
                                    last = nc.tensor.matmul(
                                        psum[:, j], act_k, wide((w0 + 4 * g + q) % RING)[:, kk],
                                        start=(k == 0), stop=(k == KT - 1))
                            last.then_inc(w_used, 1)

                @block.scalar
                def _(act):
                    for g in range(2):
                        act.wait_ge(w_used, w0 + 4 * g + 4)
                        for j in range(4):
                            nc.scalar.activation(vx[:, j, g * S:(g + 1) * S], psum[:, j],
                                                 ACT.Copy).then_inc(bank_free[j], 1)
                        for j in range(2):
                            nc.scalar.activation(vc[:, j, g * S:(g + 1) * S], psum[:, 4 + j], ACT.Copy)
                        act.drain().then_inc(iv_read, 1)
            took(8, 8)

            yg = tiles(36, KT)
            mask = arena[:, 44 * S:44 * S + 15 * P].rearrange("p (l n) -> p l n", n=P)
            ones = arena[:, 44 * S + 15 * P:48 * S]
            B = 48
            q_s = tiles(B, 2)
            g_s = tiles(B + 2, 2)
            k_s = [tiles(B + 4 + 2 * b, 2) for b in range(2)]
            kc_s = [tiles(B + 8 + b, 1).rearrange("p a (t n) -> p (a t) n", t=2) for b in range(2)]
            lf = tiles(B + 10, 2)
            lc = tiles(B + 12, 1).rearrange("p a (t n) -> p (a t) n", t=2)
            run_f = tiles(B + 13, 1)[:, 0].rearrange("p (c n) -> p c n", n=CH)
            RB = CH + 1
            run_b = arena[:, (B + 14) * S:(B + 14) * S + 4 * RB].rearrange("p (c n) -> p c n", n=RB)
            run_c = arena[:, (B + 15) * S + 8:(B + 15) * S + 8 + 2 * (CTX + 1)].rearrange(
                "p (t n) -> p t n", t=2)
            qd = tiles(B + 17, 2)
            kd = tiles(B + 19, 2)
            kcd = tiles(B + 21, 1).rearrange("p a (t n) -> p (a t) n", t=2)
            k_t = tiles(B + 22, 3).rearrange("p a (c n) -> p (a c) n", n=P)
            st = tiles(B + 25, 2).rearrange("p a (c n) -> p (a c) n", n=P)
            lev = tiles(B + 27, 2)
            sc = tiles(B + 29, 1)[:, 0]
            v_st = tiles(B + 30, 1)[:, 0].rearrange("p (j n) -> p j n", n=P)
            vc_st = tiles(B + 31, 1)[:, 0, 0:2 * P].rearrange("p (j n) -> p j n", n=P)
            o_s, o_r = tiles(B + 32, 1)[:, 0], lev[:, 0]
            e_end = tiles(B + 31, 1)[:, 0, 2 * P:2 * P + 16]
            assert B + 32 < 81
            n_ = "r_"
            tab0 = tab_at[0]
            tab_at[0] += 16
            front_in = sem(n_ + "front_in")
            clipped = sem(n_ + "clipped")
            logged = sem(n_ + "logged")
            summed = sem(n_ + "summed")
            ctx_free = sem(n_ + "ctx_free")
            decayed = sem(n_ + "decayed")
            kd_done = sem(n_ + "kd_done")
            tr_done, tr_read = sem(n_ + "tr_done"), sem(n_ + "tr_read")
            kv_done, st_done = sem(n_ + "kv_done"), sem(n_ + "st_done")
            diff_done, exp_done = sem(n_ + "diff_done"), sem(n_ + "exp_done")
            lev_done, sc_done = sem(n_ + "lev_done"), sem(n_ + "sc_done")
            sc_read = sem(n_ + "sc_read")
            picks = sem(n_ + "picks")
            v_in = sem(n_ + "v_in")
            out_done = sem(n_ + "out_done")
            sq_done, var_done = sem(n_ + "sq_done"), sem(n_ + "var_done")
            rt_done, head_done = sem(n_ + "rt_done"), sem(n_ + "head_done")
            NL = 2 * LEVELS + 1
            w0, o0 = w_at[0], o_at[0]
            TRG = 3

            def halves(ap, level):
                v = ap.rearrange("p (b h n) -> p b h n", h=2, n=1 << level)
                return v[:, :, 0], v[:, :, 1]

            with nc.Block() as block:
                @block.sync
                def _(sp):
                    sp.dma_start(arena[:, 44 * S:44 * S + 15 * P], d["gla_mask"]).then_inc(tab_in, 16)
                    refill(sp, w0, 32)

                @block.gpsimd
                def _(pool):
                    with pool.Fori(0, KT) as hd:
                        pool.wait_ge(head_done, hd + 1)
                        nc.gpsimd.tensor_copy(v_st, vx[:, :, bass.ds(hd * P, P)])
                        nc.gpsimd.tensor_copy(vc_st, vc[:, :, bass.ds(hd * P, P)])
                        pool.drain().then_inc(v_in, 1)

                @block.tensor
                def _(pe):
                    def proj(it, hd, s):
                        t, k0 = s // 4, 2 * (s % 4)
                        if k0 == 0:
                            tile_ready(pe, w0, it, 4 * hd + t)
                            bank_ready(pe, o0, it, 4 * hd + t)
                            if t == 1:
                                pe.wait_ge(ctx_free, it * 2 + hd + 1)
                        for k in (k0, k0 + 1):
                            wt = slot((w0 + 4 * hd + t) % RING)[:, k]
                            last = nc.tensor.matmul(psum[:, t], wt, hn[:, k], start=(k == 0),
                                                    stop=(k == KT - 1))
                            if t in (1, 2):
                                last = nc.tensor.matmul(psum[:, 4, CTX * (t - 1):CTX * t], wt,
                                                        ctx_h[:, k], start=(k == 0),
                                                        stop=(k == KT - 1))
                        if k0 == 6:
                            last.then_inc(w_used, 1)

                    def head(it, hd, follow):
                        n = it * 2 + hd

                        def between(s):
                            if follow:
                                proj(it, hd + 1, s)
                        pe.wait_ge(kd_done, n + 1)
                        groups = ([(kcd[:, t, c * P:(c + 1) * P]) for t in range(2) for c in range(2)],
                                  [kd[:, 0, c * P:(c + 1) * P] for c in range(3)],
                                  [kd[:, 1, c * P:(c + 1) * P] for c in range(1, 4)])
                        for i, g in enumerate(groups):
                            if i == 2:
                                pe.wait_ge(tr_read, it * (2 * TRG) + (TRG * hd + 1))
                            for c, src in enumerate(g):
                                last = nc.tensor.transpose(psum[:, 5 + i % 2, c * P:(c + 1) * P],
                                                           src, ident)
                            last.then_inc(tr_done, 1)
                        pe.wait_ge(tr_read, it * (2 * TRG) + (TRG * hd + 3))
                        pe.wait_ge(v_in, n + 1)
                        for t, bank in ((0, 7), (1, 6)):
                            for c in range(2):
                                nc.tensor.matmul(psum[:, bank, 0:P], k_t[:, 2 * t + c], vc_st[:, c],
                                                 start=(c == 0), stop=(c == 1))
                            for c in range(3):
                                last = nc.tensor.matmul(psum[:, bank, (c + 1) * P:(c + 2) * P],
                                                        k_t[:, 4 + 3 * t + c], v_st[:, c + t],
                                                        start=True, stop=True)
                        last.then_inc(kv_done, 1)
                        between(0)
                        pe.wait_ge(st_done, n + 1)
                        for i in range(NL):
                            pe.wait_ge(lev_done, it * (2 * NL) + (NL * hd + i + 1))
                            pe.wait_ge(sc_read, it * (2 * NL) + (NL * hd + i + 1))
                            for c in range(4):
                                cols_ = slice(c * P, (c + 1) * P)
                                last = nc.tensor.matmul(
                                    psum[:, 5 + (NL * hd + i) % 2, cols_],
                                    lev[:, i % 2, cols_],
                                    q_s[:, hd, cols_] if i == NL - 1 else lev[:, i % 2, cols_],
                                    start=True, stop=True)
                            last.then_inc(sc_done, 1)
                            between(i + 1)
                        pe.wait_ge(sc_read, it * (2 * NL) + (NL * hd + NL + 2))
                        for c in range(4):
                            cols_ = slice(c * P, (c + 1) * P)
                            nc.tensor.matmul(psum[:, 7, cols_], st[:, c], qd[:, 0, cols_],
                                             start=True, stop=False)
                            nc.tensor.matmul(psum[:, 7, cols_], st[:, 4 + c], qd[:, 1, cols_],
                                             start=False, stop=False)
                            last = nc.tensor.matmul(psum[:, 7, cols_], v_st[:, c], sc[:, cols_],
                                                    start=False, stop=True)
                        last.then_inc(out_done, 1)
                        pe.wait_ge(sq_done, n + 1)
                        nc.tensor.matmul(psum[:, 7], mean_h, o_r, start=True,
                                         stop=True).then_inc(var_done, 1)

                    for s in range(16):
                        proj(0, 0, s)
                    with pe.Fori(0, KT // 2 - 1) as it:
                        head(it, 0, True)
                        head(it, 1, True)
                    head(KT // 2 - 1, 0, True)
                    head(KT // 2 - 1, 1, False)

                def first_inputs_(act, it, hd):
                    base = it * 8 + (w0 + 4 * hd)
                    act.wait_ge(w_used, base + 1)
                    nc.scalar.activation(q_s[:, hd], psum[:, 0], ACT.Copy)
                    act.drain().then_inc(bank_free[0], 1)
                    for t in range(2):
                        act.wait_ge(w_used, base + 2 + t)
                        nc.scalar.activation(lf[:, t], psum[:, 1 + t], ACT.Sigmoid)
                        nc.scalar.activation(k_s[t][:, hd], psum[:, 1 + t], ACT.Sigmoid, scale=-1.0)
                        act.drain().then_inc(bank_free[1 + t], 1)
                    nc.scalar.activation(lc, psum[:, 4].rearrange("p (t n) -> p t n", t=2), ACT.Sigmoid)
                    nc.scalar.activation(kc_s[hd], psum[:, 4].rearrange("p (t n) -> p t n", t=2),
                                         ACT.Sigmoid, scale=-1.0)
                    act.drain().then_inc(ctx_free, 1)
                    act.sem_inc(front_in, 1)

                @block.scalar
                def _(act):
                    def front(it, hd):
                        n = it * 2 + hd
                        first_inputs_(act, it, hd)
                        act.wait_ge(w_used, it * 8 + (w0 + 4 * hd + 4))
                        nc.scalar.activation(g_s[:, hd], psum[:, 3], ACT.Silu).then_inc(bank_free[3], 1)
                        act.wait_ge(clipped, n + 1)
                        nc.scalar.activation(lf, lf, ACT.Ln)
                        nc.scalar.activation(lc, lc, ACT.Ln)
                        act.drain().then_inc(logged, 1)

                    def body(it, hd):
                        n = it * 2 + hd
                        act.wait_ge(summed, n + 1)
                        nc.scalar.activation(qd[:, 0].rearrange("p (c n) -> p c n", n=CH), run_f,
                                             ACT.Exp)
                        nc.scalar.activation(kd[:, 1].rearrange("p (c n) -> p c n", n=CH),
                                             run_b[:, :, 0:CH], ACT.Exp)
                        nc.scalar.activation(kcd[:, 1], run_c[:, 1, 0:CTX], ACT.Exp)
                        nc.scalar.activation(kcd[:, 0], run_c[:, 0, 1:CTX + 1], ACT.Exp, scale=-1.0,
                                             bias=run_c[:, 0, CTX:CTX + 1])
                        for c in range(4):
                            nc.scalar.activation(kd[:, 0, c * CH:(c + 1) * CH], run_f[:, c], ACT.Exp,
                                                 scale=-1.0, bias=run_f[:, c, CH - 1:CH])
                            nc.scalar.activation(qd[:, 1, c * CH:(c + 1) * CH], run_b[:, c, 0:CH],
                                                 ACT.Exp, scale=-1.0, bias=run_b[:, c, CH:CH + 1])
                        nc.scalar.activation(e_end[:, 0:4], run_f[:, :, CH - 1], ACT.Exp)
                        nc.scalar.activation(e_end[:, 4:8], run_b[:, :, CH], ACT.Exp)
                        act.drain().then_inc(decayed, 1)
                        for i, (at, m) in enumerate(((0, 4), (4, 3), (7, 3))):
                            act.wait_ge(tr_done, it * (2 * TRG) + (TRG * hd + i + 1))
                            nc.scalar.activation(k_t[:, at:at + m], psum[:, 5 + i % 2, 0:m * P].rearrange(
                                "p (c n) -> p c n", n=P), ACT.Copy).then_inc(tr_read, 1)
                        for i in range(NL - 1):
                            act.wait_ge(diff_done, it * (2 * NL - 2) + ((NL - 1) * hd + i + 1))
                            nc.scalar.activation(lev[:, i % 2], lev[:, i % 2],
                                                 ACT.Exp).then_inc(exp_done, 1)
                        act.wait_ge(out_done, n + 1)
                        nc.scalar.activation(o_s, psum[:, 7], ACT.Copy)
                        nc.scalar.activation(o_r, psum[:, 7], ACT.Square)
                        act.drain().then_inc(sq_done, 1)
                        act.wait_ge(var_done, n + 1)
                        nc.scalar.activation(o_r, psum[:, 7], ACT.Sqrt,
                                             bias=ccol("eps")).then_inc(rt_done, 1)

                    front(0, 0)
                    with act.Fori(0, KT // 2 - 1) as it:
                        body(it, 0)
                        front(it, 1)
                        body(it, 1)
                        front(it + 1, 0)
                    body(KT // 2 - 1, 0)
                    front(KT // 2 - 1, 1)
                    body(KT // 2 - 1, 1)

                @block.vector
                def _(dve):
                    dve.sem_inc(ctx_free, 1)
                    dve.sem_inc(sc_read, 2)
                    dve.sem_inc(head_done, 1)
                    dve.wait_ge(tab_in, tab0 + 16)
                    nc.vector.memset(ones, 1.0)
                    nc.vector.memset(run_b[:, :, 0:1], 0.0)
                    nc.vector.memset(run_c[:, :, 0:1], 0.0)
                    dve.drain()

                    def front(it, hd):
                        n = it * 2 + hd
                        dve.wait_ge(front_in, n + 1)
                        for t in (lf, lc):
                            nc.vector.tensor_scalar(t, t, 1e-6, 1.0, ALU.max, ALU.min)
                        dve.drain().then_inc(clipped, 1)

                    def body(it, hd):
                        n = it * 2 + hd
                        dve.wait_ge(logged, n + 1)
                        for c in range(4):
                            nc.vector.tensor_tensor_scan(run_f[:, c], ones, lf[:, 0, c * CH:(c + 1) * CH],
                                                         0.0, ALU.mult, ALU.add)
                            nc.vector.tensor_tensor_scan(run_b[:, c, 1:RB], ones,
                                                         lf[:, 1, c * CH:(c + 1) * CH],
                                                         0.0, ALU.mult, ALU.add)
                        for t in range(2):
                            nc.vector.tensor_tensor_scan(run_c[:, t, 1:CH + 1], ones, lc[:, t, 0:CH],
                                                         0.0, ALU.mult, ALU.add)
                        dve.drain()
                        for t in range(2):
                            nc.vector.tensor_tensor_scan(run_c[:, t, CH + 1:CTX + 1], ones,
                                                         lc[:, t, CH:CTX], run_c[:, t, CH:CH + 1],
                                                         ALU.mult, ALU.add)
                        dve.drain().then_inc(summed, 1)
                        dve.wait_ge(decayed, n + 1)
                        for t in range(2):
                            nc.vector.tensor_tensor(qd[:, t], qd[:, t], q_s[:, hd], ALU.mult)
                            nc.vector.tensor_tensor(kd[:, t], kd[:, t], k_s[t][:, hd], ALU.mult)
                            nc.vector.tensor_tensor(kcd[:, t], kcd[:, t], kc_s[hd][:, t], ALU.mult)
                        dve.drain().then_inc(kd_done, 1)

                        def diff(i):
                            level, bwd = i // 2, i % 2
                            if i >= 2:
                                dve.wait_ge(sc_done, it * (2 * NL) + (NL * hd + i - 1))
                            lo, hi = halves(lev[:, i % 2], level)
                            w = 1 << level
                            nb = CH // (2 * w)
                            if not bwd:
                                blk = run_f.rearrange("p c (b h n) -> p (c b) h n", h=2, n=w)
                                s_lo, s_hi = blk[:, :, 0], blk[:, :, 1]
                                ref = blk[:, :, 0, w - 1:w].to_broadcast([P, 4 * nb, w])
                                nc.vector.tensor_tensor(lo, ref, s_lo, ALU.subtract)
                                nc.vector.tensor_tensor(hi, s_hi, ref, ALU.subtract)
                            else:
                                blk = run_b[:, :, 0:CH].rearrange("p c (b h n) -> p c b h n", h=2, n=w)
                                lo4 = lo.rearrange("p (c b) n -> p c b n", c=4)
                                hi4 = hi.rearrange("p (c b) n -> p c b n", c=4)
                                ref = blk[:, :, :, 1, 0:1].to_broadcast([P, 4, nb, w])
                                nc.vector.tensor_tensor(lo4, ref, blk[:, :, :, 0], ALU.subtract)
                                nc.vector.tensor_tensor(hi4, blk[:, :, :, 1], ref, ALU.subtract)
                            dve.drain().then_inc(diff_done, 1)

                        def fill(i):
                            level, bwd = i // 2, i % 2
                            dve.wait_ge(exp_done, it * (2 * NL - 2) + ((NL - 1) * hd + i + 1))
                            lo, hi = halves(lev[:, i % 2], level)
                            k_lo, k_hi = halves(k_s[bwd][:, hd], level)
                            q_lo, q_hi = halves(q_s[:, hd], level)
                            nc.vector.tensor_tensor(lo, lo, q_lo if bwd else k_lo, ALU.mult)
                            nc.vector.tensor_tensor(hi, hi, k_hi if bwd else q_hi, ALU.mult)
                            dve.drain().then_inc(lev_done, 1)

                        def pick(i):
                            dve.wait_ge(sc_done, it * (2 * NL) + (NL * hd + i + 1))
                            dve.sem_inc(picks, 1)
                            nc.vector.copy_predicated(
                                sc.rearrange("p (c n) -> p c n", n=P),
                                mask[:, i].unsqueeze(1).to_broadcast([P, 4, P]).bitcast(mybir.dt.int32),
                                psum[:, 5 + (NL * hd + i) % 2].rearrange("p (c n) -> p c n", n=P))
                            dve.drain().then_inc(sc_read, 1)

                        diff(0)
                        diff(1)
                        dve.wait_ge(kv_done, n + 1)
                        nc.vector.tensor_copy(st[:, 0], psum[:, 7, 0:P])
                        nc.vector.tensor_copy(st[:, 7], psum[:, 6, 0:P])
                        dve.drain()
                        for c in range(3):
                            nc.vector.scalar_tensor_tensor(
                                st[:, c + 1], st[:, c], e_end[:, c:c + 1],
                                psum[:, 7, (c + 1) * P:(c + 2) * P], ALU.mult, ALU.add)
                            b = 3 - c
                            nc.vector.scalar_tensor_tensor(
                                st[:, 4 + b - 1], st[:, 4 + b], e_end[:, 4 + b:5 + b],
                                psum[:, 6, b * P:(b + 1) * P], ALU.mult, ALU.add)
                            dve.drain()
                        dve.sem_inc(st_done, 1)
                        for i in range(NL - 1):
                            fill(i)
                            pick(i)
                            if i + 2 < NL - 1:
                                diff(i + 2)
                        dve.wait_ge(sc_done, it * (2 * NL) + (NL * hd + NL - 2))
                        nc.vector.tensor_tensor(lev[:, (NL - 1) % 2], k_s[0][:, hd], k_s[1][:, hd],
                                                ALU.add).then_inc(lev_done, 1)
                        pick(NL - 1)
                        dve.wait_ge(rt_done, n + 1)
                        nc.vector.reciprocal(o_r, o_r)
                        dve.drain()
                        nc.vector.tensor_tensor(o_s, o_s, o_r, ALU.mult)
                        dve.drain()
                        nc.vector.scalar_tensor_tensor(yg[:, n], o_s, pcol("gnorm_w"), g_s[:, hd],
                                                       ALU.mult, ALU.mult)
                        dve.drain().then_inc(head_done, 1)

                    front(0, 0)
                    with dve.Fori(0, KT // 2 - 1) as it:
                        body(it, 0)
                        front(it, 1)
                        body(it, 1)
                        front(it + 1, 0)
                    body(KT // 2 - 1, 0)
                    front(KT // 2 - 1, 1)
                    body(KT // 2 - 1, 1)
            took(32, 32)
            if upto == 2:
                dump_tiles(36, 8)
                return
            merge(hn, yg, mg, 78, True)

            TAPS = 31
            HALF = TAPS // 2
            UW = S + TAPS - 1
            cv = tiles(36, KT)
            upad = [arena[:, (44 + 2 * b) * S:(44 + 2 * b) * S + UW] for b in range(2)]
            sg = tiles(48, 2)
            acc = tiles(50, 2)
            sg_in, u_done = sem("c_sg_in"), sem("c_u_done")
            w0, o0 = w_at[0], o_at[0]
            with nc.Block() as block:
                @block.sync
                def _(sp):
                    refill(sp, w0, 16)

                @block.tensor
                def _(pe):
                    project(pe, w0, o0, 16, lambda j, k: hn[:, k])

                @block.scalar
                def _(act):
                    def one(it, j):
                        act.wait_ge(w_used, it * 4 + (w0 + 2 * j + 2))
                        act.wait_ge(u_done, it * 2 + j + 1)
                        b = (o0 + 2 * j + 1) % NBANK
                        nc.scalar.activation(sg[:, j], psum[:, b], ACT.Sigmoid)
                        act.drain().then_inc(bank_free[b], 1)
                        act.sem_inc(sg_in, 1)
                    turns(act, KT, one, 2)

                @block.vector
                def _(dve):
                    dve.sem_inc(u_done, 2)
                    for b in range(2):
                        nc.vector.memset(upad[b][:, :HALF], 0.0)
                        nc.vector.memset(upad[b][:, HALF + S:], 0.0)
                    dve.drain()

                    def one(it, j):
                        def tap_w(t):
                            return par[:, bass.ds(it * 2 + (PCOL["cv_w"] + 8 * t + j), 1)]
                        dve.wait_ge(w_used, it * 4 + (w0 + 2 * j + 1))
                        dve.wait_ge(sg_in, it * 2 + j + 1)
                        b = (o0 + 2 * j) % NBANK
                        nc.vector.tensor_tensor(upad[j][:, HALF:HALF + S], sg[:, j], psum[:, b],
                                                ALU.mult)
                        dve.drain().then_inc(bank_free[b], 1)
                        dve.sem_inc(u_done, 1)
                        nc.vector.tensor_scalar(acc[:, 0], upad[j][:, 0:S], tap_w(0),
                                                par[:, bass.ds(it * 2 + (PCOL["cv_b"] + j), 1)],
                                                ALU.mult, ALU.add)
                        nc.vector.tensor_scalar(acc[:, 1], upad[j][:, 1:1 + S], tap_w(1), None,
                                                ALU.mult)
                        for t in range(2, TAPS):
                            if t % 2 == 0:
                                dve.drain()
                            nc.vector.scalar_tensor_tensor(acc[:, t % 2], upad[j][:, t:t + S],
                                                           tap_w(t), acc[:, t % 2], ALU.mult, ALU.add)
                        dve.drain()
                        nc.vector.tensor_tensor(cv[:, it * 2 + j], acc[:, 0], acc[:, 1], ALU.add)
                        dve.drain()
                    turns(dve, KT, one, 2)
            took(16, 16)

            def silu_ln(k):
                nc.scalar.activation(cv[:, k], cv[:, k], ACT.Silu, scale=pcol("cv_ln_w", k),
                                     bias=pcol("cv_ln_b", k))
            norm("r_cv", cv, cv, 44, silu_ln, mean=True)
            merge(hn, cv, mg, 48, False)
            if upto == 3:
                dump_tiles(24, 8)
                return

            def add_gated(gate_at, n_w, blocks_of, act_of):
                w0, o0 = w_at[0], o_at[0]
                with nc.Block() as block:
                    @block.sync
                    def _(sp):
                        refill(sp, w0, n_w)

                    @block.tensor
                    def _(pe):
                        if blocks_of == KT:
                            project(pe, w0, o0, n_w, lambda j, k: act_of(k))
                        else:
                            for m in range(KT):
                                for k in range(blocks_of):
                                    i = m * blocks_of + k
                                    if i % KT == 0:
                                        tile_ready(pe, w0, 0, i // KT)
                                    if k == 0:
                                        bank_ready(pe, o0, 0, m)
                                    last = nc.tensor.matmul(
                                        psum[:, (o0 + m) % NBANK],
                                        slot((w0 + i // KT) % RING)[:, i % KT], act_of(k),
                                        start=(k == 0), stop=(k == blocks_of - 1))
                                    if i % KT == KT - 1:
                                        last.then_inc(w_used, 1)

                    @block.vector
                    def _(dve):
                        for m in range(KT):
                            dve.wait_ge(w_used, w0 + -(-(m + 1) * blocks_of // KT))
                            nc.vector.scalar_tensor_tensor(
                                x[:, m], psum[:, (o0 + m) % NBANK], mod[:, gate_at + m, 0:1], x[:, m],
                                ALU.mult, ALU.add).then_inc(bank_free[(o0 + m) % NBANK], 1)
                took(n_w, KT)

            add_gated(16, 8, KT, lambda k: mg[:, k])
            if upto == 4:
                dump_tiles(0, 8)
                return

            norm("r_n2", x, hn, 76, affine(hn, lambda k: a2[:, k:k + 1],
                                           lambda k: mod[:, 24 + k, 0:1]))
            GW, GH = 64, 8
            PW, PH = GW + 2, GH + 2
            gt = tiles(24, FT)
            grid = [arena[:, (46 + 2 * b) * S:(46 + 2 * b) * S + PW * PH].rearrange(
                "p (r c) -> p r c", c=PW) for b in range(2)]
            acc = [tiles(50 + 2 * b, 2) for b in range(2)]
            ge = tiles(54, 2)
            u_in, u_used = sem("f_u_in"), sem("f_u_used")
            cv_done, ge_done = sem("f_cv_done"), sem("f_ge_done")
            w0, o0 = w_at[0], o_at[0]
            zeros = sem("f_zeros")
            with nc.Block() as block:
                @block.sync
                def _(sp):
                    refill(sp, w0, 2 * FT)

                @block.tensor
                def _(pe):
                    project(pe, w0, o0, 2 * FT, lambda j, k: hn[:, k])

                @block.scalar
                def _(act):
                    act.wait_ge(zeros, 1)

                    def load(it, j):
                        act.wait_ge(w_used, it * 4 + (w0 + 2 * j + 1))
                        act.wait_ge(u_used, it * 2 + j + 1)
                        b = (o0 + 2 * j) % NBANK
                        nc.scalar.activation(grid[j][:, 1:GH + 1, 1:GW + 1],
                                             psum[:, b].rearrange("p (r c) -> p r c", c=GW), ACT.Copy)
                        act.drain().then_inc(bank_free[b], 1)
                        act.sem_inc(u_in, 1)

                    def gelu(it, j):
                        act.wait_ge(cv_done, it * 2 + j + 1)
                        nc.scalar.activation(ge[:, j], acc[j][:, 0], ACT.Gelu,
                                             bias=par[:, bass.ds(it * 2 + (PCOL["ffn_b"] + j), 1)]
                                             ).then_inc(ge_done, 1)

                    def one(it, j):
                        load(it, j)
                        if j == 1:
                            gelu(it, 0)
                            gelu(it, 1)
                    turns(act, FT, one, 2)

                @block.vector
                def _(dve):
                    for b in range(2):
                        nc.vector.memset(grid[b], 0.0)
                    dve.drain().then_inc(zeros, 1)
                    dve.sem_inc(u_used, 2)

                    def conv(it, j):
                        dve.wait_ge(u_in, it * 2 + j + 1)
                        for t in range(9):
                            src = grid[j][:, t // 3:t // 3 + GH, t % 3:t % 3 + GW]
                            w_t = par[:, bass.ds(it * 2 + (PCOL["ffn_w"] + FT * t + j), 1)]
                            a = acc[j][:, t % 2].rearrange("p (r c) -> p r c", c=GW)
                            if t and t % 2 == 0:
                                dve.drain()
                            if t < 2:
                                nc.vector.tensor_scalar(a, src, w_t, None, ALU.mult)
                            else:
                                nc.vector.scalar_tensor_tensor(a, src, w_t, a, ALU.mult, ALU.add)
                        dve.drain().then_inc(u_used, 1)
                        nc.vector.tensor_tensor(acc[j][:, 0], acc[j][:, 0], acc[j][:, 1], ALU.add)
                        dve.drain().then_inc(cv_done, 1)

                    def mul(it, j):
                        dve.wait_ge(w_used, it * 4 + (w0 + 2 * j + 2))
                        dve.wait_ge(ge_done, it * 2 + j + 1)
                        b = (o0 + 2 * j + 1) % NBANK
                        nc.vector.tensor_tensor(gt[:, it * 2 + j], ge[:, j], psum[:, b],
                                                ALU.mult)
                        dve.drain().then_inc(bank_free[b], 1)

                    def one(it, j):
                        conv(it, j)
                        if j == 1:
                            mul(it, 0)
                            mul(it, 1)
                    turns(dve, FT, one, 2)
            took(2 * FT, 2 * FT)
            if upto == 7:
                dump_tiles(24, 22)
                return
            add_gated(40, FT, FT, lambda k: gt[:, k])
            if upto == 8:
                dump_tiles(0, 8)
                return

            def times(k):
                nc.scalar.activation(x[:, k], x[:, k], ACT.Copy, scale=pcol("final_w", k))
            norm("r_out", x, x, 76, times)
            stored = sem("stored")
            with nc.Block() as block:
                @block.sync
                def _(sp):
                    sp.dma_start(out_t.rearrange("(k p) n -> p k n", p=P), x).then_inc(stored, 16)
                    sp.wait_ge(stored, 16)

        if 1 in parts:
            first_block()
        if 2 in parts:
            hybrid_block()
        if 3 in parts:
            recurrent_block()


def blocks(w):
    k, n = w.shape
    b = w.reshape(k // P, P, n // P, P).transpose(2, 0, 1, 3).reshape(-1, 8, P, P)
    return b.transpose(0, 2, 1, 3).reshape(-1, P, 1024)


def wide_blocks(w):
    k, n = w.shape
    b = w.reshape(k // (2 * P), 2, P, n // S, S).transpose(3, 0, 2, 1, 4)
    return b.reshape(-1, P, 1024)


def cols(v):
    return v.reshape(-1, P).T


def host(inp):
    a = {k: np.asarray(v) for k, v in inp.items()}
    ws = [blocks(a["w_in_a"][0][:, :2048]), blocks(a["w_in_a"][0][:, 2048:])]
    g = a["w_grp_a"][0].reshape(4, 4, P, 4, P).transpose(0, 3, 1, 2, 4).reshape(8, 8, P, P)
    ws += [g.transpose(0, 2, 1, 3).reshape(8, P, 1024), blocks(a["w_out_a"][0])]
    wb, wk = a["w_in_b"][0], a["w_kv"]
    for half in range(2):
        at = 512 * half
        ws += [blocks(wb[:, 1024 * i + at:1024 * i + at + 512]) for i in range(3)]
        ws += [blocks(wk[:, 1024 * i + at:1024 * i + at + 512]) for i in range(3)]
        ws += [blocks(wb[:, 3072 + at:3072 + at + 512])]
        ws += [wide_blocks(wk[:, 3072 + 1024 * i + at:3072 + 1024 * i + at + 512]) for i in range(3)]
    ws += [blocks(a["w_out_b"][0])]
    first = ws
    ws = [blocks(a["w_ada_2"][0])]
    w = a["w_in_2"][0]
    order = np.concatenate([c * D + m * P + np.arange(P) for m in range(KT) for c in (1, 2, 0, 3)])
    ws.append(blocks(w[:, order]))
    b0 = 4 * D
    c0 = b0 + 2 * D + 6 * 256 + 48
    g0 = c0 + 3 * D

    def gated(gate_w, branch_w):
        pair = np.stack([blocks(gate_w), blocks(branch_w)], axis=1)
        return pair.reshape(-1, P, 1024)

    def branch(i):
        return gated(w[:, g0 + i * D:g0 + (i + 1) * D], a["w_br_2"][0, i])
    ws.append(branch(0))
    kv = b0 + D
    ws.append(blocks(np.concatenate([w[:, b0:kv + 768], w[:, kv + 1024:kv + 1280],
                                     w[:, kv + 1536:kv + 1536 + D]], axis=1)))
    ws.append(wide_blocks(np.concatenate([w[:, kv + 768:kv + 1024], w[:, kv + 1280:kv + 1536]], axis=1)))
    ws.append(branch(1))
    ws += [wide_blocks(w[:, c0 + D:c0 + 2 * D]), blocks(w[:, c0:c0 + D]), blocks(w[:, c0 + 2 * D:c0 + 3 * D])]
    ws.append(branch(2))
    ws.append(blocks(a["w_out_2"][0]))
    second = ws
    gl = w[:, kv + 1536 + D:c0]
    extra = {
        "w_gl": gl.reshape(KT, P, 48).transpose(1, 0, 2).reshape(P, -1),
        "w_ck1": a["w_ck1_2"][0], "w_cv1": a["w_cv1_2"][0],
        "w_c2": np.concatenate([a["w_ck2_2"][0], a["w_cv2_2"][0]], axis=1),
        "pos": np.concatenate([np.concatenate([a["pos_ck_2"][0].T] * 2),
                               np.concatenate([a["pos_cv_2"][0].T] * 2)], axis=1),
        "ln_bc": np.broadcast_to(np.concatenate([a["ln_g_2"][0], a["ln_b_2"][0]]), (P, 2 * D)),
        "w_s": a["w_s_2"][0].transpose(2, 0, 1).reshape(P, -1),
        "b_s": a["b_s_2"][0].reshape(1, -1),
    }
    par = {n: np.zeros((P, c), np.float32) for n, c in PARAMS}
    par["scale_a"] = cols(a["scale_a"])
    par["ln_g"], par["ln_b"] = cols(a["ln_g"]), cols(a["ln_b"])
    for name, key in (("g_pre", "g_pre_2"), ("g_post", "g_post_2"), ("c_2", "c_2"),
                      ("b_ada", "b_ada_2"), ("conv_w", "conv_w_2"), ("conv_b", "conv_b_2")):
        par[name] = cols(a[key])
    w = a["w_in_3"][0]
    part = [w[:, i * D:(i + 1) * D] for i in range(9)]
    heads = np.concatenate([part[i][:, m * P:(m + 1) * P] for m in range(KT) for i in (0, 1, 2, 4)],
                           axis=1)
    up = a["w_up_3"][0]
    ff = FT * P
    third = [blocks(a["w_mod_3"][0]), wide_blocks(part[3]), blocks(heads),
             gated(part[7], a["w_hg_out_3"][0]), gated(part[5], part[6]),
             gated(part[8], a["w_cv_out_3"][0]), blocks(a["w_out_3"][0]),
             gated(up[:, :ff], up[:, ff:]), blocks(a["w_down_3"][0])]
    par["c_3"] = np.stack([cols(a["c_3"]), cols(a["c_ctx_3"])], axis=2).reshape(P, 16)
    for name, key in (("b_mod", "b_mod_3"), ("norm1_w", "norm1_w_3"), ("gnorm_w", "hg_gnorm_w_3"),
                      ("cv_w", "cv_dw_w_3"), ("cv_b", "cv_dw_b_3"), ("cv_ln_w", "cv_ln_w_3"),
                      ("cv_ln_b", "cv_ln_b_3"), ("norm2_w", "norm2_w_3"), ("ffn_w", "ffn_dw_w_3"),
                      ("ffn_b", "ffn_dw_b_3"), ("final_w", "final_norm_w_3")):
        par[name] = cols(a[key])
    extra["ctx_t"] = a["ctx_3"][0].T
    return (first, second, third), par, extra, a


def tables():
    i = np.arange(1, 49, dtype=np.float32)
    s1 = (2.0 ** (-8.0 * i / 48)).astype(np.float32)
    i = np.arange(1, 17, dtype=np.float32)
    s2 = (2.0 ** (-8.0 * i / 16)).astype(np.float32)
    fix = np.ones((4, 16), np.float32)
    for g, w in enumerate(WINDOWS):
        fix[g, :w] = w / np.arange(1, w + 1, dtype=np.float32)
    p = np.arange(P)
    valid = np.ones((P, 4), np.float32)
    valid[:31, 0] = 0
    con = np.concatenate([
        np.broadcast_to(-s1, (P, 48)), np.broadcast_to(-s2, (P, 16)), valid,
        np.broadcast_to(fix.reshape(-1), (P, 64)), np.eye(P), np.full((P, P), 1 / D),
        np.full((P, P), 1 / P), np.full((P, 1), EPS), np.full((P, 1), LN_EPS)], axis=1)
    d = 4 * p[:, None] + 3 - np.arange(S + 3)[None, :]
    dist0 = np.where((d >= 0) & (d <= 128), d, MASKED)
    d = p[:, None] - p[None, :]
    dist12 = np.concatenate([np.where(d >= 0, 4 * d, MASKED),
                             np.where((d >= 0) & (d % 4 == 0), 4 * d, MASKED)], axis=1)
    c = np.arange(S)[None, :] - 384
    rel = np.where(p[:, None] >= c, p[:, None] - c, MASKED)
    t = P * np.arange(4)[None, :, None] + p[:, None, None]
    d = t - 16 * np.arange(N_CMP)[None, None, :] - 31
    cmp_dist = np.where(d >= 0, d, MASKED).reshape(P, -1)
    out = {"con": con, "dist0": dist0, "dist12": dist12, "rel": rel, "cmp_dist": cmp_dist}
    s, t = p[:, None], p[None, :]
    masks = []
    for level in range(LEVELS):
        pair = (s >> (level + 1)) == (t >> (level + 1))
        lower_s = ((s >> level) & 1) == 0
        lower_t = ((t >> level) & 1) == 0
        masks += [pair & lower_s & ~lower_t, pair & ~lower_s & lower_t]
    masks.append(s == t)
    out["gla_mask"] = np.concatenate(masks, axis=1)
    return {n: np.ascontiguousarray(v, dtype=np.float32) for n, v in out.items()}


def kernel(**inputs):
    import concourse.bacc as bacc
    from concourse.bass_utils import run_bass_kernel_spmd

    (first, second, third), par, extra, a = host(inputs)
    arrays = {"x_t": a["x"][0].T, "weights": np.concatenate(first + second + third),
              "par": np.concatenate([par[n] for n, _ in PARAMS], axis=1), **tables(), **extra}
    arrays = {f"in_{n}": np.ascontiguousarray(v) for n, v in arrays.items()}
    nc = bacc.Bacc("TRN2", target_bir_lowering=False, num_devices=1)
    d = {n[3:]: nc.dram_tensor(n, v.shape, mybir.dt.from_np(v.dtype), kind="ExternalInput").ap()
         for n, v in arrays.items()}
    out_t = nc.dram_tensor("out_t", (D, S), F32, kind="ExternalOutput").ap()
    build(nc, d, out_t)
    r = run_bass_kernel_spmd(nc, [arrays], core_ids=[0])
    return np.ascontiguousarray(r.results[0]["out_t"].T)[None]
```

```python
import math
import numpy as np
import concourse.bass as bass
from concourse import mybir
from contextlib import ExitStack

F32 = mybir.dt.float32
F32R = mybir.dt.float32r
ACT = mybir.ActivationFunctionType
ALU = mybir.AluOpType
AX = mybir.AxisListType

P = 128
S = 512
D = 1024
KT = D // P
DEPTH = 2
ALPHA = (2 * DEPTH) ** 0.25
LN_EPS = 1e-5
EPS = 1e-6
NH, HD, NG = 16, 64, 3
RING = 8
NBANK = 4
N_CMP = 31
FT = 22
WINDOWS = (2, 4, 8, 16)
MASKED = 1e33
CTX = 256
CH = 128
LEVELS = 7
ARENA = 84

PARAMS = [
    ("scale_a", 16), ("ln_g", 16), ("ln_b", 16),
    ("g_pre", 8), ("g_post", 8), ("c_2", 8), ("b_ada", 24), ("conv_w", 24), ("conv_b", 8),
    ("c_3", 16), ("b_mod", 48), ("norm1_w", 8), ("gnorm_w", 1), ("cv_w", 31 * 8),
    ("cv_b", 8), ("cv_ln_w", 8), ("cv_ln_b", 8), ("norm2_w", 8), ("ffn_w", 9 * FT),
    ("ffn_b", FT), ("final_w", 8),
]
CONSTS = [("neg_slope_1", 48), ("neg_slope_2", 16), ("cmp_valid", 4), ("pool_fix", 64),
          ("identity", 128), ("mean_d", 128), ("mean_h", 128), ("eps", 1), ("eps_ln", 1)]


def columns(spec):
    at, out = 0, {}
    for name, n in spec:
        out[name] = at
        at += n
    return out, at


PCOL, NPAR = columns(PARAMS)
CCOL, NCON = columns(CONSTS)


def build(nc, d, out_t):
    weights = d["weights"]
    n_tiles = weights.shape[0]
    ctx = ExitStack()
    with ctx:
        def sb(name, n):
            return ctx.enter_context(nc.sbuf_tensor(name, [P, n], F32))

        def sem(name):
            return ctx.enter_context(nc.semaphore(name))

        arena = sb("arena", ARENA * S)
        arena_at = nc.sbuf_base - ARENA * S * 4
        rounded = {}

        def as_r(t0, n):
            if (t0, n) not in rounded:
                rounded[t0, n] = nc.alloc_sbuf_tensor_at(f"arena_r_{t0}_{n}", [P, n * S], F32R,
                                                         offset=arena_at + t0 * S * 4)
            return rounded[t0, n][:, 0:n * S]

        ring = sb("ring", RING * 1024)
        par = sb("par", NPAR)
        con = sb("con", NCON)
        small = sb("small", 256)
        psum = ctx.enter_context(nc.psum_tensor("psum", [P, 8, S], F32))

        def slot(s):
            return ring[:, s * 1024:(s + 1) * 1024].rearrange("p (b m) -> p b m", m=P)

        def wide(s):
            return ring[:, s * 1024:(s + 1) * 1024].rearrange("p (b m) -> p b m", m=S)

        def tiles(t0, n):
            return arena[:, t0 * S:(t0 + n) * S].rearrange("p (k n) -> p k n", n=S)

        def pcol(name, i=0):
            return par[:, PCOL[name] + i:PCOL[name] + i + 1]

        def ccol(name, i=0, n=1):
            return con[:, CCOL[name] + i:CCOL[name] + i + n]

        ident = ccol("identity", 0, P)
        mean_d = ccol("mean_d", 0, P)
        mean_h = ccol("mean_h", 0, P)

        w_in = [sem(f"w_in{s}") for s in range(RING)]
        w_used = sem("w_used")
        bank_free = [sem(f"bank_free{b}") for b in range(NBANK)]
        par_in = sem("par_in")
        tab_in = sem("tab_in")
        pool_in = sem("pool_in")
        split_begun = sem("split_begun")
        w_split = sem("w_split")
        hi_in = sem("hi_in")
        lo_in = sem("lo_in")
        splits, cuts = [0], [0]
        pool_at = [0]
        w_at = [0]
        o_at = [0]
        tab_at = [0]

        def turns(eng, n, body, unroll=RING):
            full = n // unroll
            if full > 1:
                with eng.Fori(0, full) as it:
                    for j in range(unroll):
                        body(it, j)
            elif full == 1:
                for j in range(unroll):
                    body(0, j)
            for j in range(n % unroll):
                body(full, j)

        def refill(sp, w0, n):
            n = min(n, n_tiles - RING - w0)

            def load(it, j):
                s = (w0 + j) % RING
                sp.wait_ge(w_used, it * RING + w0 + j + 1)
                sp.dma_start(ring[:, s * 1024:(s + 1) * 1024],
                             weights[it * RING + (w0 + j + RING)]).then_inc(w_in[s], 16)

            if n > 0:
                turns(sp, n, load)

        def tile_ready(pe, w0, it, j):
            pe.wait_ge(w_in[(w0 + j) % RING], it * 16 + ((w0 + j) // RING + 1) * 16)

        def bank_ready(pe, o0, it, j, per_turn=RING):
            pe.wait_ge(bank_free[(o0 + j) % NBANK],
                       it * (per_turn // NBANK) + ((o0 + j) // NBANK + 1))

        def project(pe, w0, o0, n, act, per_out=1):
            def one(it, j):
                tile_ready(pe, w0, it, j)
                part = j % per_out
                if part == 0:
                    bank_ready(pe, o0, it, j // per_out, RING // per_out)
                for k in range(KT):
                    last = nc.tensor.matmul(
                        psum[:, (o0 + j // per_out) % NBANK], slot((w0 + j) % RING)[:, k],
                        act(j, part * KT + k), start=(part == 0 and k == 0),
                        stop=(part == per_out - 1 and k == KT - 1))
                last.then_inc(w_used, 1)

            turns(pe, n, one)

        def project_wide(pe, w0, o0, n_groups, tok):
            for g in range(n_groups):
                for q in range(4):
                    tile_ready(pe, w0, 0, 4 * g + q)
                    for kk in range(2):
                        for j in range(4):
                            if q == 0 and kk == 0:
                                bank_ready(pe, o0, 0, 4 * g + j)
                            last = nc.tensor.matmul(psum[:, (o0 + j) % NBANK],
                                                    tok(g, 2 * q + kk, j),
                                                    wide((w0 + 4 * g + q) % RING)[:, kk],
                                                    start=(q == 0 and kk == 0),
                                                    stop=(q == 3 and kk == 1))
                    last.then_inc(w_used, 1)

        def cut(src, hi0, lo0, n=KT):
            c = {"src": src, "hi": [as_r(hi0 + k, 1) for k in range(n)],
                 "lo": [as_r(lo0 + k, 1) for k in range(n)], "n": n, "at": cuts[0]}
            cuts[0] += n
            return c

        def cut_hi(act, c):
            for k in range(c["n"]):
                nc.scalar.activation(c["hi"][k], c["src"][:, k], ACT.Copy).then_inc(hi_in, 1)

        def cut_lo(dve, c):
            for k in range(c["n"]):
                dve.wait_ge(hi_in, c["at"] + k + 1)
                nc.vector.tensor_tensor(c["lo"][k], c["src"][:, k], c["hi"][k].bitcast(F32),
                                        ALU.subtract).then_inc(lo_in, 1)

        def cut_wait(pe, c):
            pe.wait_ge(lo_in, c["at"] + c["n"])

        def split_tile(ws0, b):
            return as_r(ws0 + 2 * b, 2), as_r(ws0 + 4 + 2 * b, 2)

        def split_weights(pool, w0, n, ws0):
            def one(it, j):
                tile_ready(pool, w0, it, j)
                if w0 + j >= 2:
                    pool.wait_ge(w_used, it * RING + (w0 + j - 1))
                src = ring[:, (w0 + j) % RING * 1024:((w0 + j) % RING + 1) * 1024]
                hi, lo = split_tile(ws0, j % 2)
                pool.sem_inc(split_begun, 1)
                nc.gpsimd.tensor_scalar(hi, src, 1.0, 1.0, ALU.mult, ALU.mult)
                pool.drain()
                nc.gpsimd.tensor_tensor(lo, src, hi.bitcast(F32), ALU.subtract)
                pool.drain().then_inc(w_split, 1)

            if w0 == 0:
                for t in range(n):
                    one(0, t)
            else:
                turns(pool, n, one)

        def project3(pe, w0, o0, n, ws0, s0, hi, lo, per_out=1, b0=0):
            def one(it, j):
                pe.wait_ge(w_split, it * RING + (s0 + j + 1))
                part = j % per_out
                if part == 0:
                    bank_ready(pe, o0, it, j // per_out, RING // per_out)
                w_hi, w_lo = (w.rearrange("p (b m) -> p b m", m=P) for w in split_tile(ws0, (b0 + j) % 2))
                out = psum[:, (o0 + j // per_out) % NBANK]
                for k in range(KT):
                    kk = part * KT + k
                    nc.tensor.matmul(out, w_hi[:, k], hi(j, kk), start=(kk == 0), stop=False)
                    nc.tensor.matmul(out, w_hi[:, k], lo(j, kk), start=False, stop=False)
                    last = nc.tensor.matmul(out, w_lo[:, k], hi(j, kk), start=False,
                                            stop=(kk == per_out * KT - 1))
                last.then_inc(w_used, 1)

            turns(pe, n, one)

        def project_wide3(pe, w0, o0, n_groups, ws0, s0, hi, lo):
            for g in range(n_groups):
                for q in range(4):
                    pe.wait_ge(w_split, s0 + 4 * g + q + 1)
                    w_hi, w_lo = (w.rearrange("p (b m) -> p b m", m=S)
                                  for w in split_tile(ws0, q % 2))
                    for kk in range(2):
                        for j in range(4):
                            first, end = q == 0 and kk == 0, q == 3 and kk == 1
                            if first:
                                bank_ready(pe, o0, 0, 4 * g + j)
                            out, k = psum[:, (o0 + j) % NBANK], 2 * q + kk
                            nc.tensor.matmul(out, hi(g, k, j), w_hi[:, kk], start=first, stop=False)
                            nc.tensor.matmul(out, lo(g, k, j), w_hi[:, kk], start=False, stop=False)
                            last = nc.tensor.matmul(out, hi(g, k, j), w_lo[:, kk], start=False,
                                                    stop=end)
                    last.then_inc(w_used, 1)

        def split_took(n):
            at = splits[0]
            splits[0] += n
            return at

        def took(n_w, n_o):
            w_at[0] += n_w
            o_at[0] += n_o

        mean_in = sem("norm_mean_in")
        centred = sem("norm_centred")
        squared = sem("norm_squared")
        summed = sem("norm_summed")
        rooted = sem("norm_rooted")
        scaled = sem("norm_scaled")
        norms, means = [0], [0]
        sig_in = sem("sig_in")
        sig_used = sem("sig_used")
        merges = [0]

        def norm(z, h, sq0, finish, mean=False, eps="eps", n=S, add=None):
            sq, st = tiles(sq0, 2), tiles(sq0 + 2, 2)
            n0, m0 = norms[0], means[0]
            norms[0] += 1
            means[0] += mean
            with nc.Block() as block:
                @block.tensor
                def _(pe):
                    if mean:
                        for k in range(KT):
                            last = nc.tensor.matmul(psum[:, 4, :n], mean_d, z[:, k],
                                                    start=(k == 0), stop=(k == KT - 1))
                        last.then_inc(mean_in, 1)
                    for k in range(KT):
                        pe.wait_ge(squared, KT * n0 + k + 1)
                        nc.tensor.matmul(psum[:, 5, :n], mean_d, sq[:, k % 2, :n], start=(k == 0),
                                         stop=(k == KT - 1)).then_inc(summed, 1)

                @block.scalar
                def _(act):
                    for k in range(KT):
                        if mean:
                            act.wait_ge(centred, KT * m0 + k + 1)
                        if k >= 2:
                            act.wait_ge(summed, KT * n0 + k - 1)
                        nc.scalar.activation(sq[:, k % 2, :n], z[:, k],
                                             ACT.Square).then_inc(squared, 1)
                    act.wait_ge(summed, KT * (n0 + 1))
                    nc.scalar.activation(st[:, 0, :n], psum[:, 5, :n], ACT.Sqrt,
                                         bias=ccol(eps)).then_inc(rooted, 1)
                    if finish is not None:
                        for k in range(KT):
                            act.wait_ge(scaled, KT * n0 + k + 1)
                            finish(k)

                @block.vector
                def _(dve):
                    if mean:
                        dve.wait_ge(mean_in, m0 + 1)
                        for k in range(KT):
                            nc.vector.tensor_tensor(z[:, k], z[:, k], psum[:, 4, :n],
                                                    ALU.subtract).then_inc(centred, 1)
                    dve.wait_ge(rooted, n0 + 1)
                    nc.vector.reciprocal(st[:, 1, :n], st[:, 0, :n])
                    dve.drain()
                    for k in range(KT):
                        nc.vector.tensor_tensor(h[:, k], z[:, k], st[:, 1, :n],
                                                ALU.mult).then_inc(scaled, 1)
                    if add is not None:
                        dve.drain()
                        for k in range(KT):
                            add(k)

        def affine(t, scale_of, bias_of):
            def finish(k):
                nc.scalar.activation(t[:, k], t[:, k], ACT.Identity, scale=scale_of(k),
                                     bias=bias_of(k))
            return finish

        def merge(gate, branch, out, sg0, first, ws0, make):
            s0 = split_took(2 * KT)
            sgm = tiles(sg0, 2)
            n0 = KT * merges[0]
            merges[0] += 1
            w0, o0 = w_at[0], o_at[0]
            with nc.Block() as block:
                @block.sync
                def _(sp):
                    refill(sp, w0, 2 * KT)

                @block.tensor
                def _(pe):
                    for c in make:
                        cut_wait(pe, c)
                    project3(pe, w0, o0, 2 * KT, ws0, s0,
                             lambda j, k: (branch if j % 2 else gate)["hi"][k],
                             lambda j, k: (branch if j % 2 else gate)["lo"][k])

                @block.gpsimd
                def _(pool):
                    split_weights(pool, w0, 2 * KT, ws0)

                @block.scalar
                def _(act):
                    for c in make:
                        cut_hi(act, c)

                    def one(it, j):
                        act.wait_ge(w_used, it * 4 + (w0 + 2 * j + 1))
                        act.wait_ge(sig_used, it * 2 + (n0 + j + 1))
                        b = (o0 + 2 * j) % NBANK
                        nc.scalar.activation(sgm[:, j], psum[:, b], ACT.Sigmoid)
                        act.drain().then_inc(bank_free[b], 1)
                        act.sem_inc(sig_in, 1)
                    turns(act, KT, one, 2)

                @block.vector
                def _(dve):
                    for c in make:
                        cut_lo(dve, c)

                    def one(it, j):
                        dve.wait_ge(w_used, it * 4 + (w0 + 2 * j + 2))
                        dve.wait_ge(sig_in, it * 2 + (n0 + j + 1))
                        b = (o0 + 2 * j + 1) % NBANK
                        m = it * 2 + j
                        if first:
                            nc.vector.tensor_tensor(out[:, m], sgm[:, j], psum[:, b],
                                                    ALU.mult)
                            dve.drain().then_inc(bank_free[b], 1)
                            dve.sem_inc(sig_used, 1)
                        else:
                            nc.vector.tensor_tensor(sgm[:, j], sgm[:, j], psum[:, b], ALU.mult)
                            dve.drain().then_inc(bank_free[b], 1)
                            nc.vector.tensor_tensor(out[:, m], out[:, m], sgm[:, j],
                                                    ALU.add).then_inc(sig_used, 1)
                    turns(dve, KT, one, 2)
            took(2 * KT, 2 * KT)

        def modulation(vec, n_vec, n_out, dst, bias):
            w0 = w_at[0]
            with nc.Block() as block:
                @block.sync
                def _(sp):
                    refill(sp, w0, n_out)

                @block.tensor
                def _(pe):
                    for t in range(n_out // RING):
                        for j in range(RING):
                            tile_ready(pe, w0, 0, RING * t + j)
                            m = RING * t + j
                            for k in range(KT):
                                last = nc.tensor.matmul(
                                    psum[:, 6, n_vec * m:n_vec * m + n_vec],
                                    slot((w0 + j) % RING)[:, k], vec[:, k, :], start=(k == 0),
                                    stop=(k == KT - 1))
                            last.then_inc(w_used, 1)

                @block.vector
                def _(dve):
                    dve.wait_ge(w_used, w0 + n_out)
                    for i in range(n_vec):
                        nc.vector.tensor_tensor(
                            dst[:, :, i], psum[:, 6, 0:n_vec * n_out].rearrange(
                                "p (m i) -> p m i", i=n_vec)[:, :, i], bias, ALU.add)
            took(n_out, 0)

        with nc.Block() as block:
            @block.sync
            def _(sp):
                sp.dma_start(tiles(0, KT), d["x_t"].rearrange("(k p) n -> p k n", p=P)).then_inc(par_in, 16)
                sp.dma_start(con[:], d["con"]).then_inc(par_in, 16)
                sp.dma_start(par[:], d["par"]).then_inc(par_in, 16)
                for s in range(RING):
                    sp.dma_start(ring[:, s * 1024:(s + 1) * 1024], weights[s]).then_inc(w_in[s], 16)
                sp.wait_ge(par_in, 48)

            @block.vector
            def _(dve):
                for b in range(NBANK):
                    dve.sem_inc(bank_free[b], 1)
                dve.sem_inc(sig_used, 2)

        def first_block():
            X0, PL0, SG0 = 0, 8, 24
            x_in, pooled, sg = tiles(X0, KT), tiles(PL0, 16), tiles(SG0, 16)
            PADS = 16
            WID = PADS + S
            ubuf = [arena[:, 40 * S + b * WID:40 * S + (b + 1) * WID] for b in range(2)]
            sbuf = [arena[:, 44 * S + b * WID:44 * S + (b + 1) * WID] for b in range(2)]
            u_in = sem("u_in")
            u_free = sem("u_free")
            pads = sem("pads")
            w0, o0 = w_at[0], o_at[0]
            x_cut, WS0 = cut(x_in, 48, 56), 64
            s0 = split_took(16)
            with nc.Block() as block:
                @block.sync
                def _(sp):
                    refill(sp, w0, 16)

                @block.gpsimd
                def _(pool):
                    split_weights(pool, w0, 16, WS0)

                @block.tensor
                def _(pe):
                    cut_wait(pe, x_cut)
                    project3(pe, w0, o0, 16, WS0, s0, lambda j, k: x_cut["hi"][k],
                             lambda j, k: x_cut["lo"][k])

                @block.scalar
                def _(act):
                    cut_hi(act, x_cut)
                    act.wait_ge(pads, 1)
                    for o in range(16):
                        act.wait_ge(w_used, w0 + o + 1)
                        if o >= 2:
                            act.wait_ge(u_free, o - 1)
                        nc.scalar.activation(ubuf[o % 2][:, PADS:], psum[:, (o0 + o) % NBANK],
                                             ACT.Copy).then_inc(bank_free[(o0 + o) % NBANK], 1)
                        act.drain().then_inc(u_in, 1)

                @block.vector
                def _(dve):
                    for b in range(2):
                        nc.vector.memset(ubuf[b][:, :PADS], 0.0)
                        nc.vector.memset(sbuf[b][:, :PADS], 0.0)
                    dve.drain().then_inc(pads, 1)
                    cut_lo(dve, x_cut)
                    for o in range(16):
                        dve.wait_ge(u_in, o + 1)
                        g = o // 4
                        src = ubuf[o % 2]
                        u = src
                        for level in range(g + 1):
                            sh, dst = 1 << level, sbuf[level % 2]
                            nc.vector.tensor_tensor(dst[:, sh:], src[:, sh:], src[:, :WID - sh], ALU.add)
                            dve.drain()
                            src = dst
                        nc.vector.tensor_tensor(src[:, PADS:2 * PADS], src[:, PADS:2 * PADS],
                                                ccol("pool_fix", 16 * g, 16), ALU.mult)
                        dve.drain()
                        nc.vector.scalar_tensor_tensor(pooled[:, o], src[:, PADS:], 1.0 / WINDOWS[g],
                                                       u[:, PADS:], ALU.mult,
                                                       ALU.subtract).then_inc(u_free, 1)
                        dve.drain()
            took(16, 16)

            w0, o0 = w_at[0], o_at[0]
            s0 = split_took(16)
            with nc.Block() as block:
                @block.sync
                def _(sp):
                    refill(sp, w0, 16)

                @block.gpsimd
                def _(pool):
                    split_weights(pool, w0, 16, WS0)

                @block.tensor
                def _(pe):
                    project3(pe, w0, o0, 16, WS0, s0, lambda j, k: x_cut["hi"][k],
                             lambda j, k: x_cut["lo"][k])

                @block.scalar
                def _(act):
                    def one(it, j):
                        act.wait_ge(w_used, it * NBANK + w0 + j + 1)
                        nc.scalar.activation(sg[:, it * NBANK + j], psum[:, (o0 + j) % NBANK],
                                             ACT.Silu).then_inc(bank_free[(o0 + j) % NBANK], 1)
                    turns(act, 16, one, NBANK)
            took(16, 16)

            w0, o0 = w_at[0], o_at[0]
            with nc.Block() as block:
                @block.sync
                def _(sp):
                    refill(sp, w0, 8)

                @block.tensor
                def _(pe):
                    for j in range(8):
                        tile_ready(pe, w0, 0, j)
                        for half in range(2):
                            o = 2 * j + half
                            bank_ready(pe, o0, 0, o)
                            for k in range(4):
                                last = nc.tensor.matmul(psum[:, (o0 + o) % NBANK],
                                                        slot((w0 + j) % RING)[:, 4 * half + k],
                                                        pooled[:, 4 * (o // 4) + k],
                                                        start=(k == 0), stop=(k == 3))
                        last.then_inc(w_used, 1)

                @block.vector
                def _(dve):
                    def one(it, j):
                        dve.wait_ge(w_used, it * 2 + w0 + j // 2 + 1)
                        nc.vector.scalar_tensor_tensor(
                            sg[:, it * NBANK + j], psum[:, (o0 + j) % NBANK],
                            par[:, bass.ds(it * NBANK + (PCOL["scale_a"] + j), 1)], sg[:, it * NBANK + j],
                            ALU.mult, ALU.mult).then_inc(bank_free[(o0 + j) % NBANK], 1)
                    turns(dve, 16, one, NBANK)
            took(8, 16)

            Z0 = 8
            z = tiles(Z0, KT)
            w0, o0 = w_at[0], o_at[0]

            def residual(w0, o0, per_out, resid, c, ws0, z):
                s0 = split_took(8 * per_out)
                with nc.Block() as block:
                    @block.sync
                    def _(sp):
                        refill(sp, w0, 8 * per_out)

                    @block.gpsimd
                    def _(pool):
                        split_weights(pool, w0, 8 * per_out, ws0)

                    @block.scalar
                    def _(act):
                        cut_hi(act, c)

                    @block.tensor
                    def _(pe):
                        cut_wait(pe, c)
                        project3(pe, w0, o0, 8 * per_out, ws0, s0, lambda j, k: c["hi"][k],
                                 lambda j, k: c["lo"][k], per_out)

                    @block.vector
                    def _(dve):
                        cut_lo(dve, c)

                        def one(it, j):
                            dve.wait_ge(w_used, it * NBANK * per_out + w0 + (j + 1) * per_out)
                            nc.vector.scalar_tensor_tensor(
                                z[:, it * NBANK + j], resid[:, it * NBANK + j], ALPHA,
                                psum[:, (o0 + j) % NBANK], ALU.mult, ALU.add).then_inc(bank_free[(o0 + j) % NBANK], 1)
                        turns(dve, 8, one, NBANK)
                took(8 * per_out, 8)

            residual(w0, o0, 2, x_in, cut(sg, 40, 56, 16), 72, z)
            norm(z, x_in, 40, affine(x_in, lambda k: pcol("ln_g", k), lambda k: pcol("ln_b", k)),
                 mean=True, eps="eps_ln")

            h = tiles(0, KT)
            M0, Q0, K0, V0, ST0, S0, D0 = 8, 16, 28, 40, 52, 70, 78
            gated, qt, kt = tiles(M0, KT), tiles(Q0, 12), tiles(K0, 12)
            q_st = [tiles(ST0 + 6 * b, 3) for b in range(2)]
            k_st = [tiles(ST0 + 6 * b + 3, 3) for b in range(2)]
            v_st = [tiles(ST0 + 12 + 3 * b, 3).rearrange("p a (c m) -> p (a c) m", m=P) for b in range(2)]
            score = [arena[:, S0 * S + b * 768:S0 * S + (b + 1) * 768] for b in range(3)]
            prob_t = [arena[:, S0 * S + (3 + b) * 768:S0 * S + (4 + b) * 768] for b in range(2)]
            dist0 = arena[:, D0 * S:D0 * S + S + 3]
            dist12 = arena[:, D0 * S + S + 4:D0 * S + S + 260]
            nmax = [small[:, b:b + 1] for b in range(3)]
            rsum = [small[:, 3 + b:4 + b] for b in range(3)]
            rinv = [small[:, 6 + b:7 + b] for b in range(3)]
            with nc.Block() as block:
                @block.sync
                def _(sp):
                    sp.dma_start(dist0, d["dist0"]).then_inc(tab_in, 16)
                    sp.dma_start(dist12, d["dist12"]).then_inc(tab_in, 16)
                    sp.wait_ge(tab_in, 32)
            tab_at[0] += 32

            for half in range(2):
                w0, o0 = w_at[0], o_at[0]
                h_cut, WS0 = cut(h, 52, 60), 68
                s0 = split_took(40)
                with nc.Block() as block:
                    @block.sync
                    def _(sp):
                        refill(sp, w0, 40)

                    @block.gpsimd
                    def _(pool):
                        split_weights(pool, w0, 40, WS0)

                    @block.tensor
                    def _(pe):
                        cut_wait(pe, h_cut)
                        project3(pe, w0, o0, 28, WS0, s0, lambda j, k: h_cut["hi"][k],
                                 lambda j, k: h_cut["lo"][k])

                        def tokens(part):
                            def tok(g, k, j):
                                t = h_cut[part]
                                return t[k][:, j * P:(j + 1) * P] if g == 0 else t[k][:, j::4]
                            return tok
                        project_wide3(pe, w0 + 28, o0 + 28, NG, WS0, s0 + 28, tokens("hi"),
                                      tokens("lo"))

                    @block.vector
                    def _(dve):
                        cut_lo(dve, h_cut)

                    @block.scalar
                    def _(act):
                        cut_hi(act, h_cut)

                        def q_out(it, j):
                            act.wait_ge(w_used, it * NBANK + w0 + j + 1)
                            nc.scalar.activation(qt[:, it * NBANK + j], psum[:, (o0 + j) % NBANK],
                                                 ACT.Copy, scale=HD ** -0.5).then_inc(bank_free[(o0 + j) % NBANK], 1)
                        turns(act, 12, q_out, NBANK)

                        def k_out(it, j):
                            act.wait_ge(w_used, it * NBANK + w0 + 12 + j + 1)
                            nc.scalar.activation(kt[:, it * NBANK + j], psum[:, (o0 + j) % NBANK],
                                                 ACT.Copy).then_inc(bank_free[(o0 + j) % NBANK], 1)
                        turns(act, 12, k_out, NBANK)
                        for j in range(4):
                            act.wait_ge(w_used, w0 + 24 + j + 1)
                            nc.scalar.activation(gated[:, 4 * half + j], psum[:, (o0 + j) % NBANK],
                                                 ACT.Silu).then_inc(bank_free[(o0 + j) % NBANK], 1)
                        for g in range(NG):
                            act.wait_ge(w_used, w0 + 28 + 4 * g + 4)
                            for j in range(4):
                                nc.scalar.activation(tiles(V0 + 3 * j + g, 1)[:, 0],
                                                     psum[:, (o0 + j) % NBANK],
                                                     ACT.Copy).then_inc(bank_free[(o0 + j) % NBANK], 1)
                took(40, 40)

                n = f"a{half}_"
                staged = [sem(n + "staged0"), sem(n + "staged1")]
                qk_done = sem(n + "qk_done")
                qk_read = sem(n + "qk_read")
                max_done = sem(n + "max_done")
                exp_done = sem(n + "exp_done")
                p_done = sem(n + "p_done")
                tr_done = sem(n + "tr_done")
                pt_done = sem(n + "pt_done")
                pv_done = sem(n + "pv_done")
                out_read = sem(n + "out_read")
                UNITS = 16
                with nc.Block() as block:
                    @block.sync
                    def _(sp):
                        with sp.Fori(0, 2) as it:
                            for b in range(2):
                                sp.wait_ge(pv_done, it * UNITS + 8 * b + 1)
                                pair = it * 2 + b
                                for g in range(NG):
                                    sp.dma_start(q_st[b][:, g], qt[:, pair + 4 * g]).then_inc(staged[b], 16)
                                    sp.dma_start(k_st[b][:, g], kt[:, pair + 4 * g]).then_inc(staged[b], 16)
                                sp.dma_start(v_st[b], arena[:, V0 * S:(V0 + 12) * S].rearrange(
                                    "p (c a m) -> p c a m", a=4, m=P)[:, :, pair, :]).then_inc(staged[b], 16)

                    @block.tensor
                    def _(pe):
                        pe.sem_inc(tr_done, 3)
                        pe.sem_inc(pv_done, 9)

                        def unit(u):
                            return u // 8, 64 * (u // 4 % 2), u % 4

                        def qk(it, u):
                            b, off, r = unit(u)
                            if u % 8 == 0:
                                pe.wait_ge(staged[b], it * 112 + 112)
                            pe.wait_ge(qk_read, it * UNITS + u + 1)
                            bank = 2 * (u % 2)
                            nc.tensor.matmul(psum[:, bank], q_st[b][off:off + HD, 0, r::4],
                                             k_st[b][off:off + HD, 0], start=True, stop=True)
                            for g in (1, 2):
                                last = nc.tensor.matmul(psum[:, bank + 1, (g - 1) * P:g * P],
                                                        q_st[b][off:off + HD, g, r::4],
                                                        k_st[b][off:off + HD, g, r::4],
                                                        start=True, stop=True)
                            last.then_inc(qk_done, 1)

                        with pe.Fori(0, 2) as it:
                            qk(it, 0)
                            qk(it, 1)
                            for u in range(UNITS):
                                b, off, r = unit(u)
                                pe.wait_ge(p_done, it * UNITS + u + 1)
                                pe.wait_ge(pt_done, it * UNITS + u + 1)
                                for c in range(6):
                                    last = nc.tensor.transpose(
                                        psum[:, 4 + c // 4, (c % 4) * P:(c % 4 + 1) * P],
                                        score[u % 3][:, c * P:(c + 1) * P], ident)
                                last.then_inc(tr_done, 1)
                                if u + 2 < UNITS:
                                    qk(it, u + 2)
                                pe.wait_ge(pt_done, it * UNITS + u + 2)
                                if u % 8 == 0:
                                    pe.wait_ge(out_read, it * 2 + b + 1)
                                for c in range(6):
                                    vi = 3 * c if c < 4 else 3 * r + c - 3
                                    last = nc.tensor.matmul(psum[off:off + HD, 6 + b, r::4],
                                                            v_st[b][:, vi, off:off + HD],
                                                            prob_t[u % 2][:, c * P:(c + 1) * P],
                                                            start=(c == 0), stop=(c == 5))
                                last.then_inc(pv_done, 1)

                    @block.vector
                    def _(dve):
                        dve.sem_inc(qk_read, 2)
                        dve.sem_inc(out_read, 2)

                        def front(it, u):
                            pair, head, r = u // 8, u // 4, u % 4
                            sc = score[u % 3]
                            bank = 2 * (u % 2)
                            dve.wait_ge(qk_done, it * UNITS + u + 1)
                            dve.wait_ge(tr_done, it * UNITS + u + 1)

                            def slope(g):
                                return con[:, bass.ds(it * 4 + (CCOL["neg_slope_1"] + g * NH + 8 * half + head), 1)]
                            nc.vector.scalar_tensor_tensor(sc[:, 0:S], dist0[:, 3 - r:3 - r + S], slope(0), psum[:, bank],
                                                           ALU.mult, ALU.add)
                            nc.vector.scalar_tensor_tensor(sc[:, S:S + P], dist12[:, 0:P], slope(1),
                                                           psum[:, bank + 1, 0:P], ALU.mult, ALU.add)
                            nc.vector.scalar_tensor_tensor(sc[:, S + P:], dist12[:, P:], slope(2),
                                                           psum[:, bank + 1, P:2 * P], ALU.mult,
                                                           ALU.add).then_inc(qk_read, 1)
                            dve.drain()
                            nc.vector.tensor_reduce(nmax[u % 3], sc, axis=AX.X, op=ALU.max,
                                                    negate=True).then_inc(max_done, 1)

                        def back(it, u):
                            dve.wait_ge(exp_done, it * UNITS + u + 1)
                            nc.vector.reciprocal(rinv[u % 3], rsum[u % 3])
                            dve.drain()
                            nc.vector.tensor_scalar(score[u % 3], score[u % 3], rinv[u % 3], None,
                                                    ALU.mult).then_inc(p_done, 1)

                        def gate(it, b):
                            dve.wait_ge(pv_done, it * UNITS + 8 * (b + 1) + 9)
                            t = gated[:, it * 2 + (4 * half + b)]
                            nc.vector.tensor_tensor(t, psum[:, 6 + b], t, ALU.mult).then_inc(out_read, 1)

                        with dve.Fori(0, 2) as it:
                            front(it, 0)
                            front(it, 1)
                            for u in range(UNITS):
                                back(it, u)
                                if u + 2 < UNITS:
                                    front(it, u + 2)
                                if u == 9:
                                    gate(it, 0)
                            gate(it, 1)
                            dve.drain()

                    @block.scalar
                    def _(act):
                        act.sem_inc(pt_done, 1)

                        def exp(it, u):
                            act.wait_ge(max_done, it * UNITS + u + 1)
                            nc.scalar.activation(score[u % 3], score[u % 3], ACT.Exp, bias=nmax[u % 3],
                                                 accum_out=rsum[u % 3])
                            act.drain().then_inc(exp_done, 1)

                        with act.Fori(0, 2) as it:
                            exp(it, 0)
                            exp(it, 1)
                            for u in range(UNITS):
                                act.wait_ge(tr_done, it * UNITS + u + 4)
                                act.wait_ge(pv_done, it * UNITS + u + 8)
                                nc.scalar.activation(prob_t[u % 2], psum[:, 4:6].rearrange(
                                    "p a n -> p (a n)")[:, 0:768], ACT.Copy).then_inc(pt_done, 1)
                                if u + 2 < UNITS:
                                    exp(it, u + 2)

            w0, o0 = w_at[0], o_at[0]
            Z0 = 16
            z = tiles(Z0, KT)
            residual(w0, o0, 1, h, cut(gated, 40, 48), 56, z)
            norm(z, h, 40, affine(h, lambda k: pcol("ln_g", 8 + k), lambda k: pcol("ln_b", 8 + k)),
                 mean=True, eps="eps_ln")

        def hybrid_block():
            x, hn, y, mg = tiles(0, KT), tiles(8, KT), tiles(16, KT), tiles(24, KT)
            mod = small[:, 16:40].rearrange("p (m i) -> p m i", i=1)
            a_col, g_col = small[:, 40:48], small[:, 48:56]
            c_silu = small[:, 56:64]

            with nc.Block() as block:
                @block.scalar
                def _(act):
                    nc.scalar.activation(c_silu, par[:, PCOL["c_2"]:PCOL["c_2"] + 8], ACT.Silu)
            modulation(c_silu.rearrange("p (k i) -> p k i", i=1), 1, 24, mod,
                       par[:, PCOL["b_ada"]:PCOL["b_ada"] + 24])
            with nc.Block() as block:
                @block.vector
                def _(dve):
                    nc.vector.scalar_tensor_tensor(a_col, small[:, 24:32], 1.0,
                                                   par[:, PCOL["g_pre"]:PCOL["g_pre"] + 8],
                                                   ALU.add, ALU.mult)
                    nc.vector.tensor_tensor(g_col, small[:, 32:40],
                                            par[:, PCOL["g_post"]:PCOL["g_post"] + 8], ALU.mult)
            norm(x, hn, 72, affine(hn, lambda k: a_col[:, k:k + 1],
                                            lambda k: small[:, 16 + k:17 + k]))

            TAPS = 3
            YW = S + TAPS - 1
            cg = tiles(72, 2)
            zs = tiles(74, 2)
            ypad = [arena[:, (32 + 2 * b) * S:(32 + 2 * b) * S + YW] for b in range(2)]
            acc = tiles(36, 2)
            cg_in, z_in = sem("cv_cg_in"), sem("cv_z_in")
            cg_used, z_used = sem("cv_cg_used"), sem("cv_z_used")
            w0, o0 = w_at[0], o_at[0]
            hn_cut, WS0 = cut(hn, 40, 48), 56
            s0 = split_took(32)
            with nc.Block() as block:
                @block.sync
                def _(sp):
                    refill(sp, w0, 32)

                @block.gpsimd
                def _(pool):
                    split_weights(pool, w0, 32, WS0)

                @block.tensor
                def _(pe):
                    cut_wait(pe, hn_cut)
                    project3(pe, w0, o0, 32, WS0, s0, lambda j, k: hn_cut["hi"][k],
                             lambda j, k: hn_cut["lo"][k])

                @block.scalar
                def _(act):
                    cut_hi(act, hn_cut)

                    def one(it, j):
                        act.wait_ge(w_used, it * 8 + (w0 + 4 * j + 1))
                        act.wait_ge(cg_used, it * 2 + j + 1)
                        b = o0 % NBANK
                        nc.scalar.activation(cg[:, j], psum[:, b], ACT.Copy)
                        act.drain().then_inc(bank_free[b], 1)
                        act.sem_inc(cg_in, 1)
                        act.wait_ge(w_used, it * 8 + (w0 + 4 * j + 4))
                        act.wait_ge(z_used, it * 2 + j + 1)
                        b = (o0 + 3) % NBANK
                        nc.scalar.activation(zs[:, j], psum[:, b], ACT.Silu)
                        act.drain().then_inc(bank_free[b], 1)
                        act.sem_inc(z_in, 1)
                    turns(act, KT, one, 2)

                @block.vector
                def _(dve):
                    dve.sem_inc(cg_used, 2)
                    dve.sem_inc(z_used, 2)
                    for b in range(2):
                        nc.vector.memset(ypad[b][:, :TAPS - 1], 0.0)
                    dve.drain()
                    cut_lo(dve, hn_cut)

                    def one(it, j):
                        def par_m(name, tap):
                            return par[:, bass.ds(it * 2 + (PCOL[name] + 8 * tap + j), 1)]
                        dve.wait_ge(w_used, it * 8 + (w0 + 4 * j + 2))
                        dve.wait_ge(cg_in, it * 2 + j + 1)
                        b = (o0 + 1) % NBANK
                        nc.vector.tensor_tensor(ypad[j][:, TAPS - 1:], cg[:, j], psum[:, b],
                                                ALU.mult)
                        dve.drain().then_inc(bank_free[b], 1)
                        dve.sem_inc(cg_used, 1)
                        nc.vector.tensor_scalar(acc[:, j], ypad[j][:, 0:S], par_m("conv_w", 0),
                                                par_m("conv_b", 0), ALU.mult, ALU.add)
                        for tap in range(1, TAPS):
                            dve.drain()
                            nc.vector.scalar_tensor_tensor(acc[:, j], ypad[j][:, tap:tap + S],
                                                           par_m("conv_w", tap), acc[:, j],
                                                           ALU.mult, ALU.add)
                        dve.drain()
                        dve.wait_ge(w_used, it * 8 + (w0 + 4 * j + 3))
                        b = (o0 + 2) % NBANK
                        nc.vector.tensor_tensor(acc[:, j], acc[:, j], psum[:, b], ALU.mult)
                        dve.drain().then_inc(bank_free[b], 1)
                        dve.wait_ge(z_in, it * 2 + j + 1)
                        nc.vector.tensor_tensor(y[:, it * 2 + j], acc[:, j], zs[:, j],
                                                ALU.mult).then_inc(z_used, 1)
                        dve.drain()
                    turns(dve, KT, one, 2)
            took(32, 32)
            y_cut = cut(y, 32, 16)
            merge(hn_cut, y_cut, mg, 72, True, WS0, (y_cut,))

            pt, v_all = tiles(32, 16), tiles(48, 4)
            wgl = tiles(52, 1)[:, 0, 0:KT * 48].rearrange("p (k n) -> p k n", n=48)
            gates = tiles(53, 1)[:, 0, 0:192]
            w1 = [arena[:, (54 + 8 * t) * S:(62 + 8 * t) * S].rearrange("p (l m) -> p l m", m=P)
                  for t in range(2)]
            w2 = arena[:, 76 * S:76 * S + P]
            hid = [arena[:, 76 * S + P + 124 * t:76 * S + P + 124 * (t + 1)] for t in range(2)]
            kcmp = arena[:, 77 * S:77 * S + 124]
            vcmp = arena[0:N_CMP, 77 * S + 128:77 * S + 384]
            pos = arena[:, 70 * S:70 * S + 64]
            hb = small[:, 64:66]
            rel, cdist = tiles(79, 1)[:, 0], tiles(80, 1)[:, 0, 0:124]
            w0, o0 = w_at[0], o_at[0]
            t0 = pool_at[0]
            pool_at[0] += 9 * 16
            gl_done, gl_read = sem("gl_done"), sem("gl_read")
            pb_done, pb_read = sem("pb_done"), sem("pb_read")
            hd_done, hd_read = sem("hd_done"), sem("hd_read")
            cm_done = sem("cm_done")
            with nc.Block() as block:
                @block.gpsimd
                def _(pool):
                    w1_src = [d[n].rearrange("(l d) m -> d l m", d=HD) for n in ("w_ck1", "w_cv1")]
                    pool.dma_start(tiles(52, 1)[:, 0, 0:KT * 48], d["w_gl"]).then_inc(pool_in, 16)
                    for t in range(2):
                        for half in range(2):
                            pool.dma_start(w1[t][half * HD:(half + 1) * HD],
                                           w1_src[t]).then_inc(pool_in, 16)
                    pool.dma_start(w2, d["w_c2"]).then_inc(pool_in, 16)
                    pool.dma_start(pos, d["pos"]).then_inc(pool_in, 16)
                    pool.dma_start(rel, d["rel"]).then_inc(pool_in, 16)
                    pool.dma_start(cdist, d["cmp_dist"]).then_inc(pool_in, 16)
                    pool.wait_ge(pool_in, t0 + 144)

                @block.sync
                def _(sp):
                    refill(sp, w0, 28)

                @block.tensor
                def _(pe):
                    project(pe, w0, o0, 24, lambda j, k: hn[:, k])
                    project_wide(pe, w0 + 24, o0 + 24, 1,
                                 lambda g, k, j: hn[:, k, j * P:(j + 1) * P])
                    pe.wait_ge(pool_in, t0 + 144)
                    for j in range(4):
                        for k in range(KT):
                            last = nc.tensor.matmul(psum[:, 4, 48 * j:48 * (j + 1)],
                                                    hn[:, k, j * P:(j + 1) * P], wgl[:, k],
                                                    start=(k == 0), stop=(k == KT - 1))
                    last.then_inc(gl_done, 1)
                    for t in range(2):
                        for l in range(32):
                            last = nc.tensor.matmul(psum[:, 7, t:t + 1], w1[t][0:HD, l],
                                                    pos[0:HD, 32 * t + l:32 * t + l + 1],
                                                    start=(l == 0), stop=(l == 31))
                    last.then_inc(pb_done, 1)
                    pe.wait_ge(cm_done, 1)
                    for t in range(2):
                        for half in range(2):
                            rows = slice(half * HD, (half + 1) * HD)
                            for l in range(32):
                                last = nc.tensor.matmul(
                                    psum[:, 5 + half, 64 * t:64 * t + 62],
                                    w1[t][rows, l],
                                    pt[rows, 8 + 2 * t:10 + 2 * t, l:l + 16 * N_CMP - 15:16],
                                    start=(l == 0), stop=(l == 31))
                    last.then_inc(hd_done, 1)
                    pe.wait_ge(hd_read, 1)
                    nc.tensor.matmul(psum[0:HD, 7, 0:124], w2[:, 0:HD], hid[0], start=True, stop=True)
                    nc.tensor.matmul(psum[HD:P, 7, 0:124], w2[:, 0:HD], hid[0], start=True, stop=True)
                    for g in range(4):
                        at = g * N_CMP
                        last = nc.tensor.matmul(psum[0:N_CMP, 4, HD * g:HD * (g + 1)],
                                                hid[1][:, at:at + N_CMP], w2[:, HD:P],
                                                start=True, stop=True)
                    last.then_inc(cm_done, 1)

                @block.scalar
                def _(act):
                    def q_out(it, j):
                        act.wait_ge(w_used, it * NBANK + (w0 + j + 1))
                        nc.scalar.activation(pt[:, it * NBANK + j], psum[:, (o0 + j) % NBANK],
                                             ACT.Copy, scale=HD ** -0.5
                                             ).then_inc(bank_free[(o0 + j) % NBANK], 1)
                    turns(act, 8, q_out, NBANK)

                    def kv_out(it, j):
                        act.wait_ge(w_used, it * NBANK + (w0 + 8 + j + 1))
                        nc.scalar.activation(pt[:, it * NBANK + (8 + j)], psum[:, (o0 + j) % NBANK],
                                             ACT.Copy).then_inc(bank_free[(o0 + j) % NBANK], 1)
                    turns(act, 8, kv_out, NBANK)
                    act.drain().then_inc(cm_done, 1)

                    def z_out(it, j):
                        act.wait_ge(w_used, it * NBANK + (w0 + 16 + j + 1))
                        nc.scalar.activation(y[:, it * NBANK + j], psum[:, (o0 + j) % NBANK],
                                             ACT.Silu).then_inc(bank_free[(o0 + j) % NBANK], 1)
                    turns(act, 8, z_out, NBANK)
                    act.wait_ge(w_used, w0 + 28)
                    for j in range(4):
                        nc.scalar.activation(v_all[:, j], psum[:, (o0 + j) % NBANK],
                                             ACT.Copy).then_inc(bank_free[(o0 + j) % NBANK], 1)
                    act.wait_ge(gl_done, 1)
                    nc.scalar.activation(gates, psum[:, 4, 0:192], ACT.Sigmoid)
                    act.wait_ge(pb_done, 1)
                    nc.scalar.activation(hb, psum[:, 7, 0:2], ACT.Copy)
                    act.drain()
                    act.wait_ge(hd_done, 1)
                    for t in range(2):
                        for half in range(2):
                            nc.scalar.activation(
                                hid[t].rearrange("p (g n) -> p g n", g=4)[:, half::2],
                                psum[:, 5 + half, 64 * t:64 * t + 62].rearrange(
                                    "p (g n) -> p g n", g=2), ACT.Silu, bias=hb[:, t:t + 1])
                    act.drain().then_inc(hd_read, 1)
                    act.wait_ge(cm_done, 2)
                    nc.scalar.activation(kcmp, psum[:, 7, 0:124], ACT.Copy)
                    nc.scalar.activation(vcmp, psum[0:N_CMP, 4, 0:256], ACT.Copy)
            took(28, 28)

            k_dup = tiles(54, 8)
            dup_in = sem("dup_in")
            with nc.Block() as block:
                @block.sync
                def _(sp):
                    for g in range(4):
                        rows = slice(HD * (g % 2), HD * (g % 2) + HD)
                        for half in range(2):
                            for kind in range(2):
                                sp.dma_start(k_dup[half * HD:(half + 1) * HD, 4 * kind + g],
                                             pt[rows, 12 + 2 * kind + g // 2]).then_inc(dup_in, 16)
                    sp.wait_ge(dup_in, 256)

            q_st, ks_st, kw_st = tiles(71, 2), tiles(73, 1)[:, 0], tiles(74, 1)[:, 0]
            v_st = tiles(75, 1)[:, 0].rearrange("p (j c m) -> p j c m", j=4, m=HD)
            kc_st = tiles(78, 1)[:, 0, 0:N_CMP]
            vc_st = arena[0:N_CMP, 78 * S + 64:78 * S + 128]
            WB = P + 2 * S
            score = [arena[:, 62 * S + b * WB:62 * S + (b + 1) * WB] for b in range(3)]
            prob_t = [arena[:, 40 * S + b * WB:40 * S + (b + 1) * WB] for b in range(2)]
            nmax = [small[:, 64 + 4 * b:67 + 4 * b] for b in range(3)]
            rsum = [small[:, 76 + 4 * b:79 + 4 * b] for b in range(3)]
            coef = [small[:, 88 + 4 * b:91 + 4 * b] for b in range(3)]
            staged = sem("n_staged")
            qk_done, qk_read = sem("n_qk_done"), sem("n_qk_read")
            max_done, exp_done, p_done = sem("n_max_done"), sem("n_exp_done"), sem("n_p_done")
            tr_done, pt_done = sem("n_tr_done"), sem("n_pt_done")
            pv_done, out_read = sem("n_pv_done"), sem("n_out_read")
            UNITS = 16

            def unit(u):
                n, i = u // 4, u % 4
                return n, i, HD * (n % 2), P * (i + 1)

            with nc.Block() as block:
                @block.sync
                def _(sp):
                    with sp.Fori(0, 4) as it:
                        sp.wait_ge(pv_done, it * UNITS + 2)
                        sp.dma_start(q_st, arena[:, bass.ds(it * 2 * S + 32 * S, 2 * S)].rearrange(
                            "p (k n) -> p k n", n=S)).then_inc(staged, 16)
                        sp.dma_start(ks_st, k_dup[:, it]).then_inc(staged, 16)
                        sp.dma_start(kw_st, k_dup[:, it + 4]).then_inc(staged, 16)
                        for c in range(2):
                            sp.dma_start(v_st[:, :, c], v_all[:, :, bass.ds(it * HD + 256 * c, HD)]
                                         ).then_inc(staged, 16)
                        sp.dma_start(kc_st, kcmp[:, bass.ds(it * N_CMP, N_CMP)]).then_inc(staged, 16)
                        sp.dma_start(vc_st, vcmp[:, bass.ds(it * HD, HD)]).then_inc(staged, 16)

                @block.tensor
                def _(pe):
                    pe.sem_inc(tr_done, 3)
                    pe.sem_inc(pv_done, 2)

                    def qk(it, u):
                        n, i, off, w = unit(u)
                        if u == 0:
                            pe.wait_ge(staged, it * 112 + 112)
                        pe.wait_ge(qk_read, it * UNITS + u + 1)
                        b = u % 2
                        q = q_st[off:off + HD, n // 2, i * P:(i + 1) * P]
                        nc.tensor.matmul(psum[:, 2 * b, 0:w], q, ks_st[off:off + HD, 0:w],
                                         start=True, stop=True)
                        nc.tensor.matmul(psum[:, 2 * b + 1, 0:w], q, kw_st[off:off + HD, 0:w],
                                         start=True, stop=True)
                        pe.wait_ge(qk_read, it * UNITS + u + 2)
                        if u >= 2:
                            pe.wait_ge(pt_done, it * UNITS + u)
                        nc.tensor.matmul(psum[:, 4, 32 * b:32 * b + N_CMP], q,
                                         kc_st[off:off + HD], start=True,
                                         stop=True).then_inc(qk_done, 1)

                    with pe.Fori(0, 4) as it:
                        qk(it, 0)
                        qk(it, 1)
                        for u in range(UNITS):
                            n, i, off, w = unit(u)
                            pe.wait_ge(p_done, it * UNITS + u + 1)
                            pe.wait_ge(pt_done, it * UNITS + u + 1)
                            for c in range(2 * (i + 1)):
                                nc.tensor.transpose(
                                    psum[:, 5 + c // 4, (c % 4) * P:(c % 4 + 1) * P],
                                    score[u % 3][:, (c + 1) * P:(c + 2) * P], ident)
                            pe.wait_ge(qk_read, it * UNITS + min(u + 2, UNITS) + 2)
                            last = nc.tensor.transpose(psum[:, 4, P:2 * P], score[u % 3][:, 0:P], ident)
                            last.then_inc(tr_done, 1)
                            if u + 2 < UNITS:
                                qk(it, u + 2)
                            pe.wait_ge(pt_done, it * UNITS + u + 2)
                            if u % 8 == 0:
                                pe.wait_ge(out_read, it * 2 + u // 8 + 1)
                            out = psum[off:off + HD, 7, i * P:(i + 1) * P]
                            nc.tensor.matmul(out, vc_st, prob_t[u % 2][0:N_CMP, 0:P], start=True,
                                             stop=False)
                            for c in range(2 * (i + 1)):
                                last = nc.tensor.matmul(out, v_st[:, c % (i + 1), c // (i + 1)],
                                                        prob_t[u % 2][:, (c + 1) * P:(c + 2) * P],
                                                        start=False, stop=(c == 2 * i + 1))
                            last.then_inc(pv_done, 1)

                @block.vector
                def _(dve):
                    dve.sem_inc(qk_read, 2)
                    dve.sem_inc(out_read, 1)
                    for b in range(3):
                        nc.vector.memset(score[b][:, 0:P], 0.0)
                    dve.drain()

                    def front(it, u):
                        n, i, off, w = unit(u)
                        b, bank = u % 3, 2 * (u % 2)
                        dve.wait_ge(qk_done, it * UNITS + u + 1)
                        dve.wait_ge(tr_done, it * UNITS + u + 1)
                        slope = con[:, bass.ds(it * 4 + (CCOL["neg_slope_2"] + n), 1)]
                        reach = rel[:, S - w:S]
                        nc.vector.scalar_tensor_tensor(score[b][:, P:P + w], reach, slope,
                                                       psum[:, bank, 0:w], ALU.mult, ALU.add)
                        nc.vector.scalar_tensor_tensor(score[b][:, P + w:P + 2 * w], reach, slope,
                                                       psum[:, bank + 1, 0:w], ALU.mult, ALU.add)
                        nc.vector.scalar_tensor_tensor(
                            score[b][:, 0:N_CMP], cdist[:, N_CMP * i:N_CMP * (i + 1)], slope,
                            psum[:, 4, 16 * bank:16 * bank + N_CMP], ALU.mult, ALU.add)
                        dve.drain().then_inc(qk_read, 1)
                        nc.vector.tensor_reduce(nmax[b][:, 0:1], score[b][:, 0:N_CMP], axis=AX.X,
                                                op=ALU.max, negate=True)
                        nc.vector.tensor_reduce(
                            nmax[b][:, 1:3], score[b][:, P:P + 2 * w].rearrange(
                                "p (c w) -> p c w", c=2), axis=AX.X, op=ALU.max, negate=True)
                        dve.drain().then_inc(max_done, 1)

                    def back(it, u):
                        n, i, off, w = unit(u)
                        b = u % 3
                        dve.wait_ge(exp_done, it * UNITS + u + 1)
                        nc.vector.reciprocal(coef[b], rsum[b])
                        dve.drain()
                        nc.vector.tensor_tensor(
                            coef[b], coef[b], gates[:, bass.ds(it * 12 + (48 * i + 3 * n), 3)],
                            ALU.mult)
                        if i == 0:
                            dve.drain()
                            nc.vector.tensor_tensor(coef[b][:, 0:1], coef[b][:, 0:1],
                                                    ccol("cmp_valid"), ALU.mult)
                        dve.drain()
                        nc.vector.tensor_scalar(score[b][:, 0:N_CMP], score[b][:, 0:N_CMP],
                                                coef[b][:, 0:1], None, ALU.mult)
                        for c in range(2):
                            part = score[b][:, P + c * w:P + (c + 1) * w]
                            nc.vector.tensor_scalar(part, part, coef[b][:, 1 + c:2 + c], None,
                                                    ALU.mult)
                        dve.drain().then_inc(p_done, 1)

                    def gate(it, a):
                        dve.wait_ge(pv_done, it * UNITS + 8 * (a + 1) + 2)
                        t = y[:, it * 2 + a]
                        nc.vector.tensor_tensor(t, psum[:, 7], t, ALU.mult).then_inc(out_read, 1)

                    with dve.Fori(0, 4) as it:
                        front(it, 0)
                        front(it, 1)
                        for u in range(UNITS):
                            back(it, u)
                            if u + 2 < UNITS:
                                front(it, u + 2)
                            if u == 7:
                                gate(it, 0)
                        gate(it, 1)
                        dve.drain()

                @block.scalar
                def _(act):
                    act.sem_inc(pt_done, 1)

                    def exp(it, u):
                        n, i, off, w = unit(u)
                        b = u % 3
                        act.wait_ge(max_done, it * UNITS + u + 1)
                        for c, (lo, hi) in enumerate(((0, N_CMP), (P, P + w), (P + w, P + 2 * w))):
                            nc.scalar.activation(score[b][:, lo:hi], score[b][:, lo:hi], ACT.Exp,
                                                 bias=nmax[b][:, c:c + 1],
                                                 accum_out=rsum[b][:, c:c + 1])
                        act.drain().then_inc(exp_done, 1)

                    with act.Fori(0, 4) as it:
                        exp(it, 0)
                        exp(it, 1)
                        for u in range(UNITS):
                            n, i, off, w = unit(u)
                            act.wait_ge(tr_done, it * UNITS + u + 4)
                            act.wait_ge(pv_done, it * UNITS + u + 1)
                            nc.scalar.activation(prob_t[u % 2][:, 0:P], psum[:, 4, P:2 * P], ACT.Copy)
                            nc.scalar.activation(prob_t[u % 2][:, P:P + 2 * w],
                                                 psum[:, 5:7].rearrange("p a n -> p (a n)")[:, 0:2 * w],
                                                 ACT.Copy)
                            act.drain().then_inc(pt_done, 1)
                            if u + 2 < UNITS:
                                exp(it, u + 2)
            hn_cut, y_cut = cut(hn, 54, 62), cut(y, 32, 16)
            merge(hn_cut, y_cut, mg, 72, False, 40, (hn_cut, y_cut))

            vt = arena[:, 32 * S:40 * S].rearrange("p (j n) -> p j n", j=4)
            ln_bc = tiles(44, 4).rearrange("p a n -> p (a n)")
            ws = arena[:, 48 * S:50 * S].rearrange("p (g i) -> p g i", i=P)
            bs, ones = arena[0:1, 50 * S:52 * S], arena[0:1, 52 * S:52 * S + P]
            stats = arena[:, 53 * S:53 * S + 64]
            zs, WS0 = tiles(74, 2), 76
            w0, o0 = w_at[0], o_at[0]
            s0 = split_took(24)
            t0 = pool_at[0]
            pool_at[0] += 48
            v_in, v_ready, ws_ready = sem("g_v_in"), sem("g_v_ready"), sem("g_ws_ready")
            var_in, root_in = sem("g_var_in"), sem("g_root_in")
            z_in, z_used, u_in = sem("g_z_in"), sem("g_z_used"), sem("g_u_in")
            sp_done, sp_read = sem("g_sp_done"), sem("g_sp_read")
            with nc.Block() as block:
                @block.gpsimd
                def _(pool):
                    pool.dma_start(ln_bc, d["ln_bc"]).then_inc(pool_in, 16)
                    pool.dma_start(arena[:, 48 * S:50 * S], d["w_s"]).then_inc(pool_in, 16)
                    pool.dma_start(bs, d["b_s"]).then_inc(pool_in, 16)
                    nc.gpsimd.memset(ones, 1.0)
                    pool.wait_ge(pool_in, t0 + 48)
                    nc.gpsimd.affine_select(out=ws, in_=ws, pattern=[[0, 8], [1, P]],
                                            compare_op=ALU.is_ge, fill=0.0, base=0,
                                            channel_multiplier=-1)
                    pool.drain().then_inc(ws_ready, 1)
                    split_weights(pool, w0, 24, WS0)

                @block.sync
                def _(sp):
                    refill(sp, w0, 24)

                @block.tensor
                def _(pe):
                    project_wide3(pe, w0, o0, 2, WS0, s0,
                                  lambda g, k, j: hn_cut["hi"][k][:, j * P:(j + 1) * P],
                                  lambda g, k, j: hn_cut["lo"][k][:, j * P:(j + 1) * P])
                    project3(pe, w0 + 8, o0 + 8, 8, WS0, s0 + 8, lambda j, k: hn_cut["hi"][k],
                             lambda j, k: hn_cut["lo"][k])
                    pe.wait_ge(ws_ready, 1)
                    pe.wait_ge(v_ready, 1)
                    for g in range(8):
                        pe.wait_ge(sp_read, g + 1)
                        b = 4 + g % 2
                        nc.tensor.matmul(psum[:, b].rearrange("p (n i) -> p n i", i=P), ones,
                                         bs[:, g * P:(g + 1) * P].unsqueeze(1).to_broadcast(
                                             [1, 4, P]), start=True, stop=False,
                                         skip_group_check=True)
                        for n in range(4):
                            last = nc.tensor.matmul(psum[:, b, n * P:(n + 1) * P],
                                                    vt[:, n, g * P:(g + 1) * P], ws[:, g],
                                                    start=False, stop=(n == 3),
                                                    skip_group_check=True)
                        last.then_inc(sp_done, 1)
                        project3(pe, w0 + 16 + g, o0 + 16 + g, 1, WS0, s0 + 16 + g,
                                 lambda j, k: hn_cut["hi"][k], lambda j, k: hn_cut["lo"][k],
                                 b0=g % 2)

                @block.scalar
                def _(act):
                    for g in range(2):
                        act.wait_ge(w_used, w0 + 4 * g + 4)
                        for j in range(4):
                            nc.scalar.activation(vt[:, j, g * S:(g + 1) * S],
                                                 psum[:, (o0 + j) % NBANK], ACT.Gelu_apprx_tanh
                                                 ).then_inc(bank_free[(o0 + j) % NBANK], 1)
                    act.drain().then_inc(v_in, 1)

                    def u_out(it, j):
                        act.wait_ge(w_used, it * NBANK + (w0 + 8 + j + 1))
                        nc.scalar.activation(y[:, it * NBANK + j], psum[:, (o0 + j) % NBANK],
                                             ACT.Gelu_apprx_tanh
                                             ).then_inc(bank_free[(o0 + j) % NBANK], 1)
                    act.wait_ge(var_in, 1)
                    for j in range(4):
                        nc.scalar.activation(stats[:, 56 + j:57 + j], stats[:, 49 + 2 * j:50 + 2 * j],
                                             ACT.Sqrt, bias=ccol("eps"))
                    act.drain().then_inc(root_in, 1)
                    turns(act, 8, u_out, NBANK)
                    act.drain().then_inc(u_in, 1)
                    for g in range(8):
                        act.wait_ge(w_used, w0 + 16 + g + 1)
                        act.wait_ge(z_used, g + 1)
                        b = (o0 + g) % NBANK
                        nc.scalar.activation(zs[:, g % 2], psum[:, b], ACT.Silu)
                        act.drain().then_inc(bank_free[b], 1)
                        act.sem_inc(z_in, 1)

                @block.vector
                def _(dve):
                    dve.sem_inc(z_used, 2)
                    dve.sem_inc(sp_read, 2)
                    dve.wait_ge(v_in, 1)
                    for j in range(4):
                        for g in range(2):
                            nc.vector.bn_stats(stats[:, 12 * j + 6 * g:12 * j + 6 * g + 6],
                                               vt[:, j, g * S:(g + 1) * S])
                    dve.drain()
                    for j in range(4):
                        nc.vector.bn_aggr(stats[:, 48 + 2 * j:50 + 2 * j], stats[:, 12 * j:12 * j + 12])
                    dve.drain().then_inc(var_in, 1)
                    dve.wait_ge(root_in, 1)
                    nc.vector.reciprocal(stats[:, 60:64], stats[:, 56:60])
                    dve.drain()
                    dve.wait_ge(pool_in, t0 + 48)
                    for j in range(4):
                        nc.vector.tensor_scalar(vt[:, j], vt[:, j], stats[:, 48 + 2 * j:49 + 2 * j],
                                                stats[:, 60 + j:61 + j], ALU.subtract, ALU.mult)
                    dve.drain()
                    for j in range(4):
                        nc.vector.tensor_tensor(vt[:, j], vt[:, j], ln_bc[:, 0:D], ALU.mult)
                    dve.drain()
                    for j in range(4):
                        nc.vector.tensor_tensor(vt[:, j], vt[:, j], ln_bc[:, D:2 * D], ALU.add)
                    dve.drain().then_inc(v_ready, 1)
                    dve.wait_ge(u_in, 1)
                    for g in range(8):
                        dve.wait_ge(sp_done, g + 1)
                        nc.vector.tensor_tensor(y[:, g], y[:, g], psum[:, 4 + g % 2], ALU.mult)
                        dve.drain().then_inc(sp_read, 1)
                        dve.wait_ge(z_in, g + 1)
                        nc.vector.tensor_tensor(y[:, g], y[:, g], zs[:, g % 2],
                                                ALU.mult).then_inc(z_used, 1)
            took(24, 24)
            y_cut = cut(y, 32, 16)
            merge(hn_cut, y_cut, mg, 72, False, WS0, (y_cut,))

            z = tiles(32, KT)
            w0, o0 = w_at[0], o_at[0]
            mg_cut = cut(mg, 40, 24)
            s0 = split_took(8)
            with nc.Block() as block:
                @block.sync
                def _(sp):
                    refill(sp, w0, 8)

                @block.tensor
                def _(pe):
                    cut_wait(pe, mg_cut)
                    project3(pe, w0, o0, 8, WS0, s0, lambda j, k: mg_cut["hi"][k],
                             lambda j, k: mg_cut["lo"][k])

                @block.gpsimd
                def _(pool):
                    split_weights(pool, w0, 8, WS0)

                @block.vector
                def _(dve):
                    cut_lo(dve, mg_cut)

                @block.scalar
                def _(act):
                    cut_hi(act, mg_cut)
                    for o in range(8):
                        act.wait_ge(w_used, w0 + o + 1)
                        nc.scalar.activation(z[:, o], psum[:, (o0 + o) % NBANK], ACT.Copy
                                             ).then_inc(bank_free[(o0 + o) % NBANK], 1)
            took(8, 8)

            def add(k):
                nc.vector.scalar_tensor_tensor(x[:, k], z[:, k], g_col[:, k:k + 1], x[:, k],
                                               ALU.mult, ALU.add)
            norm(z, z, 72, None, add=add)

        def recurrent_block():
            x, hn, mg = tiles(0, KT), tiles(8, KT), tiles(24, KT)
            mod = small[:, 88:184].rearrange("p (m i) -> p m i", i=2)
            a1, a1c, a2 = small[:, 184:192], small[:, 192:200], small[:, 200:208]
            c_silu = small[:, 208:224]
            XC, HC = 40, 16
            ctx_x = arena[:, XC * S:(XC + 4) * S].rearrange("p (k n) -> p k n", n=CTX)
            ctx_h = arena[:, HC * S:(HC + 4) * S].rearrange("p (k n) -> p k n", n=CTX)
            ctx_in = sem("ctx_in")

            with nc.Block() as block:
                @block.scalar
                def _(act):
                    nc.scalar.activation(c_silu, par[:, PCOL["c_3"]:PCOL["c_3"] + 16], ACT.Silu)

                @block.gpsimd
                def _(pool):
                    pool.dma_start(ctx_x, d["ctx_t"].rearrange("(k p) n -> p k n", p=P)
                                   ).then_inc(ctx_in, 16)
                    pool.wait_ge(ctx_in, 16)
            modulation(c_silu.rearrange("p (k i) -> p k i", i=2), 2, 48, mod,
                       par[:, PCOL["b_mod"]:PCOL["b_mod"] + 48])
            with nc.Block() as block:
                @block.vector
                def _(dve):
                    for dst, at, i, name in ((a1, 8, 0, "norm1_w"), (a1c, 8, 1, "norm1_w"),
                                             (a2, 32, 0, "norm2_w")):
                        nc.vector.scalar_tensor_tensor(dst, mod[:, at:at + 8, i], 1.0,
                                                       par[:, PCOL[name]:PCOL[name] + 8],
                                                       ALU.add, ALU.mult)
            norm(x, hn, 76, affine(hn, lambda k: a1[:, k:k + 1], lambda k: mod[:, k, 0:1]))
            norm(ctx_x, ctx_h, 76, affine(ctx_h, lambda k: a1c[:, k:k + 1],
                                                   lambda k: mod[:, k, 1:2]), n=CTX)

            vx = tiles(24, KT).rearrange("p (j a) n -> p j (a n)", j=4)
            vc = tiles(32, 4).rearrange("p (j a) n -> p j (a n)", j=2)
            iv_read = sem("iv_read")
            w0, o0 = w_at[0], o_at[0]
            with nc.Block() as block:
                @block.sync
                def _(sp):
                    refill(sp, w0, 8)

                @block.tensor
                def _(pe):
                    for g in range(2):
                        for q in range(4):
                            tile_ready(pe, w0, 0, 4 * g + q)
                            for kk in range(2):
                                k = 2 * q + kk
                                for j in range(6):
                                    if q == 0 and kk == 0:
                                        if j < 4:
                                            bank_ready(pe, o0, 0, 4 * g + j)
                                        elif g == 1:
                                            pe.wait_ge(iv_read, 1)
                                    act_k = (hn[:, k, j * P:(j + 1) * P] if j < 4 else
                                             ctx_h[:, k, (j - 4) * P:(j - 3) * P])
                                    last = nc.tensor.matmul(
                                        psum[:, j], act_k, wide((w0 + 4 * g + q) % RING)[:, kk],
                                        start=(k == 0), stop=(k == KT - 1))
                            last.then_inc(w_used, 1)

                @block.scalar
                def _(act):
                    for g in range(2):
                        act.wait_ge(w_used, w0 + 4 * g + 4)
                        for j in range(4):
                            nc.scalar.activation(vx[:, j, g * S:(g + 1) * S], psum[:, j],
                                                 ACT.Copy).then_inc(bank_free[j], 1)
                        for j in range(2):
                            nc.scalar.activation(vc[:, j, g * S:(g + 1) * S], psum[:, 4 + j], ACT.Copy)
                        act.drain().then_inc(iv_read, 1)
            took(8, 8)

            yg = tiles(36, KT)
            mask = arena[:, 44 * S:44 * S + 15 * P].rearrange("p (l n) -> p l n", n=P)
            ones = arena[:, 44 * S + 15 * P:48 * S]
            B = 48
            q_s = tiles(B, 2)
            g_s = tiles(B + 2, 2)
            k_s = [tiles(B + 4 + 2 * b, 2) for b in range(2)]
            kc_s = [tiles(B + 8 + b, 1).rearrange("p a (t n) -> p (a t) n", t=2) for b in range(2)]
            lf = tiles(B + 10, 2)
            lc = tiles(B + 12, 1).rearrange("p a (t n) -> p (a t) n", t=2)
            run_f = [tiles(t, 1)[:, 0].rearrange("p (c n) -> p c n", n=CH)
                     for t in (B + 13, 21)]
            RB = CH + 1
            run_b = [arena[:, t * S:t * S + 4 * RB].rearrange("p (c n) -> p c n", n=RB)
                     for t in (B + 14, B + 34)]
            run_c = arena[:, (B + 15) * S + 8:(B + 15) * S + 8 + 2 * (CTX + 1)].rearrange(
                "p (t n) -> p t n", t=2)
            qd = tiles(B + 17, 2)
            kd = tiles(B + 19, 2)
            kcd = tiles(B + 21, 1).rearrange("p a (t n) -> p (a t) n", t=2)
            k_t = tiles(B + 22, 3).rearrange("p a (c n) -> p (a c) n", n=P)
            st = tiles(B + 25, 2).rearrange("p a (c n) -> p (a c) n", n=P)
            lev = [tiles(t, 1)[:, 0] for t in (B + 27, B + 28, 20)]
            sc = [tiles(t, 1)[:, 0] for t in (B + 29, 22)]
            v_st = tiles(B + 30, 1)[:, 0].rearrange("p (j n) -> p j n", n=P)
            vc_st = tiles(B + 31, 1)[:, 0, 0:2 * P].rearrange("p (j n) -> p j n", n=P)
            o_s, o_r = tiles(B + 32, 1)[:, 0], tiles(B + 33, 1)[:, 0]
            e_end = tiles(B + 31, 1)[:, 0, 2 * P:2 * P + 16]
            tab0 = tab_at[0]
            tab_at[0] += 16
            front_in = sem("r_front_in")
            clipped = sem("r_clipped")
            logged = sem("r_logged")
            summed = sem("r_summed")
            ctx_free = sem("r_ctx_free")
            decayed = sem("r_decayed")
            kd_done = sem("r_kd_done")
            tr_done, tr_read = sem("r_tr_done"), sem("r_tr_read")
            kv_done, st_done = sem("r_kv_done"), sem("r_st_done")
            diff_done, exp_done = sem("r_diff_done"), sem("r_exp_done")
            lev_done, sc_done = sem("r_lev_done"), sem("r_sc_done")
            sc_read = sem("r_sc_read")
            picks = sem("r_picks")
            v_in = sem("r_v_in")
            out_done = sem("r_out_done")
            sq_done, var_done = sem("r_sq_done"), sem("r_var_done")
            rt_done, head_done = sem("r_rt_done"), sem("r_head_done")
            NL = 2 * LEVELS + 1
            w0, o0 = w_at[0], o_at[0]
            TRG = 3

            def halves(ap, level):
                v = ap.rearrange("p (b h n) -> p b h n", h=2, n=1 << level)
                return v[:, :, 0], v[:, :, 1]

            def by_pairs(eng, step):
                def pair(it, first, last):
                    for hd in range(2):
                        before = (it, 0) if hd else None if first else (it - 1, 1)
                        after = (it, 1) if hd == 0 else None if last else (it + 1, 0)
                        for i in range(NL):
                            step(it, hd, i, before, after)

                pair(0, True, False)
                with eng.Fori(1, KT // 2 - 1) as it:
                    pair(it, False, False)
                pair(KT // 2 - 1, False, True)

            with nc.Block() as block:
                @block.sync
                def _(sp):
                    sp.dma_start(arena[:, 44 * S:44 * S + 15 * P], d["gla_mask"]).then_inc(tab_in, 16)
                    refill(sp, w0, 32)

                @block.gpsimd
                def _(pool):
                    with pool.Fori(0, KT) as hd:
                        pool.wait_ge(head_done, hd + 1)
                        nc.gpsimd.tensor_copy(v_st, vx[:, :, bass.ds(hd * P, P)])
                        nc.gpsimd.tensor_copy(vc_st, vc[:, :, bass.ds(hd * P, P)])
                        pool.drain().then_inc(v_in, 1)

                @block.tensor
                def _(pe):
                    def proj(it, hd, s):
                        t, k0 = s // 4, 2 * (s % 4)
                        if k0 == 0:
                            tile_ready(pe, w0, it, 4 * hd + t)
                            bank_ready(pe, o0, it, 4 * hd + t)
                            if t == 1:
                                pe.wait_ge(ctx_free, it * 2 + hd + 1)
                        for k in (k0, k0 + 1):
                            wt = slot((w0 + 4 * hd + t) % RING)[:, k]
                            last = nc.tensor.matmul(psum[:, t], wt, hn[:, k], start=(k == 0),
                                                    stop=(k == KT - 1))
                            if t in (1, 2):
                                last = nc.tensor.matmul(psum[:, 4, CTX * (t - 1):CTX * t], wt,
                                                        ctx_h[:, k], start=(k == 0),
                                                        stop=(k == KT - 1))
                        if k0 == 6:
                            last.then_inc(w_used, 1)

                    def scores(it, hd, i):
                        g = NL * hd + i
                        pe.wait_ge(lev_done, it * (2 * NL) + (g + 1))
                        pe.wait_ge(sc_read, it * (2 * NL) + (g + 1))
                        for c in range(4):
                            cols_ = slice(c * P, (c + 1) * P)
                            last = nc.tensor.matmul(
                                psum[:, 5 + g % 2, cols_], lev[i % 3][:, cols_],
                                q_s[:, hd, cols_] if i == NL - 1 else lev[i % 3][:, cols_],
                                start=True, stop=True)
                        last.then_inc(sc_done, 1)

                    def to_tokens(n, i):
                        groups = ([(kcd[:, t, c * P:(c + 1) * P]) for t in range(2) for c in range(2)],
                                  [kd[:, 0, c * P:(c + 1) * P] for c in range(3)],
                                  [kd[:, 1, c * P:(c + 1) * P] for c in range(1, 4)])
                        if i > 0:
                            pe.wait_ge(tr_read, n * TRG + i)
                        for c, src in enumerate(groups[i]):
                            last = nc.tensor.transpose(psum[:, 7, c * P:(c + 1) * P], src, ident)
                        last.then_inc(tr_done, 1)

                    def chunk_sums(t):
                        for c in range(2):
                            nc.tensor.matmul(psum[:, 7, 0:P], k_t[:, 2 * t + c], vc_st[:, c],
                                             start=(c == 0), stop=(c == 1))
                        for c in range(3):
                            last = nc.tensor.matmul(psum[:, 7, (c + 1) * P:(c + 2) * P],
                                                    k_t[:, 4 + 3 * t + c], v_st[:, c + t],
                                                    start=True, stop=True)
                        last.then_inc(kv_done, 1)

                    def outputs(it, hd):
                        n = it * 2 + hd
                        pe.wait_ge(sc_read, n * NL + (NL + 2))
                        pe.wait_ge(st_done, n * 2 + 2)
                        pe.wait_ge(kd_done, n * 2 + 2)
                        for c in range(4):
                            cols_ = slice(c * P, (c + 1) * P)
                            nc.tensor.matmul(psum[:, 7, cols_], st[:, c], qd[:, 0, cols_],
                                             start=True, stop=False)
                            nc.tensor.matmul(psum[:, 7, cols_], st[:, 4 + c], qd[:, 1, cols_],
                                             start=False, stop=False)
                            last = nc.tensor.matmul(psum[:, 7, cols_], v_st[:, c],
                                                    sc[hd][:, cols_], start=False, stop=True)
                        last.then_inc(out_done, 1)

                    def mean_square(it, hd):
                        pe.wait_ge(sq_done, it * 2 + hd + 1)
                        nc.tensor.matmul(psum[:, 7], mean_h, o_r, start=True,
                                         stop=True).then_inc(var_done, 1)

                    def step(it, hd, i, before, after):
                        n = it * 2 + hd
                        scores(it, hd, i)
                        if i == 0 and before is not None:
                            outputs(*before)
                        if i == 2 and before is not None:
                            mean_square(*before)
                        if i == 5:
                            pe.wait_ge(kd_done, n * 2 + 1)
                            if before is not None:
                                pe.wait_ge(rt_done, n)
                        if i in (5, 6, 7):
                            to_tokens(n, i - 5)
                        if i == 8:
                            pe.wait_ge(tr_read, n * TRG + 3)
                            pe.wait_ge(v_in, n + 1)
                            chunk_sums(0)
                        if i == 10:
                            pe.wait_ge(st_done, n * 2 + 1)
                            chunk_sums(1)
                        if after is not None:
                            for part in range(2 * i, 2 * i + 2) if i < 4 else range(i + 4, i + 5):
                                if part < 16:
                                    proj(it, hd + 1, part)

                    for s in range(16):
                        proj(0, 0, s)
                    by_pairs(pe, step)
                    outputs(KT // 2 - 1, 1)
                    mean_square(KT // 2 - 1, 1)

                def inputs(act, it, hd):
                    base = it * 8 + (w0 + 4 * hd)
                    act.wait_ge(w_used, base + 1)
                    nc.scalar.activation(q_s[:, hd], psum[:, 0], ACT.Copy)
                    act.drain().then_inc(bank_free[0], 1)
                    for t in range(2):
                        act.wait_ge(w_used, base + 2 + t)
                        nc.scalar.activation(lf[:, t], psum[:, 1 + t], ACT.Sigmoid)
                        nc.scalar.activation(k_s[t][:, hd], psum[:, 1 + t], ACT.Sigmoid, scale=-1.0)
                        act.drain().then_inc(bank_free[1 + t], 1)
                    nc.scalar.activation(lc, psum[:, 4].rearrange("p (t n) -> p t n", t=2), ACT.Sigmoid)
                    nc.scalar.activation(kc_s[hd], psum[:, 4].rearrange("p (t n) -> p t n", t=2),
                                         ACT.Sigmoid, scale=-1.0)
                    act.drain().then_inc(ctx_free, 1)
                    act.sem_inc(front_in, 1)

                @block.scalar
                def _(act):
                    def gate_silu(it, hd):
                        act.wait_ge(w_used, it * 8 + (w0 + 4 * hd + 4))
                        nc.scalar.activation(g_s[:, hd], psum[:, 3], ACT.Silu).then_inc(bank_free[3], 1)

                    def logs(it, hd):
                        act.wait_ge(clipped, it * 2 + hd + 1)
                        nc.scalar.activation(lf, lf, ACT.Ln)
                        nc.scalar.activation(lc, lc, ACT.Ln)
                        act.drain().then_inc(logged, 1)

                    def key_decays(it, hd):
                        act.wait_ge(summed, it * 2 + hd + 1)
                        rf, rb = run_f[hd], run_b[hd]
                        nc.scalar.activation(kcd[:, 1], run_c[:, 1, 0:CTX], ACT.Exp)
                        nc.scalar.activation(kcd[:, 0], run_c[:, 0, 1:CTX + 1], ACT.Exp, scale=-1.0,
                                             bias=run_c[:, 0, CTX:CTX + 1])
                        nc.scalar.activation(kd[:, 1].rearrange("p (c n) -> p c n", n=CH),
                                             rb[:, :, 0:CH], ACT.Exp)
                        for c in range(4):
                            nc.scalar.activation(kd[:, 0, c * CH:(c + 1) * CH], rf[:, c], ACT.Exp,
                                                 scale=-1.0, bias=rf[:, c, CH - 1:CH])
                        nc.scalar.activation(e_end[:, 0:4], rf[:, :, CH - 1], ACT.Exp)
                        nc.scalar.activation(e_end[:, 4:8], rb[:, :, CH], ACT.Exp)
                        act.drain().then_inc(decayed, 1)

                    def query_decays(hd):
                        rf, rb = run_f[hd], run_b[hd]
                        nc.scalar.activation(qd[:, 0].rearrange("p (c n) -> p c n", n=CH), rf, ACT.Exp)
                        for c in range(4):
                            nc.scalar.activation(qd[:, 1, c * CH:(c + 1) * CH], rb[:, c, 0:CH],
                                                 ACT.Exp, scale=-1.0, bias=rb[:, c, CH:CH + 1])
                        act.drain().then_inc(decayed, 1)

                    def level_exp(it, hd, i):
                        act.wait_ge(diff_done, it * (2 * NL - 2) + ((NL - 1) * hd + i + 1))
                        nc.scalar.activation(lev[i % 3], lev[i % 3], ACT.Exp).then_inc(exp_done, 1)

                    def out_squares(it, hd):
                        act.wait_ge(out_done, it * 2 + hd + 1)
                        nc.scalar.activation(o_s, psum[:, 7], ACT.Copy)
                        nc.scalar.activation(o_r, psum[:, 7], ACT.Square)
                        act.drain().then_inc(sq_done, 1)

                    def out_root(it, hd):
                        act.wait_ge(var_done, it * 2 + hd + 1)
                        nc.scalar.activation(o_r, psum[:, 7], ACT.Sqrt,
                                             bias=ccol("eps")).then_inc(rt_done, 1)

                    def step(it, hd, i, before, after):
                        if i + 2 < NL - 1:
                            level_exp(it, hd, i + 2)
                        elif i + 2 >= NL and after is not None:
                            level_exp(*after, i + 2 - NL)
                        if i == 1 and before is not None:
                            out_squares(*before)
                        if i == 2:
                            key_decays(it, hd)
                        if i == 3:
                            query_decays(hd)
                            if before is not None:
                                out_root(*before)
                        if i in (5, 6, 7):
                            at, m = ((0, 4), (4, 3), (7, 3))[i - 5]
                            act.wait_ge(tr_done, it * (2 * TRG) + (TRG * hd + i - 5 + 1))
                            nc.scalar.activation(k_t[:, at:at + m], psum[:, 7, 0:m * P].rearrange(
                                "p (c n) -> p c n", n=P), ACT.Copy).then_inc(tr_read, 1)
                        if after is not None:
                            if i == 8:
                                inputs(act, *after)
                            if i == 10:
                                logs(*after)
                            if i == 12:
                                gate_silu(*after)

                    inputs(act, 0, 0)
                    gate_silu(0, 0)
                    logs(0, 0)
                    level_exp(0, 0, 0)
                    level_exp(0, 0, 1)
                    by_pairs(act, step)
                    out_squares(KT // 2 - 1, 1)
                    out_root(KT // 2 - 1, 1)

                @block.vector
                def _(dve):
                    dve.sem_inc(ctx_free, 1)
                    dve.sem_inc(sc_read, 2)
                    dve.sem_inc(head_done, 1)
                    dve.wait_ge(tab_in, tab0 + 16)
                    nc.vector.memset(ones, 1.0)
                    for b in range(2):
                        nc.vector.memset(run_b[b][:, :, 0:1], 0.0)
                    nc.vector.memset(run_c[:, :, 0:1], 0.0)
                    dve.drain()

                    def clip(it, hd):
                        dve.wait_ge(front_in, it * 2 + hd + 1)
                        for t in (lf, lc):
                            nc.vector.tensor_scalar(t, t, 1e-6, 1.0, ALU.max, ALU.min)
                        dve.drain().then_inc(clipped, 1)

                    def sums(it, hd, part):
                        if part == 0:
                            dve.wait_ge(logged, it * 2 + hd + 1)
                            for c in range(4):
                                at = slice(c * CH, (c + 1) * CH)
                                nc.vector.tensor_tensor_scan(run_f[hd][:, c], ones, lf[:, 0, at],
                                                             0.0, ALU.mult, ALU.add)
                                nc.vector.tensor_tensor_scan(run_b[hd][:, c, 1:RB], ones,
                                                             lf[:, 1, at], 0.0, ALU.mult, ALU.add)
                        else:
                            for t in range(2):
                                nc.vector.tensor_tensor_scan(run_c[:, t, 1:CH + 1], ones,
                                                             lc[:, t, 0:CH], 0.0, ALU.mult, ALU.add)
                            dve.drain()
                            for t in range(2):
                                nc.vector.tensor_tensor_scan(run_c[:, t, CH + 1:CTX + 1], ones,
                                                             lc[:, t, CH:CTX], run_c[:, t, CH:CH + 1],
                                                             ALU.mult, ALU.add)
                            dve.drain().then_inc(summed, 1)

                    def decayed_keys(it, hd):
                        dve.wait_ge(decayed, it * 4 + (2 * hd + 1))
                        for t in range(2):
                            nc.vector.tensor_tensor(kd[:, t], kd[:, t], k_s[t][:, hd], ALU.mult)
                            nc.vector.tensor_tensor(kcd[:, t], kcd[:, t], kc_s[hd][:, t], ALU.mult)
                        dve.drain().then_inc(kd_done, 1)

                    def decayed_queries(it, hd):
                        dve.wait_ge(decayed, it * 4 + (2 * hd + 2))
                        for t in range(2):
                            nc.vector.tensor_tensor(qd[:, t], qd[:, t], q_s[:, hd], ALU.mult)
                        dve.drain().then_inc(kd_done, 1)

                    def diff(hd, i):
                        level, bwd = i // 2, i % 2
                        lo, hi = halves(lev[i % 3], level)
                        w = 1 << level
                        nb = CH // (2 * w)
                        if not bwd:
                            blk = run_f[hd].rearrange("p c (b h n) -> p (c b) h n", h=2, n=w)
                            ref = blk[:, :, 0, w - 1:w].to_broadcast([P, 4 * nb, w])
                            nc.vector.tensor_tensor(lo, ref, blk[:, :, 0], ALU.subtract)
                            nc.vector.tensor_tensor(hi, blk[:, :, 1], ref, ALU.subtract)
                        else:
                            blk = run_b[hd][:, :, 0:CH].rearrange("p c (b h n) -> p c b h n", h=2, n=w)
                            lo4 = lo.rearrange("p (c b) n -> p c b n", c=4)
                            hi4 = hi.rearrange("p (c b) n -> p c b n", c=4)
                            ref = blk[:, :, :, 1, 0:1].to_broadcast([P, 4, nb, w])
                            nc.vector.tensor_tensor(lo4, ref, blk[:, :, :, 0], ALU.subtract)
                            nc.vector.tensor_tensor(hi4, blk[:, :, :, 1], ref, ALU.subtract)
                        dve.drain().then_inc(diff_done, 1)

                    def fill(it, hd, i):
                        level, bwd = i // 2, i % 2
                        dve.wait_ge(exp_done, it * (2 * NL - 2) + ((NL - 1) * hd + i + 1))
                        lo, hi = halves(lev[i % 3], level)
                        k_lo, k_hi = halves(k_s[bwd][:, hd], level)
                        q_lo, q_hi = halves(q_s[:, hd], level)
                        nc.vector.tensor_tensor(lo, lo, q_lo if bwd else k_lo, ALU.mult)
                        nc.vector.tensor_tensor(hi, hi, k_hi if bwd else q_hi, ALU.mult)
                        dve.drain().then_inc(lev_done, 1)

                    def pick(it, hd, i):
                        dve.wait_ge(sc_done, it * (2 * NL) + (NL * hd + i + 1))
                        dve.sem_inc(picks, 1)
                        nc.vector.copy_predicated(
                            sc[hd].rearrange("p (c n) -> p c n", n=P),
                            mask[:, i].unsqueeze(1).to_broadcast([P, 4, P]).bitcast(mybir.dt.int32),
                            psum[:, 5 + (NL * hd + i) % 2].rearrange("p (c n) -> p c n", n=P))
                        dve.drain().then_inc(sc_read, 1)

                    def states(it, hd, t):
                        dve.wait_ge(kv_done, it * 4 + (2 * hd + t + 1))
                        first = 7 if t else 0
                        nc.vector.tensor_copy(st[:, first], psum[:, 7, 0:P])
                        dve.drain()
                        for c in range(3):
                            src, dst = (7 - c, 6 - c) if t else (c, c + 1)
                            at = (3 - c) if t else c + 1
                            nc.vector.scalar_tensor_tensor(
                                st[:, dst], st[:, src], e_end[:, src:src + 1],
                                psum[:, 7, at * P:(at + 1) * P], ALU.mult, ALU.add)
                            dve.drain()
                        dve.sem_inc(st_done, 1)

                    def head_out(it, hd):
                        dve.wait_ge(rt_done, it * 2 + hd + 1)
                        nc.vector.reciprocal(o_r, o_r)
                        dve.drain()
                        nc.vector.tensor_tensor(o_s, o_s, o_r, ALU.mult)
                        dve.drain()
                        nc.vector.scalar_tensor_tensor(yg[:, it * 2 + hd], o_s, pcol("gnorm_w"),
                                                       g_s[:, hd], ALU.mult, ALU.mult)
                        dve.drain().then_inc(head_done, 1)

                    def step(it, hd, i, before, after):
                        if i < NL - 1:
                            fill(it, hd, i)
                        else:
                            nc.vector.tensor_tensor(lev[i % 3], k_s[0][:, hd], k_s[1][:, hd],
                                                    ALU.add).then_inc(lev_done, 1)
                        if i > 0:
                            pick(it, hd, i - 1)
                        elif before is not None:
                            pick(*before, NL - 1)
                        if i + 2 < NL - 1:
                            diff(hd, i + 2)
                        elif i + 2 >= NL and after is not None:
                            diff(1 - hd, i + 2 - NL)
                        if i == 4:
                            decayed_keys(it, hd)
                        if i == 5:
                            decayed_queries(it, hd)
                        if i == 6 and before is not None:
                            head_out(*before)
                        if i == 9:
                            states(it, hd, 0)
                        if i == 11:
                            states(it, hd, 1)
                        if after is not None:
                            if i == 9:
                                clip(*after)
                            if i in (11, 12):
                                sums(*after, i - 11)

                    clip(0, 0)
                    sums(0, 0, 0)
                    sums(0, 0, 1)
                    diff(0, 0)
                    diff(0, 1)
                    by_pairs(dve, step)
                    pick(KT // 2 - 1, 1, NL - 1)
                    head_out(KT // 2 - 1, 1)
            took(32, 32)
            hn_cut, yg_cut, WS0 = cut(hn, 48, 56), cut(yg, 64, 36), 72
            merge(hn_cut, yg_cut, mg, 80, True, WS0, (hn_cut, yg_cut))

            TAPS = 31
            HALF = TAPS // 2
            UW = S + TAPS - 1
            cv = tiles(36, KT)
            upad = [arena[:, (44 + 2 * b) * S:(44 + 2 * b) * S + UW] for b in range(2)]
            sg = tiles(80, 2)
            acc = tiles(82, 2)
            sg_in, u_done = sem("c_sg_in"), sem("c_u_done")
            w0, o0 = w_at[0], o_at[0]
            s0 = split_took(16)
            with nc.Block() as block:
                @block.sync
                def _(sp):
                    refill(sp, w0, 16)

                @block.gpsimd
                def _(pool):
                    split_weights(pool, w0, 16, WS0)

                @block.tensor
                def _(pe):
                    project3(pe, w0, o0, 16, WS0, s0, lambda j, k: hn_cut["hi"][k],
                             lambda j, k: hn_cut["lo"][k])

                @block.scalar
                def _(act):
                    def one(it, j):
                        act.wait_ge(w_used, it * 4 + (w0 + 2 * j + 2))
                        act.wait_ge(u_done, it * 2 + j + 1)
                        b = (o0 + 2 * j + 1) % NBANK
                        nc.scalar.activation(sg[:, j], psum[:, b], ACT.Sigmoid)
                        act.drain().then_inc(bank_free[b], 1)
                        act.sem_inc(sg_in, 1)
                    turns(act, KT, one, 2)

                @block.vector
                def _(dve):
                    dve.sem_inc(u_done, 2)
                    for b in range(2):
                        nc.vector.memset(upad[b][:, :HALF], 0.0)
                        nc.vector.memset(upad[b][:, HALF + S:], 0.0)
                    dve.drain()

                    def one(it, j):
                        def tap_w(t):
                            return par[:, bass.ds(it * 2 + (PCOL["cv_w"] + 8 * t + j), 1)]
                        dve.wait_ge(w_used, it * 4 + (w0 + 2 * j + 1))
                        dve.wait_ge(sg_in, it * 2 + j + 1)
                        b = (o0 + 2 * j) % NBANK
                        nc.vector.tensor_tensor(upad[j][:, HALF:HALF + S], sg[:, j], psum[:, b],
                                                ALU.mult)
                        dve.drain().then_inc(bank_free[b], 1)
                        dve.sem_inc(u_done, 1)
                        nc.vector.tensor_scalar(acc[:, 0], upad[j][:, 0:S], tap_w(0),
                                                par[:, bass.ds(it * 2 + (PCOL["cv_b"] + j), 1)],
                                                ALU.mult, ALU.add)
                        nc.vector.tensor_scalar(acc[:, 1], upad[j][:, 1:1 + S], tap_w(1), None,
                                                ALU.mult)
                        for t in range(2, TAPS):
                            if t % 2 == 0:
                                dve.drain()
                            nc.vector.scalar_tensor_tensor(acc[:, t % 2], upad[j][:, t:t + S],
                                                           tap_w(t), acc[:, t % 2], ALU.mult, ALU.add)
                        dve.drain()
                        nc.vector.tensor_tensor(cv[:, it * 2 + j], acc[:, 0], acc[:, 1], ALU.add)
                        dve.drain()
                    turns(dve, KT, one, 2)
            took(16, 16)

            def silu_ln(k):
                nc.scalar.activation(cv[:, k], cv[:, k], ACT.Silu, scale=pcol("cv_ln_w", k),
                                     bias=pcol("cv_ln_b", k))
            norm(cv, cv, 44, silu_ln, mean=True)
            cv_cut = cut(cv, 64, 36)
            merge(hn_cut, cv_cut, mg, 80, False, WS0, (cv_cut,))

            def add_gated(gate_at, n_w, c, ws0):
                w0, o0 = w_at[0], o_at[0]
                s0, blocks_of = split_took(n_w), c["n"]
                with nc.Block() as block:
                    @block.sync
                    def _(sp):
                        refill(sp, w0, n_w)

                    @block.gpsimd
                    def _(pool):
                        split_weights(pool, w0, n_w, ws0)

                    @block.scalar
                    def _(act):
                        cut_hi(act, c)

                    @block.tensor
                    def _(pe):
                        for m in range(KT):
                            out = psum[:, (o0 + m) % NBANK]
                            for k in range(blocks_of):
                                i = m * blocks_of + k
                                if m == 0:
                                    pe.wait_ge(lo_in, c["at"] + k + 1)
                                if i % KT == 0:
                                    pe.wait_ge(w_split, s0 + i // KT + 1)
                                if k == 0:
                                    bank_ready(pe, o0, 0, m)
                                w_hi, w_lo = (w[:, i % KT * P:(i % KT + 1) * P]
                                              for w in split_tile(ws0, i // KT % 2))
                                nc.tensor.matmul(out, w_hi, c["hi"][k], start=(k == 0),
                                                 stop=False)
                                nc.tensor.matmul(out, w_hi, c["lo"][k], start=False, stop=False)
                                last = nc.tensor.matmul(out, w_lo, c["hi"][k], start=False,
                                                        stop=(k == blocks_of - 1))
                                if i % KT == KT - 1:
                                    last.then_inc(w_used, 1)

                    @block.vector
                    def _(dve):
                        cut_lo(dve, c)
                        for m in range(KT):
                            dve.wait_ge(w_used, w0 + -(-(m + 1) * blocks_of // KT))
                            nc.vector.scalar_tensor_tensor(
                                x[:, m], psum[:, (o0 + m) % NBANK], mod[:, gate_at + m, 0:1], x[:, m],
                                ALU.mult, ALU.add).then_inc(bank_free[(o0 + m) % NBANK], 1)
                took(n_w, KT)

            add_gated(16, 8, cut(mg, 40, 24), 48)

            norm(x, hn, 76, affine(hn, lambda k: a2[:, k:k + 1],
                                           lambda k: mod[:, 24 + k, 0:1]))
            GW, GH = 64, 8
            PW, PH = GW + 2, GH + 2
            gt = tiles(24, FT)
            grid = [arena[:, (46 + 2 * b) * S:(46 + 2 * b) * S + PW * PH].rearrange(
                "p (r c) -> p r c", c=PW) for b in range(2)]
            acc = [tiles(50 + 2 * b, 2) for b in range(2)]
            ge = tiles(54, 2)
            u_in, u_used = sem("f_u_in"), sem("f_u_used")
            cv_done, ge_done = sem("f_cv_done"), sem("f_ge_done")
            w0, o0 = w_at[0], o_at[0]
            zeros = sem("f_zeros")
            hn_cut, WS0 = cut(hn, 16, 8), 68
            s0 = split_took(2 * FT)
            with nc.Block() as block:
                @block.sync
                def _(sp):
                    refill(sp, w0, 2 * FT)

                @block.gpsimd
                def _(pool):
                    split_weights(pool, w0, 2 * FT, WS0)

                @block.tensor
                def _(pe):
                    cut_wait(pe, hn_cut)
                    project3(pe, w0, o0, 2 * FT, WS0, s0, lambda j, k: hn_cut["hi"][k],
                             lambda j, k: hn_cut["lo"][k])

                @block.scalar
                def _(act):
                    cut_hi(act, hn_cut)
                    act.wait_ge(zeros, 1)

                    def load(it, j):
                        act.wait_ge(w_used, it * 4 + (w0 + 2 * j + 1))
                        act.wait_ge(u_used, it * 2 + j + 1)
                        b = (o0 + 2 * j) % NBANK
                        nc.scalar.activation(grid[j][:, 1:GH + 1, 1:GW + 1],
                                             psum[:, b].rearrange("p (r c) -> p r c", c=GW), ACT.Copy)
                        act.drain().then_inc(bank_free[b], 1)
                        act.sem_inc(u_in, 1)

                    def gelu(it, j):
                        act.wait_ge(cv_done, it * 2 + j + 1)
                        nc.scalar.activation(ge[:, j], acc[j][:, 0], ACT.Gelu,
                                             bias=par[:, bass.ds(it * 2 + (PCOL["ffn_b"] + j), 1)]
                                             ).then_inc(ge_done, 1)

                    def one(it, j):
                        load(it, j)
                        if j == 1:
                            gelu(it, 0)
                            gelu(it, 1)
                    turns(act, FT, one, 2)

                @block.vector
                def _(dve):
                    for b in range(2):
                        nc.vector.memset(grid[b], 0.0)
                    dve.drain().then_inc(zeros, 1)
                    cut_lo(dve, hn_cut)
                    dve.sem_inc(u_used, 2)

                    def conv(it, j):
                        dve.wait_ge(u_in, it * 2 + j + 1)
                        for t in range(9):
                            src = grid[j][:, t // 3:t // 3 + GH, t % 3:t % 3 + GW]
                            w_t = par[:, bass.ds(it * 2 + (PCOL["ffn_w"] + FT * t + j), 1)]
                            a = acc[j][:, t % 2].rearrange("p (r c) -> p r c", c=GW)
                            if t and t % 2 == 0:
                                dve.drain()
                            if t < 2:
                                nc.vector.tensor_scalar(a, src, w_t, None, ALU.mult)
                            else:
                                nc.vector.scalar_tensor_tensor(a, src, w_t, a, ALU.mult, ALU.add)
                        dve.drain().then_inc(u_used, 1)
                        nc.vector.tensor_tensor(acc[j][:, 0], acc[j][:, 0], acc[j][:, 1], ALU.add)
                        dve.drain().then_inc(cv_done, 1)

                    def mul(it, j):
                        dve.wait_ge(w_used, it * 4 + (w0 + 2 * j + 2))
                        dve.wait_ge(ge_done, it * 2 + j + 1)
                        b = (o0 + 2 * j + 1) % NBANK
                        nc.vector.tensor_tensor(gt[:, it * 2 + j], ge[:, j], psum[:, b],
                                                ALU.mult)
                        dve.drain().then_inc(bank_free[b], 1)

                    def one(it, j):
                        conv(it, j)
                        if j == 1:
                            mul(it, 0)
                            mul(it, 1)
                    turns(dve, FT, one, 2)
            took(2 * FT, 2 * FT)
            add_gated(40, FT, cut(gt, 46, 24, FT), 68)

            def times(k):
                nc.scalar.activation(x[:, k], x[:, k], ACT.Copy, scale=pcol("final_w", k))
            norm(x, x, 76, times)
            stored = sem("stored")
            with nc.Block() as block:
                @block.sync
                def _(sp):
                    sp.dma_start(out_t.rearrange("(k p) n -> p k n", p=P), x).then_inc(stored, 16)
                    sp.wait_ge(stored, 16)

        first_block()
        hybrid_block()
        recurrent_block()


def blocks(w):
    k, n = w.shape
    b = w.reshape(k // P, P, n // P, P).transpose(2, 0, 1, 3).reshape(-1, 8, P, P)
    return b.transpose(0, 2, 1, 3).reshape(-1, P, 1024)


def wide_blocks(w):
    k, n = w.shape
    b = w.reshape(k // (2 * P), 2, P, n // S, S).transpose(3, 0, 2, 1, 4)
    return b.reshape(-1, P, 1024)


def cols(v):
    return v.reshape(-1, P).T


def host(inp):
    a = {k: np.asarray(v) for k, v in inp.items()}
    ws = [blocks(a["w_in_a"][0][:, :2048]), blocks(a["w_in_a"][0][:, 2048:])]
    g = a["w_grp_a"][0].reshape(4, 4, P, 4, P).transpose(0, 3, 1, 2, 4).reshape(8, 8, P, P)
    ws += [g.transpose(0, 2, 1, 3).reshape(8, P, 1024), blocks(a["w_out_a"][0])]
    wb, wk = a["w_in_b"][0], a["w_kv"]
    for half in range(2):
        at = 512 * half
        ws += [blocks(wb[:, 1024 * i + at:1024 * i + at + 512]) for i in range(3)]
        ws += [blocks(wk[:, 1024 * i + at:1024 * i + at + 512]) for i in range(3)]
        ws += [blocks(wb[:, 3072 + at:3072 + at + 512])]
        ws += [wide_blocks(wk[:, 3072 + 1024 * i + at:3072 + 1024 * i + at + 512]) for i in range(3)]
    ws += [blocks(a["w_out_b"][0])]
    first = ws
    ws = [blocks(a["w_ada_2"][0])]
    w = a["w_in_2"][0]
    order = np.concatenate([c * D + m * P + np.arange(P) for m in range(KT) for c in (1, 2, 0, 3)])
    ws.append(blocks(w[:, order]))
    b0 = 4 * D
    c0 = b0 + 2 * D + 6 * 256 + 48
    g0 = c0 + 3 * D

    def gated(gate_w, branch_w):
        pair = np.stack([blocks(gate_w), blocks(branch_w)], axis=1)
        return pair.reshape(-1, P, 1024)

    def branch(i):
        return gated(w[:, g0 + i * D:g0 + (i + 1) * D], a["w_br_2"][0, i])
    ws.append(branch(0))
    kv = b0 + D
    ws.append(blocks(np.concatenate([w[:, b0:kv + 768], w[:, kv + 1024:kv + 1280],
                                     w[:, kv + 1536:kv + 1536 + D]], axis=1)))
    ws.append(wide_blocks(np.concatenate([w[:, kv + 768:kv + 1024], w[:, kv + 1280:kv + 1536]], axis=1)))
    ws.append(branch(1))
    ws += [wide_blocks(w[:, c0 + D:c0 + 2 * D]), blocks(w[:, c0:c0 + D]), blocks(w[:, c0 + 2 * D:c0 + 3 * D])]
    ws.append(branch(2))
    ws.append(blocks(a["w_out_2"][0]))
    second = ws
    gl = w[:, kv + 1536 + D:c0]
    extra = {
        "w_gl": gl.reshape(KT, P, 48).transpose(1, 0, 2).reshape(P, -1),
        "w_ck1": a["w_ck1_2"][0], "w_cv1": a["w_cv1_2"][0],
        "w_c2": np.concatenate([a["w_ck2_2"][0], a["w_cv2_2"][0]], axis=1),
        "pos": np.concatenate([np.concatenate([a["pos_ck_2"][0].T] * 2),
                               np.concatenate([a["pos_cv_2"][0].T] * 2)], axis=1),
        "ln_bc": np.broadcast_to(np.concatenate([a["ln_g_2"][0], a["ln_b_2"][0]]), (P, 2 * D)),
        "w_s": a["w_s_2"][0].transpose(2, 0, 1).reshape(P, -1),
        "b_s": a["b_s_2"][0].reshape(1, -1),
    }
    par = {n: np.zeros((P, c), np.float32) for n, c in PARAMS}
    par["scale_a"] = cols(a["scale_a"])
    par["ln_g"], par["ln_b"] = cols(a["ln_g"]), cols(a["ln_b"])
    for name, key in (("g_pre", "g_pre_2"), ("g_post", "g_post_2"), ("c_2", "c_2"),
                      ("b_ada", "b_ada_2"), ("conv_w", "conv_w_2"), ("conv_b", "conv_b_2")):
        par[name] = cols(a[key])
    w = a["w_in_3"][0]
    part = [w[:, i * D:(i + 1) * D] for i in range(9)]
    heads = np.concatenate([part[i][:, m * P:(m + 1) * P] for m in range(KT) for i in (0, 1, 2, 4)],
                           axis=1)
    up = a["w_up_3"][0]
    ff = FT * P
    third = [blocks(a["w_mod_3"][0]), wide_blocks(part[3]), blocks(heads),
             gated(part[7], a["w_hg_out_3"][0]), gated(part[5], part[6]),
             gated(part[8], a["w_cv_out_3"][0]), blocks(a["w_out_3"][0]),
             gated(up[:, :ff], up[:, ff:]), blocks(a["w_down_3"][0])]
    par["c_3"] = np.stack([cols(a["c_3"]), cols(a["c_ctx_3"])], axis=2).reshape(P, 16)
    for name, key in (("b_mod", "b_mod_3"), ("norm1_w", "norm1_w_3"), ("gnorm_w", "hg_gnorm_w_3"),
                      ("cv_w", "cv_dw_w_3"), ("cv_b", "cv_dw_b_3"), ("cv_ln_w", "cv_ln_w_3"),
                      ("cv_ln_b", "cv_ln_b_3"), ("norm2_w", "norm2_w_3"), ("ffn_w", "ffn_dw_w_3"),
                      ("ffn_b", "ffn_dw_b_3"), ("final_w", "final_norm_w_3")):
        par[name] = cols(a[key])
    extra["ctx_t"] = a["ctx_3"][0].T
    return (first, second, third), par, extra, a


def tables():
    i = np.arange(1, 49, dtype=np.float32)
    s1 = (2.0 ** (-8.0 * i / 48)).astype(np.float32)
    i = np.arange(1, 17, dtype=np.float32)
    s2 = (2.0 ** (-8.0 * i / 16)).astype(np.float32)
    fix = np.ones((4, 16), np.float32)
    for g, w in enumerate(WINDOWS):
        fix[g, :w] = w / np.arange(1, w + 1, dtype=np.float32)
    p = np.arange(P)
    valid = np.ones((P, 4), np.float32)
    valid[:31, 0] = 0
    con = np.concatenate([
        np.broadcast_to(-s1, (P, 48)), np.broadcast_to(-s2, (P, 16)), valid,
        np.broadcast_to(fix.reshape(-1), (P, 64)), np.eye(P), np.full((P, P), 1 / D),
        np.full((P, P), 1 / P), np.full((P, 1), EPS), np.full((P, 1), LN_EPS)], axis=1)
    d = 4 * p[:, None] + 3 - np.arange(S + 3)[None, :]
    dist0 = np.where((d >= 0) & (d <= 128), d, MASKED)
    d = p[:, None] - p[None, :]
    dist12 = np.concatenate([np.where(d >= 0, 4 * d, MASKED),
                             np.where((d >= 0) & (d % 4 == 0), 4 * d, MASKED)], axis=1)
    c = np.arange(S)[None, :] - 384
    rel = np.where(p[:, None] >= c, p[:, None] - c, MASKED)
    t = P * np.arange(4)[None, :, None] + p[:, None, None]
    d = t - 16 * np.arange(N_CMP)[None, None, :] - 31
    cmp_dist = np.where(d >= 0, d, MASKED).reshape(P, -1)
    out = {"con": con, "dist0": dist0, "dist12": dist12, "rel": rel, "cmp_dist": cmp_dist}
    s, t = p[:, None], p[None, :]
    masks = []
    for level in range(LEVELS):
        pair = (s >> (level + 1)) == (t >> (level + 1))
        lower_s = ((s >> level) & 1) == 0
        lower_t = ((t >> level) & 1) == 0
        masks += [pair & lower_s & ~lower_t, pair & ~lower_s & lower_t]
    masks.append(s == t)
    out["gla_mask"] = np.concatenate(masks, axis=1)
    return {n: np.ascontiguousarray(v, dtype=np.float32) for n, v in out.items()}


def kernel(**inputs):
    import concourse.bacc as bacc
    from concourse.bass_utils import run_bass_kernel_spmd

    (first, second, third), par, extra, a = host(inputs)
    arrays = {"x_t": a["x"][0].T, "weights": np.concatenate(first + second + third),
              "par": np.concatenate([par[n] for n, _ in PARAMS], axis=1), **tables(), **extra}
    arrays = {f"in_{n}": np.ascontiguousarray(v) for n, v in arrays.items()}
    nc = bacc.Bacc("TRN2", target_bir_lowering=False, num_devices=1)
    d = {n[3:]: nc.dram_tensor(n, v.shape, mybir.dt.from_np(v.dtype), kind="ExternalInput").ap()
         for n, v in arrays.items()}
    out_t = nc.dram_tensor("out_t", (D, S), F32, kind="ExternalOutput").ap()
    build(nc, d, out_t)
    r = run_bass_kernel_spmd(nc, [arrays], core_ids=[0])
    return np.ascontiguousarray(r.results[0]["out_t"].T)[None]
```
